# Optimizing a Trainium2 kernel written in Bass

```python
import math
import jax, jax.numpy as jnp
from jax import lax
import numpy as np

D_MODEL = 1024
BATCH = 1
SEQ = 512
DEPTH = 1

CHUNK = 64
N_LEFT_CHUNKS = 8
BAND = (N_LEFT_CHUNKS + 1) * CHUNK
HEAD_DIM = 64
N_HEADS_A = 8
N_HEADS_B = 8
WIDTH_A = N_HEADS_A * HEAD_DIM
WIDTH_B = N_HEADS_B * HEAD_DIM
POOL_WINDOWS = (2, 4, 8, 16)
N_POOL_GROUPS = len(POOL_WINDOWS)
POOL_GROUP_DIM = D_MODEL // 8
WIDTH_C = N_POOL_GROUPS * POOL_GROUP_DIM
N_BRANCHES = 3
MAX_REL_DIST = 2 * CHUNK
REL_TABLE = MAX_REL_DIST + CHUNK
D_FF = 2816
CONV_WIDTH = 3
Q_BLOCK = 128
EPS = 1e-6

IN_SIZES = (WIDTH_A, WIDTH_A, WIDTH_A, WIDTH_B, WIDTH_B, WIDTH_B, WIDTH_C,
            N_BRANCHES * D_MODEL)
IN_COLS = sum(IN_SIZES)
IN_SPLITS = [int(v) for v in np.cumsum(IN_SIZES)[:-1]]

kernel_name = "hybrid_chunk_causal_gated_branches"

def rms_norm(x, gain):
    xf = x.astype(jnp.float32)
    y = xf * lax.rsqrt(jnp.mean(xf * xf, axis=-1, keepdims=True) + EPS)
    return (y * gain.astype(jnp.float32)).astype(x.dtype)

def chunked_rel_attention(q, k, v, g_q, g_k, rel_bias):
    B, S, H, Dh = q.shape
    nc = S // CHUNK
    q = rms_norm(q, g_q)
    k = rms_norm(k, g_k)
    qc = q.reshape(B, nc, CHUNK, H, Dh)
    pad = ((0, 0), (N_LEFT_CHUNKS, 0), (0, 0), (0, 0), (0, 0))
    kp = jnp.pad(k.reshape(B, nc, CHUNK, H, Dh), pad)
    vp = jnp.pad(v.reshape(B, nc, CHUNK, H, Dh), pad)
    k_band = jnp.concatenate([kp[:, j:j + nc] for j in range(N_LEFT_CHUNKS + 1)], axis=2)
    v_band = jnp.concatenate([vp[:, j:j + nc] for j in range(N_LEFT_CHUNKS + 1)], axis=2)
    logits = jnp.einsum('bcqhd,bckhd->bhcqk', qc, k_band).astype(jnp.float32) / math.sqrt(Dh)
    q_off = jnp.arange(CHUNK)[:, None] + N_LEFT_CHUNKS * CHUNK
    k_off = jnp.arange(BAND)[None, :]
    rel = jnp.clip(q_off - k_off, -(CHUNK - 1), MAX_REL_DIST) + (CHUNK - 1)
    bias = rel_bias.astype(jnp.float32)[:, rel]
    valid = (jnp.arange(nc)[:, None] + k_off // CHUNK - N_LEFT_CHUNKS) >= 0
    logits = jnp.where(valid[None, None, :, None, :], logits + bias[None, :, None], -1e30)
    p = jax.nn.softmax(logits, axis=-1)
    out = jnp.einsum('bhcqk,bckhd->bcqhd', p.astype(v.dtype), v_band)
    return out.reshape(B, S, H * Dh)

def stick_breaking_attention(q, k, v):
    B, S, H, Dh = q.shape
    nb = S // Q_BLOCK
    scale = 1.0 / math.sqrt(Dh)
    qb = q.reshape(B, nb, Q_BLOCK, H, Dh).transpose(1, 0, 2, 3, 4)
    k_pos = jnp.arange(S)
    starts = jnp.arange(nb, dtype=jnp.int32) * Q_BLOCK

    def block(args):
        q_blk, start = args
        z = jnp.einsum('bqhd,bkhd->bhqk', q_blk, k).astype(jnp.float32) * scale
        q_pos = start + jnp.arange(Q_BLOCK)
        before = k_pos[None, :] < q_pos[:, None]
        log_keep = jnp.where(before, jax.nn.log_sigmoid(-z), 0.0)
        tail = lax.cumsum(log_keep, axis=3, reverse=True) - log_keep
        w = jnp.where(before, jnp.exp(jax.nn.log_sigmoid(z) + tail), 0.0)
        return jnp.einsum('bhqk,bkhd->bqhd', w.astype(v.dtype), v)

    out = lax.map(block, (qb, starts))
    return out.transpose(1, 0, 2, 3, 4).reshape(B, S, H * Dh)

def multiscale_pool(u, w_group, scale):
    B, S, _ = u.shape
    uf = u.astype(jnp.float32).reshape(B, S, N_POOL_GROUPS, POOL_GROUP_DIM)
    cs = jnp.pad(jnp.cumsum(uf, axis=1), ((0, 0), (1, 0), (0, 0), (0, 0)))
    t = jnp.arange(S)
    pooled = []
    for g, win in enumerate(POOL_WINDOWS):
        lo = jnp.maximum(t + 1 - win, 0)
        win_sum = cs[:, 1:, g] - cs[:, lo, g]
        count = (t + 1 - lo).astype(jnp.float32)
        pooled.append(win_sum / count[None, :, None])
    pooled = jnp.stack(pooled, axis=2) - uf
    mixed = jnp.einsum('bsgc,gce->bsge', pooled.astype(u.dtype), w_group)
    return mixed.reshape(B, S, WIDTH_C) * scale

def conv_gated_mlp(h, w_up, conv_w, conv_b, w_down):
    S = h.shape[1]
    u = h @ w_up
    up = jnp.pad(u, ((0, 0), (CONV_WIDTH - 1, 0), (0, 0)))
    c = conv_b + conv_w[0] * up[:, 0:S]
    for j in range(1, CONV_WIDTH):
        c = c + conv_w[j] * up[:, j:j + S]
    gate, val = jnp.split(c, 2, axis=-1)
    return (jax.nn.silu(gate) * val) @ w_down

def setup_inputs(seed: int = 0) -> dict:
    key = jax.random.key(seed)
    ks = jax.random.split(key, 20)
    f32 = jnp.float32
    n = lambda k, shape, s: jax.random.normal(k, shape, f32) * s
    L = DEPTH
    return {
        "x": n(ks[0], (BATCH, SEQ, D_MODEL), 1.0),
        "norm_mix": 1.0 + n(ks[1], (L, D_MODEL), 0.05),
        "w_in": n(ks[2], (L, D_MODEL, IN_COLS), D_MODEL ** -0.5),
        "b_gate": n(ks[3], (L, N_BRANCHES * D_MODEL), 0.1),
        "q_norm_a": 1.0 + n(ks[4], (L, HEAD_DIM), 0.05),
        "k_norm_a": 1.0 + n(ks[5], (L, HEAD_DIM), 0.05),
        "rel_bias_a": n(ks[6], (L, N_HEADS_A, REL_TABLE), 0.5),
        "w_pool": n(ks[7], (L, N_POOL_GROUPS, POOL_GROUP_DIM, POOL_GROUP_DIM), POOL_GROUP_DIM ** -0.5),
        "pool_scale": 1.0 + n(ks[8], (L, WIDTH_C), 0.1),
        "w_branch_a": n(ks[9], (L, WIDTH_A, D_MODEL), WIDTH_A ** -0.5),
        "w_branch_b": n(ks[10], (L, WIDTH_B, D_MODEL), WIDTH_B ** -0.5),
        "w_branch_c": n(ks[11], (L, WIDTH_C, D_MODEL), WIDTH_C ** -0.5),
        "w_out": n(ks[12], (L, D_MODEL, D_MODEL), D_MODEL ** -0.5),
        "norm_ffn": 1.0 + n(ks[13], (L, D_MODEL), 0.05),
        "w_up": n(ks[14], (L, D_MODEL, 2 * D_FF), D_MODEL ** -0.5),
        "conv_w": n(ks[15], (L, CONV_WIDTH, 2 * D_FF), CONV_WIDTH ** -0.5),
        "conv_b": n(ks[16], (L, 2 * D_FF), 0.02),
        "w_down": n(ks[17], (L, D_FF, D_MODEL), D_FF ** -0.5),
    }

def reference(x, norm_mix, w_in, b_gate, q_norm_a, k_norm_a, rel_bias_a, w_pool,
              pool_scale, w_branch_a, w_branch_b, w_branch_c, w_out, norm_ffn,
              w_up, conv_w, conv_b, w_down):
    B, S, D = x.shape
    for l in range(DEPTH):
        h = rms_norm(x, norm_mix[l])
        proj = h @ w_in[l]
        q_a, k_a, v_a, q_b, k_b, v_b, u_c, g_logits = jnp.split(proj, IN_SPLITS, axis=-1)
        heads_a = lambda t: t.reshape(B, S, N_HEADS_A, HEAD_DIM)
        heads_b = lambda t: t.reshape(B, S, N_HEADS_B, HEAD_DIM)
        o_a = chunked_rel_attention(heads_a(q_a), heads_a(k_a), heads_a(v_a),
                                    q_norm_a[l], k_norm_a[l], rel_bias_a[l])
        o_b = stick_breaking_attention(heads_b(q_b), heads_b(k_b), heads_b(v_b))
        o_c = multiscale_pool(u_c, w_pool[l], pool_scale[l])
        gates = jax.nn.sigmoid((g_logits + b_gate[l]).astype(jnp.float32)).astype(x.dtype)
        gates = gates.reshape(B, S, N_BRANCHES, D)
        merged = (gates[:, :, 0] * (o_a @ w_branch_a[l])
                  + gates[:, :, 1] * (o_b @ w_branch_b[l])
                  + gates[:, :, 2] * (o_c @ w_branch_c[l]))
        x = x + merged @ w_out[l]
        h2 = rms_norm(x, norm_ffn[l])
        x = x + conv_gated_mlp(h2, w_up[l], conv_w[l], conv_b[l], w_down[l])
    return x


_drawn_inputs = setup_inputs


def setup_inputs(seed=0):
    import zlib

    import numpy as np

    out = dict(_drawn_inputs(seed))
    spreads = {}
    factors = {'q_norm_a': 8.0, 'k_norm_a': 8.0, 'conv_b': 4.229}
    for name, (base, spread) in spreads.items():
        noise = np.random.default_rng([zlib.crc32(name.encode()), seed]).standard_normal(out[name].shape)
        drawn = base * np.exp(spread * noise) if base else spread * noise
        out[name] = __import__('jax').numpy.asarray(drawn.astype(out[name].dtype))
    for name, factor in factors.items():
        out[name] = (out[name] * factor).astype(out[name].dtype)
    return out
```

```python
import concourse.bass as bass
from concourse import mybir
from contextlib import ExitStack

FP32 = mybir.dt.float32
F32R = mybir.dt.float32r
ACT = mybir.ActivationFunctionType
ALU = mybir.AluOpType

P = 128
S = 512
TT = S // P
D = 1024
KD = D // P
HD = 64
PAIRS = 4
WB = 512
KB = WB // P
FF = 2816
KF = FF // P
EPS = 1e-6
REL = 192
REL_ROW = 640
MASKED = -1e30
WINDOWS = (2, 4, 8, 16)
UNIT = KD * P

Q_A, K_A, V_A, Q_B, K_B, V_B, U_C, GATE = 0, 4, 8, 12, 16, 20, 24, 28

N_VA = 0
N_QK0 = 4
N_VB = 6
N_SLOT = 10
N_MERGE = N_SLOT + 4 * 8 + 2  
N_OUT = N_MERGE + 3 * KD
N_UP = N_OUT + KD
N_DOWN = N_UP + 2 * KF
N_END = N_DOWN + KF

S_OFF = (896, 1024, 512, 0)
T_OFF = (0, 512, 1024, 896)
SCORES = 1280

PROJ = (0, 1)
Y0 = 2
X0 = 5


def build(nc, x, norm_mix, w_in, b_gate, q_norm_a, k_norm_a, rel_bias_a, w_pool, pool_scale,
          w_branch_a, w_branch_b, w_branch_c, w_out, norm_ffn, w_up, conv_w, conv_b, w_down, out):
    ctx = ExitStack()
    with ctx:
        def sb(name, shape, dt=FP32):
            return ctx.enter_context(nc.sbuf_tensor(name, shape, dt))

        def sem(name):
            return ctx.enter_context(nc.semaphore(name))

        def region(kb, *specs):
            with ExitStack() as scope:
                if kb:
                    scope.enter_context(nc.sbuf_tensor(f"below_{specs[0][0]}", [P, 256 * kb], FP32))
                return [scope.enter_context(nc.sbuf_tensor(n, s, d)) for n, s, d in specs]

        w_raw = sb("w_raw", [P, 2, UNIT])
        w_hi = sb("w_hi", [P, 2, UNIT], F32R)
        w_lo = sb("w_lo", [P, 2, UNIT], F32R)
        h_hi = sb("h_hi", [P, KD, S], F32R)
        h_lo = sb("h_lo", [P, KD, S], F32R)
        ident = sb("ident", [P, P])
        ones_heads = sb("ones_heads", [P, P])
        ones_all = sb("ones_all", [P, P])
        rows = sb("rows", [P, 2, P])
        par = sb("par", [P, 2, P])
        eps = sb("eps", [P, 1])
        tok = sb("tok", [P, 6, TT])
        hstat = sb("hstat", [P, 4, TT])
        qk_gain = sb("qk_gain", [P, 2])
        masked = sb("masked", [P, 2, HD])
        ident_b = sb("ident_b", [P, P], mybir.dt.bfloat16)
        causal_b = sb("causal_b", [P, P], mybir.dt.bfloat16)
        inv = sb("inv", [P, 3, 16])
        CW0, CW1, BG, GM, GF = (0, 0), (0, 44), (0, 88), (0, 112), (0, 120)
        CW2, CB, PSC, GQ, GK = (1, 0), (1, 44), (1, 88), (1, 92), (1, 93)

        def pcol(where, i):
            t, c = where
            return par[:, t, c + i:c + i + 1] if isinstance(i, int) else par[:, t, bass.ds(i + c, 1)]

        x_scaled, = region(0, ("x_scaled", [P, 2, D], FP32))
        x_in, = region(64, ("x_in", [P, TT, D], FP32))
        frow, = region(32, ("frow", [8, 2, REL_ROW], FP32))
        o_hi, o_lo, gates = region(0, ("o_hi", [P, 2 * KB, S], F32R), ("o_lo", [P, 2 * KB, S], F32R),
                                   ("gates", [P, 2 * KD, S], FP32))
        (v_a, v_b, bias_rev, qk_hi, qk_lo, pt_hi, pt_lo, vp_hi, vp_lo, pa, qk_raw, sq, rn, nt) = region(
            64, ("v_a", [P, TT, WB], FP32), ("v_b", [P, TT, WB], FP32), ("bias_rev", [P, 8, S], FP32),
            ("qk_hi", [P, 2, S], F32R), ("qk_lo", [P, 2, S], F32R),
            ("pt_hi", [P, SCORES], F32R), ("pt_lo", [P, SCORES], F32R),
            ("vp_hi", [P, TT, P], F32R), ("vp_lo", [P, TT, P], F32R),
            ("pa", [P, SCORES], FP32),
            ("qk_raw", [P, 2, S], FP32), ("sq", [P, 2, S], FP32), ("rn", [P, 2, S], FP32), ("nt", [P, 2, S], FP32))
        keep, beta, suffix = region(64 + 59, ("keep", [P, SCORES], FP32), ("beta", [P, SCORES], FP32),
                                    ("suffix", [P, SCORES + TT], FP32))
        u_pad, = region(64, ("u_pad", [P, 4, 16 + S], FP32))
        win, = region(73, ("win", [P, 2, 16 + S], FP32))
        pl_hi, pl_lo, wp_hi, wp_lo, wp_raw, pl = region(
            80, ("pl_hi", [P, 2, S], F32R), ("pl_lo", [P, 2, S], F32R), ("wp_hi", [P, 4, P], F32R),
            ("wp_lo", [P, 4, P], F32R), ("wp_raw", [P, 4, P], FP32), ("pl", [P, S], FP32))
        m_hi, m_lo, oc_hi, oc_lo, x_re, mg = region(
            80, ("m_hi", [P, KD, S], F32R), ("m_lo", [P, KD, S], F32R),
            ("oc_hi", [P, KB, S], F32R), ("oc_lo", [P, KB, S], F32R),
            ("x_re", [P, 2, D], FP32), ("mg", [P, 4, S], FP32))
        x_t, x1_t, act_sb = region(0, ("x_t", [P, KD, S], FP32), ("x1_t", [P, KD, S], FP32),
                                ("act", [P, KF, S], FP32))
        x1, conv_in, conv_out, sg, r_ffn, ffn_t = region(
            76, ("x1", [P, TT, D], FP32), ("conv_in", [P, 4, 2 + S], FP32), ("conv_out", [P, 4, S], FP32),
            ("sg", [P, 2, S], FP32), ("r_ffn", [P, S], FP32), ("ffn_t", [P, 2, S], FP32))
        sq_x1, = region(132, ("sq_x1", [P, 2, S], FP32))
        a_hi, a_lo = region(124, ("a_hi", [P, 2, S], F32R), ("a_lo", [P, 2, S], F32R))
        out_sb, = region(92, ("out_sb", [P, 8, S], FP32))

        ps = ctx.enter_context(nc.psum_tensor("ps", [P, 8, S], FP32))
        frow_dram = nc.dram_tensor("rel_bias_rows", (8, REL_ROW), FP32, kind="Internal").ap()

        x_landed = [sem(f"x_landed{t}") for t in range(TT)]
        rows_landed, rel_landed, bias_landed, frow_stored = (sem("rows_landed"), sem("rel_landed"),
                                                             sem("bias_landed"), sem("frow_stored"))
        wp_landed = sem("wp_landed")
        xre_landed = [sem("xre_landed0"), sem("xre_landed1")]
        w_landed = [sem("w_landed0"), sem("w_landed1")]
        hi_ready, lo_ready, unit_done = sem("hi_ready"), sem("lo_ready"), sem("unit_done")
        const_step, const_ready, rows_zero = sem("const_step"), sem("const_ready"), sem("rows_zero")
        par_in_psum, par_ready = sem("par_in_psum"), sem("par_ready")
        ssq_done, ln_done, exp0_done, tok_step, rstd_ready = (sem("ssq_done"), sem("ln_done"), sem("exp0_done"),
                                                              sem("tok_step"), sem("rstd_ready"))
        xs_ready, xs_used, h_hi_ready, h_lo_ready = sem("xs_ready"), sem("xs_used"), sem("h_hi_ready"), sem("h_lo_ready")
        frow_step, frow_ready, bias_ready = sem("frow_step"), sem("frow_ready"), sem("bias_ready")
        v_stored = sem("v_stored")
        proj_raw, proj_sq = sem("proj_raw"), sem("proj_sq")
        ss_done, ms_done, lnq_done, expq_done, newton_step, rn_ready = (
            sem("ss_done"), sem("ms_done"), sem("lnq_done"), sem("expq_done"), sem("newton_step"), sem("rn_ready"))
        heads_step = sem("heads_step")
        refined, gain_ready = sem("refined"), sem("gain_ready")
        hat_ready, qk_hi_ready, qk_lo_ready = sem("hat_ready"), sem("qk_hi_ready"), sem("qk_lo_ready")
        s_done, rowmax_done, negmax_ready, exp_done, recip_done, p_ready = (
            sem("s_done"), sem("rowmax_done"), sem("negmax_ready"), sem("exp_done"), sem("recip_done"), sem("p_ready"))
        sig_done, scan_done = sem("sig_done"), sem("scan_done")
        suffix_init = sem("suffix_init")
        t_done, pt_hi_ready, pt_lo_ready = sem("t_done"), sem("pt_hi_ready"), sem("pt_lo_ready")
        vp_hi_ready, vp_lo_ready = sem("vp_hi_ready"), sem("vp_lo_ready")
        pv_done, o_hi_ready, o_lo_ready = sem("pv_done"), sem("o_hi_ready"), sem("o_lo_ready")
        gate_stored = sem("gate_stored")
        u_init, u_stored, win_step, pl_step, pl_ready = (sem("u_init"), sem("u_stored"), sem("win_step"),
                                                         sem("pl_step"), sem("pl_ready"))
        inv_step = sem("inv_step")
        win_ready = sem("win_ready")
        pl_hi_ready, pl_lo_ready, wp_hi_ready, wp_lo_ready = (sem("pl_hi_ready"), sem("pl_lo_ready"),
                                                              sem("wp_hi_ready"), sem("wp_lo_ready"))
        mix_done, oc_hi_ready, oc_lo_ready = sem("mix_done"), sem("oc_hi_ready"), sem("oc_lo_ready")
        sig_ab, sig_c, mg_step, mg_ready = sem("sig_ab"), sem("sig_c"), sem("mg_step"), sem("mg_ready")
        m_hi_ready, m_lo_ready = sem("m_hi_ready"), sem("m_lo_ready")
        xre_t_done, xt_stored = sem("xre_t_done"), sem("xt_stored")
        x1_ready, x1_sq, x1_ss, h2_hi, h2_lo = (sem("x1_ready"), sem("x1_sq"), sem("x1_ss"), sem("h2_hi"), sem("h2_lo"))
        x1_ln, x1_exp, x1_ms, ffn_step, r_ready = (sem("x1_ln"), sem("x1_exp"), sem("x1_ms"), sem("ffn_step"), sem("r_ready"))
        x1n_t_done, x1n_stored = sem("x1n_t_done"), sem("x1n_stored")
        cin_zero, cin_ready, tap_init, tap1_done, conv_done = (sem("cin_zero"), sem("cin_ready"), sem("tap_init"),
                                                    sem("tap1_done"), sem("conv_done"))
        sg_ready, silu_ready, act_ready = sem("sg_ready"), sem("silu_ready"), sem("act_ready")
        a_hi_ready, a_lo_ready = sem("a_hi_ready"), sem("a_lo_ready")
        bank_done, out_ready, out_stored = sem("bank_done"), sem("out_ready"), sem("out_stored")

        block = ctx.enter_context(nc.Block())

        def r32(ap):
            return ap.bitcast(FP32)

        def segs():
            return [(qt, S_OFF[qt], P * (qt + 1)) for qt in (3, 2, 0, 1)]

        def seg2(qt):
            return S_OFF[qt] + (0, 1, 2, 3)[(3, 2, 0, 1).index(qt)]

        xw = x[0].rearrange("(t p) d -> p t d", p=P)
        win_v = w_in[0].rearrange("(k p) (j c) -> p k j c", p=P, c=P)
        win_c = w_in[0].rearrange("(k p) c -> p k c", p=P)
        wa_v, wb_v, wc_v = (w[0].rearrange("(k p) (j c) -> p k j c", p=P, c=P)
                            for w in (w_branch_a, w_branch_b, w_branch_c))
        wo_v = w_out[0].rearrange("(k p) (j c) -> p k j c", p=P, c=P)
        wu_v = w_up[0].rearrange("(k p) (j c) -> p k j c", p=P, c=P)
        wd_v = w_down[0].rearrange("(k p) (h c) -> p k h c", p=P, h=2)
        out_v = out[0].rearrange("(t p) (h d) -> p t h d", p=P, h=2)

        @block.sync
        def _(sp):
            for t in range(TT):
                sp.dma_start(x_in[:, t, :], xw[:, t, :]).then_inc(x_landed[t], 16)

            def load(n, slot, halves):
                if not (isinstance(n, int) and n < 2):
                    sp.wait_ge(lo_ready, n - 1)
                for i, src in enumerate(halves):
                    k, c = src.shape[1], src.shape[-1]
                    dst = w_raw[:, slot, i * k * c:(i + 1) * k * c].rearrange("p (k c) -> p k c", k=k)
                    sp.dma_start(dst, src).then_inc(w_landed[slot], 16)

            def cols(n, slot, view, j):
                load(n, slot, [view[:, 0:4, j, :], view[:, 4:8, j, :]])

            def values(n0, c0):
                for u in range(4):
                    load(n0 + u, u % 2, [win_c[:, 2 * u + i:2 * u + i + 1, c0:c0 + WB] for i in range(2)])

            values(N_VA, V_A * P)
            cols(N_QK0, 0, win_v, Q_A)
            cols(N_QK0 + 1, 1, win_v, K_A)
            values(N_VB, V_B * P)

            def slot(s, qj, kj):
                b = N_SLOT + 4 * s
                cols(b, 0, win_v, qj)
                cols(b + 1, 1, win_v, kj)
                cols(b + 2, 0, win_v, GATE + 2 * s)
                cols(b + 3, 1, win_v, GATE + 2 * s + 1)

            slot(0, Q_A + 1, K_A + 1)
            with sp.Fori(1, 3) as s:
                slot(s, s + (Q_A + 1), s + (K_A + 1))
            slot(3, Q_B, K_B)
            with sp.Fori(4, 7) as s:
                slot(s, s + (Q_B - 3), s + (K_B - 3))
            b = N_SLOT + 28
            for i in range(4):
                cols(b + i, i % 2, win_v, U_C + i)
            sp.wait_ge(rowmax_done, 8)
            sp.dma_start(wp_raw[:, :, :], w_pool[0].rearrange("g c e -> c g e")).then_inc(wp_landed, 16)
            for i in range(2):
                cols(b + 4 + i, i, win_v, GATE + 14 + i)
            with sp.Fori(0, KD // 2) as mm:
                for i in range(2):
                    m = mm * 2 + i
                    n = mm * 6 + (N_MERGE + 3 * i)
                    load(n, i, [wa_v[:, :, m, :], wb_v[:, :, m, :]])
                    cols(n + 1, 1 - i, win_v, m + (GATE + 2 * KD))
                    load(n + 2, i, [wc_v[:, 0:2, m, :], wc_v[:, 2:4, m, :]])
            sp.dma_start(x_re[:, :, :], xw[:, 0:2, :]).then_inc(xre_landed[0], 16)
            cols(N_OUT, 0, wo_v, 0)
            cols(N_OUT + 1, 1, wo_v, 1)
            sp.wait_ge(xre_t_done, 1)
            sp.dma_start(x_re[:, :, :], xw[:, 2:4, :]).then_inc(xre_landed[1], 16)
            with sp.Fori(1, KD // 2) as mm:
                for i in range(2):
                    cols(mm * 2 + (N_OUT + i), i, wo_v, mm * 2 + i)
            with sp.Fori(0, KF) as j:
                cols(j * 2 + N_UP, 0, wu_v, j)
                cols(j * 2 + (N_UP + 1), 1, wu_v, j + KF)
            with sp.Fori(0, KF // 2) as kk:
                for i in range(2):
                    load(kk * 2 + (N_DOWN + i), i, [wd_v[:, bass.ds(kk * 2 + i, 1), h, :] for h in range(2)])
            for b8 in range(8):
                sp.wait_ge(out_ready, b8 + 1)
                sp.dma_start(out_v[:, b8 // 2, b8 % 2, :], out_sb[:, b8, :]).then_inc(out_stored, 16)
            sp.wait_ge(out_stored, 8 * 16)

        @block.gpsimd
        def _(pool):
            pool.memset(rows[:, :, :], 0.0).then_inc(rows_zero, 1)
            pool.memset(ident[:, :], 0.0).then_inc(const_step, 1)
            pool.memset(ones_all[:, :], 1.0)
            pool.memset(eps[:, :], EPS)
            pool.memset(masked[:, 0, :], MASKED)
            pool.memset(masked[:, 1, :], 0.0)
            pool.memset(ident_b[:, :], 0.0)
            pool.memset(causal_b[:, :], 0.0).then_inc(const_step, 1)
            pool.wait_ge(const_step, 2)
            pool.affine_select(out=ident_b[:, :], in_=ident_b[:, :], compare_op=ALU.not_equal, fill=1.0, base=0,
                               pattern=[[-1, P]], channel_multiplier=1)
            pool.affine_select(out=causal_b[:, :], in_=causal_b[:, :], compare_op=ALU.is_gt, fill=MASKED, base=0,
                               pattern=[[-1, P]], channel_multiplier=1)
            pool.affine_select(out=ident[:, :], in_=ident[:, :], compare_op=ALU.not_equal, fill=1.0, base=0,
                               pattern=[[-1, P]], channel_multiplier=1).then_inc(const_ready, 1)
            pool.wait_ge(frow_ready, 3)
            pool.dma_start(frow_dram[:, :], frow[:, 0, :]).then_inc(frow_stored, 16)
            pool.wait_ge(frow_stored, 16)
            windows = bass.AP(frow_dram.tensor, 0, [[REL_ROW, 8], [1, P], [1, S]])

            def bias_load(hh, h):
                if not (isinstance(hh, int) and hh < 2):
                    pool.wait_ge(rowmax_done, hh - 1)
                pool.dma_start(bias_rev[:, h, :], windows[hh, :, :]).then_inc(bias_landed, 16)
                pool.wait_ge(bias_landed, hh * 16 + 16)
                pool.tensor_tensor(bias_rev[0:HD, h, 0:HD], masked[0:HD, 0, :], masked[0:HD, 1, :], ALU.add)\
                    .then_inc(bias_ready, 1)

            bias_load(0, 0)
            bias_load(1, 1)

            def newton(t, i):
                pool.wait_ge(expq_done, t + 1)
                pool.tensor_tensor(nt[:, i, :], rn[:, i, :], rn[:, i, :], ALU.mult).then_inc(newton_step, 1)
                pool.wait_ge(newton_step, t + 1)
                pool.tensor_tensor(nt[:, i, :], nt[:, i, :], sq[:, i, :], ALU.mult).then_inc(rn_ready, 1)

            newton(0, 0)
            newton(1, 1)
            with pool.Fori(0, 3) as s:
                bias_load(s * 2 + 2, 0)
                newton(s * 2 + 2, 0)
                bias_load(s * 2 + 3, 1)
                newton(s * 2 + 3, 1)

            step = 0
            for g, w in enumerate(WINDOWS):
                pool.wait_ge(u_stored, g + 1)
                src, width, n = u_pad[:, g, :], 1, 0
                if g >= 1:
                    pool.wait_ge(pl_ready, g)
                while width < w:
                    lo = 2 * width - 1
                    dst = win[:, n % 2, :]
                    ins = pool.tensor_tensor(dst[:, lo:16 + S], src[:, lo:16 + S],
                                             src[:, lo - width:16 + S - width], ALU.add)
                    src, width, n = dst, 2 * width, n + 1
                    if width < w:
                        step += 1
                        ins.then_inc(win_step, 1)
                        pool.wait_ge(win_step, step)
                ins.then_inc(win_ready, 1)

            with pool.Fori(0, KF // 2) as jj:
                for i in range(2):
                    j = jj * 2 + i
                    pool.wait_ge(sg_ready, j + 1)
                    pool.tensor_tensor(sg[:, i, :], sg[:, i, :], conv_out[:, 2 * i, :], ALU.mult).then_inc(silu_ready, 1)
                    pool.wait_ge(silu_ready, j + 1)
                    pool.wait_ge(conv_done, j * 2 + 2)
                    pool.tensor_tensor(act_sb[:, j, :],
                                       sg[:, i, :], conv_out[:, 2 * i + 1, :], ALU.mult).then_inc(act_ready, 1)

        @block.scalar
        def _(act_e):
            a = act_e
            act = nc.scalar.activation
            a.wait_ge(rows_zero, 1)
            for src, (t, c), n in ((conv_w[0, 0], CW0, 44), (conv_w[0, 1], CW1, 44), (b_gate[0], BG, 24),
                                   (norm_mix[0], GM, 8), (norm_ffn[0], GF, 8), (conv_w[0, 2], CW2, 44),
                                   (conv_b[0], CB, 44), (pool_scale[0], PSC, 4)):
                a.dma_start(rows[c:c + n, t, :], src.rearrange("(r c) -> r c", c=P)).then_inc(rows_landed, 16)
            for src, (t, c) in ((q_norm_a, GQ), (k_norm_a, GK)):
                for i in range(2):
                    a.dma_start(rows[c:c + 1, t, i * HD:(i + 1) * HD], src[:, :]).then_inc(rows_landed, 16)
            a.dma_start(frow[:, 1, 0:REL], rel_bias_a[0]).then_inc(rel_landed, 16)

            def hi(n, slot):
                a.wait_ge(w_landed[slot], ((n // 2 + 1) * 32) if isinstance(n, int) else 0)
                if not (isinstance(n, int) and n < 2):
                    a.wait_ge(unit_done, n - 1)
                act(w_hi[:, slot, :], w_raw[:, slot, :], ACT.Copy).then_inc(hi_ready, 1)

            def hi_at(n, slot, half):
                a.wait_ge(w_landed[slot], half * 32 + 32)
                a.wait_ge(unit_done, n - 1)
                act(w_hi[:, slot, :], w_raw[:, slot, :], ACT.Copy).then_inc(hi_ready, 1)

            a.preload_act_table_set("natural_log_exp_and_others")
            for t in range(TT):
                a.wait_ge(x_landed[t], 16)
                if t:
                    a.wait_ge(ssq_done, t)
                act(x_scaled[:, 1, :], x_in[:, t, :], ACT.Square, accum_out=tok[:, 0, t:t + 1]).then_inc(ssq_done, 1)
            a.wait_ge(tok_step, 1)
            act(tok[:, 2, :], tok[:, 1, :], ACT.Ln).then_inc(ln_done, 1)
            a.wait_ge(ln_done, 1)
            act(tok[:, 3, :], tok[:, 2, :], ACT.Exp, scale=-0.5).then_inc(exp0_done, 1)
            a.wait_ge(const_ready, 1)
            hi(0, 0)
            hi(1, 1)
            a.wait_ge(par_ready, 1)
            a.wait_ge(xs_used, TT)
            for k in range(KD):
                act(h_hi[:, k, :], ps[:, k, :], ACT.Copy, scale=pcol(GM, k)).then_inc(h_hi_ready, 1)

            def after(n):
                hi(n + 2, n % 2)

            for u in range(4):
                after(N_VA + u)
            for t in range(2):
                act(v_a[:, 2 * t:2 * t + 2, :], ps[:, 2 * t:2 * t + 2, :], ACT.Copy).then_inc(v_stored, 1)

            def proj_a(t, i, bank, used, prev):
                a.wait_ge(unit_done, used)
                if prev:
                    a.wait_ge(qk_lo_ready, t - 1)
                act(qk_raw[:, i, :], ps[:, bank, :], ACT.Copy).then_inc(proj_raw, 1)
                act(sq[:, i, :], ps[:, bank, :], ACT.Square).then_inc(proj_sq, 1)

            def norm_a(t, i, bank):
                a.wait_ge(ss_done, t + 1)
                act(sq[:, i, :], ps[:, bank, :], ACT.Identity, scale=1.0 / HD, bias=eps[:, :]).then_inc(ms_done, 1)
                a.wait_ge(ms_done, t + 1)
                act(rn[:, i, :], sq[:, i, :], ACT.Ln).then_inc(lnq_done, 1)
                a.wait_ge(lnq_done, t + 1)
                act(rn[:, i, :], rn[:, i, :], ACT.Exp, scale=-0.5).then_inc(expq_done, 1)

            def hat_hi(t, i):
                a.wait_ge(hat_ready, t + 1)
                act(qk_hi[:, i, :], qk_raw[:, i, :], ACT.Copy).then_inc(qk_hi_ready, 1)

            proj_a(0, 0, 4, N_QK0 + 1, False)
            after(N_QK0)
            proj_a(1, 1, 5, N_QK0 + 2, False)
            after(N_QK0 + 1)
            after(N_VB)
            norm_a(0, 0, 6)
            norm_a(1, 1, 7)
            after(N_VB + 1)
            hat_hi(0, 0)
            hat_hi(1, 1)
            after(N_VB + 2)
            after(N_VB + 3)
            for t in range(2):
                act(v_b[:, 2 * t:2 * t + 2, :], ps[:, 2 * t:2 * t + 2, :], ACT.Copy).then_inc(v_stored, 1)

            def attn_probs(s, h, branch):
                hh = s * 2 + h
                if branch == "A":
                    a.wait_ge(negmax_ready, hh + 1)
                    for qt, c, n in segs():
                        last = act(pa[:, c:c + n], pa[:, c:c + n], ACT.Exp, bias=hstat[:, 1, qt:qt + 1],
                                   accum_out=hstat[:, 2, qt:qt + 1])
                    last.then_inc(exp_done, 1)
                else:
                    a.wait_ge(s_done, hh + 1)
                    if not (isinstance(hh, int) and hh == 8):
                        a.wait_ge(p_ready, hh)
                    flat = ps[:, X0:X0 + 3, :].rearrange("p b c -> p (b c)")[:, 0:SCORES]
                    act(keep[:, :], flat, ACT.Sigmoid, scale=-0.125)
                    act(beta[:, :], flat, ACT.Sigmoid, scale=0.125).then_inc(sig_done, 1)

            def vp_split_hi(s, v, pair, first):
                if not first:
                    a.wait_ge(pv_done, s * 2)
                cols = slice(pair * P, pair * P + P) if isinstance(pair, int) else bass.ds(pair * P, P)
                act(vp_hi[:, :, :], v[:, :, cols], ACT.Copy).then_inc(vp_hi_ready, 1)

            def pt_split_hi(s, h, bank, first):
                a.wait_ge(t_done, s * 2 + h + 1)
                if not first:
                    a.wait_ge(pv_done, s * 2 + h)
                flat = ps[:, bank:bank + 3, :].rearrange("p b c -> p (b c)")[:, 0:SCORES]
                act(pt_hi[:, :], flat, ACT.Copy).then_inc(pt_hi_ready, 1)

            def o_split_hi(s, h):
                a.wait_ge(pv_done, s * 2 + h + 1)
                rowsl = slice(HD * h, HD * h + HD)
                dst = o_hi[rowsl, s, :]
                act(dst, ps[rowsl, Y0, :], ACT.Copy).then_inc(o_hi_ready, 1)

            def gate_store(g, bank, used):
                a.wait_ge(unit_done, used)
                dst = gates[:, g, :]
                act(dst, ps[:, bank, :], ACT.Identity, bias=pcol(BG, g)).then_inc(gate_stored, 1)

            def slot(s, attn, proj):
                b = s * 4 + N_SLOT
                half = s * 2 + N_SLOT // 2
                first = isinstance(s, int) and s == 0
                if attn == "A":
                    vp_split_hi(s, v_a, s, first)
                    attn_probs(s, 0, attn)
                else:
                    attn_probs(s, 0, attn)
                    vp_split_hi(s, v_b, s - 4, False)
                t = s * 2 + 2
                if proj == "A":
                    proj_a(t, 0, PROJ[0], b + 1, True)
                elif proj == "B":
                    a.wait_ge(unit_done, b + 1)
                    a.wait_ge(s_done, s * 2 + 2)
                    act(qk_hi[:, 0, :], ps[:, PROJ[0], :], ACT.Copy).then_inc(qk_hi_ready, 1)
                hi_at(b + 2, 0, half + 1)
                pt_split_hi(s, 0, Y0, first)
                attn_probs(s, 1, attn)
                if proj == "A":
                    proj_a(t + 1, 1, PROJ[1], b + 2, True)
                    norm_a(t, 0, Y0 + 1)
                elif proj == "B":
                    a.wait_ge(unit_done, b + 2)
                    act(qk_hi[:, 1, :], ps[:, PROJ[1], :], ACT.Copy).then_inc(qk_hi_ready, 1)
                hi_at(b + 3, 1, half + 1)
                o_split_hi(s, 0)
                pt_split_hi(s, 1, X0, False)
                if proj == "A":
                    norm_a(t + 1, 1, Y0 + 2)
                hi_at(b + 4, 0, half + 2)
                gate_store(s * 2, PROJ[0], b + 3)
                if proj == "A":
                    hat_hi(t, 0)
                    hat_hi(t + 1, 1)
                o_split_hi(s, 1)
                hi_at(b + 5, 1, half + 2)
                gate_store(s * 2 + 1, PROJ[1], b + 4)

            slot(0, "A", "A")
            a.preload_act_table_set("natural_log_exp_and_others")
            with a.Fori(1, 3) as s:
                slot(s, "A", "A")
            slot(3, "A", "B")
            a.preload_act_table(ACT.Sigmoid)
            with a.Fori(4, 7) as s:
                slot(s, "B", "B")

            s, b = 7, N_SLOT + 28
            half = b // 2
            attn_probs(s, 0, "B")
            vp_split_hi(s, v_b, 3, False)

            def u_store(i, bank):
                a.wait_ge(unit_done, b + i + 1)
                if i == 0:
                    a.wait_ge(u_init, 1)
                act(u_pad[:, i, 16:16 + S], ps[:, bank, :], ACT.Copy).then_inc(u_stored, 1)

            u_store(0, PROJ[0])
            hi_at(b + 2, 0, half + 1)
            pt_split_hi(s, 0, Y0, False)
            attn_probs(s, 1, "B")
            u_store(1, PROJ[1])
            hi_at(b + 3, 1, half + 1)
            a.wait_ge(wp_landed, 16)
            act(wp_hi[:, :, :], wp_raw[:, :, :], ACT.Copy).then_inc(wp_hi_ready, 1)
            o_split_hi(s, 0)
            pt_split_hi(s, 1, X0, False)
            hi_at(b + 4, 0, half + 2)
            u_store(2, PROJ[0])
            o_split_hi(s, 1)
            hi_at(b + 5, 1, half + 2)
            u_store(3, PROJ[1])

            def pl_hi_split(g):
                a.wait_ge(pl_ready, g + 1)
                if g >= 2:
                    a.wait_ge(mix_done, g - 1)
                act(pl_hi[:, g % 2, :], pl[:, :], ACT.Copy).then_inc(pl_hi_ready, 1)

            def oc_split_hi(g):
                a.wait_ge(mix_done, g + 1)
                act(oc_hi[:, g, :], ps[:, 2 + g, :], ACT.Copy, scale=pcol(PSC, g)).then_inc(oc_hi_ready, 1)

            pl_hi_split(0)
            pl_hi_split(1)
            hi(b + 6, 0)
            gate_store(14, PROJ[0], b + 5)
            hi(b + 7, 1)
            gate_store(15, PROJ[1], b + 6)
            oc_split_hi(0)
            pl_hi_split(2)
            oc_split_hi(1)
            pl_hi_split(3)
            oc_split_hi(2)
            oc_split_hi(3)

            a.wait_ge(gate_stored, 2 * KD)
            with a.Fori(0, KD // 2) as mm:
                for i in range(2):
                    m = mm * 2 + i
                    n = mm * 6 + (N_MERGE + 3 * i)
                    h3 = mm * 3
                    for br in range(2):
                        g = gates[:, m + KD * br, :]
                        last = act(g, g, ACT.Sigmoid)
                    last.then_inc(sig_ab, 1)
                    hi_at(n + 2, i, h3 + ((N_MERGE + 3 * i + 2) // 2))
                    hi_at(n + 3, 1 - i, h3 + ((N_MERGE + 3 * i + 3) // 2))
                    a.wait_ge(unit_done, n + 2)
                    act(mg[:, 3, :], ps[:, 4 * i + 2, :], ACT.Sigmoid, bias=pcol(BG, m + 2 * KD)).then_inc(sig_c, 1)
                    hi_at(n + 4, i, h3 + ((N_MERGE + 3 * i + 4) // 2))
                    a.wait_ge(mg_ready, m + 1)
                    act(m_hi[:, m, :], mg[:, 0, :], ACT.Copy).then_inc(m_hi_ready, 1)

            a.preload_act_table_set("natural_log_exp_and_others")

            def xt_store(half_no):
                a.wait_ge(xre_t_done, half_no + 1)
                for i in range(4):
                    src = ps[:, 4 + i, :].rearrange("p (k t) -> p k t", k=2)
                    act(x_t[:, 2 * i:2 * i + 2, half_no * 256:half_no * 256 + 256], src, ACT.Copy)\
                        .then_inc(xt_stored, 1)

            def out_tile(m, i, h2):
                a.wait_ge(x1_ready, m + 1)
                x1m = x1_t[:, m, :]
                if not (isinstance(m, int) and m < 2):
                    a.wait_ge(x1_ss, m - 1)
                act(sq_x1[:, i, :], x1m, ACT.Square).then_inc(x1_sq, 1)
                hm = h_hi[:, m, :]
                act(hm, x1m, ACT.Copy, scale=pcol(GF, m)).then_inc(h2_hi, 1)

            xt_store(0)
            hi(N_OUT + 2, 0)
            xt_store(1)
            hi(N_OUT + 3, 1)
            out_tile(0, 0, None)
            out_tile(1, 1, None)
            with a.Fori(1, KD // 2) as mm:
                for i in range(2):
                    n = mm * 2 + (N_OUT + i)
                    hi_at(n + 2, i, mm + (N_OUT // 2 + 1))
                    out_tile(mm * 2 + i, i, None)
            a.wait_ge(x1_ss, KD)
            act(ffn_t[:, 0, :], ps[:, 2, :], ACT.Identity, scale=1.0 / D, bias=eps[:, :]).then_inc(x1_ms, 1)
            a.wait_ge(x1_ms, 1)
            act(ffn_t[:, 1, :], ffn_t[:, 0, :], ACT.Ln).then_inc(x1_ln, 1)
            a.wait_ge(x1_ln, 1)
            act(r_ffn[:, :], ffn_t[:, 1, :], ACT.Exp, scale=-0.5).then_inc(x1_exp, 1)
            for half_no in range(2):
                a.wait_ge(x1n_t_done, half_no + 1)
                for t in range(TT):
                    last = act(x1[:, t, half_no * S:half_no * S + S], ps[:, 4 + t, :], ACT.Copy)
                last.then_inc(x1n_stored, 1)

            a.preload_act_table(ACT.Sigmoid)

            def up(jj, first):
                for i in range(2):
                    j = jj * 2 + i
                    n = jj * 4 + (N_UP + 2 * i)
                    for gv in range(2):
                        e = 2 * i + gv
                        hi_at(n + gv + 2, gv, jj * 2 + (N_UP // 2 + i + 1))
                        a.wait_ge(cin_ready, jj * 4 + (e + 1))
                        if not first:
                            a.wait_ge(act_ready, jj * 2 + (i - 1))
                        act(conv_out[:, e, :], conv_in[:, e, 2:2 + S], ACT.Identity, scale=pcol(CW2, j + KF * gv),
                            bias=pcol(CB, j + KF * gv)).then_inc(tap_init, 1)
                    a.wait_ge(conv_done, jj * 4 + (2 * i + 1))
                    act(sg[:, i, :], conv_out[:, 2 * i, :], ACT.Sigmoid).then_inc(sg_ready, 1)

            up(0, True)
            with a.Fori(1, KF // 2) as jj:
                up(jj, False)

            def a_split(k, slot, half, first, last):
                a.wait_ge(act_ready, k + 1)
                if not first:
                    a.wait_ge(unit_done, k + (N_DOWN - 1))
                src = act_b(k)
                act(a_hi[:, slot, :], src, ACT.Copy).then_inc(a_hi_ready, 1)

            def act_b(k):
                return act_sb[:, k, :]

            a_split(0, 0, 0, True, False)
            a_split(1, 1, 0, True, False)
            with a.Fori(0, KF // 2 - 1) as kk:
                for i in range(2):
                    hi_at(kk * 2 + (N_DOWN + i + 2), i, kk + (N_DOWN // 2 + 1))
                    a_split(kk * 2 + (i + 2), i, 0, False, False)

        @block.vector
        def _(d):
            v = nc.vector

            def lo(n, slot):
                d.wait_ge(hi_ready, n + 1)
                v.tensor_tensor(w_lo[:, slot, :], w_raw[:, slot, :], r32(w_hi[:, slot, :]), ALU.subtract)\
                    .then_inc(lo_ready, 1)

            v.memset(ones_heads[:, :], 0.0).then_inc(heads_step, 1)
            d.wait_ge(heads_step, 1)
            v.memset(ones_heads[0:HD, 0:HD], 1.0)
            v.memset(ones_heads[HD:P, HD:P], 1.0).then_inc(heads_step, 1)
            d.wait_ge(rel_landed, 16)
            v.tensor_scalar(frow[:, 0, 64:64 + REL], frow[:, 1, 0:REL], 8.0, None, ALU.mult).then_inc(frow_ready, 1)
            d.wait_ge(frow_ready, 1)
            v.tensor_copy(frow[:, 0, 0:64], frow[:, 0, 64:65].to_broadcast([8, 64])).then_inc(frow_ready, 1)
            v.tensor_copy(frow[:, 0, 64 + REL:], frow[:, 0, 63 + REL:64 + REL].to_broadcast([8, REL_ROW - 64 - REL]))\
                .then_inc(frow_ready, 1)
            d.wait_ge(par_in_psum, 1)
            v.tensor_copy(par[:, :, :], ps[:, 0, 0:2 * P].rearrange("p (t c) -> p t c", t=2)).then_inc(par_ready, 1)
            d.wait_ge(par_ready, 1)
            v.tensor_scalar(qk_gain[:, :], par[:, GQ[0], GQ[1]:GQ[1] + 2], -0.5, None, ALU.mult).then_inc(gain_ready, 1)
            d.wait_ge(ssq_done, TT)
            v.tensor_scalar(tok[:, 1, :], tok[:, 0, :], 1.0 / D, EPS, ALU.mult, ALU.add).then_inc(tok_step, 1)
            d.wait_ge(exp0_done, 1)
            v.tensor_tensor(tok[:, 4, :], tok[:, 3, :], tok[:, 3, :], ALU.mult).then_inc(tok_step, 1)
            d.wait_ge(tok_step, 2)
            v.tensor_tensor(tok[:, 4, :], tok[:, 4, :], tok[:, 1, :], ALU.mult).then_inc(tok_step, 1)
            d.wait_ge(tok_step, 3)
            v.tensor_scalar(tok[:, 4, :], tok[:, 4, :], -0.5, 1.5, ALU.mult, ALU.add).then_inc(tok_step, 1)
            d.wait_ge(tok_step, 4)
            v.tensor_tensor(tok[:, 5, :], tok[:, 4, :], tok[:, 3, :], ALU.mult).then_inc(rstd_ready, 1)
            d.wait_ge(rstd_ready, 1)
            d.wait_ge(gain_ready, 1)
            for t in range(TT):
                if t >= 2:
                    d.wait_ge(xs_used, t - 1)
                v.tensor_scalar(x_scaled[:, t % 2, :], x_in[:, t, :], tok[:, 5, t:t + 1], None, ALU.mult)\
                    .then_inc(xs_ready, 1)
            lo(0, 0)
            lo(1, 1)
            for k in range(KD):
                d.wait_ge(h_hi_ready, k + 1)
                v.scalar_tensor_tensor(out=h_lo[:, k, :], in0=ps[:, k, :], scalar=pcol(GM, k), in1=r32(h_hi[:, k, :]),
                                       op0=ALU.mult, op1=ALU.subtract).then_inc(h_lo_ready, 1)
            for u in range(4):
                lo(N_VA + u + 2, u % 2)

            def hat(t, i, s_wait):
                d.wait_ge(rn_ready, t + 1)
                d.wait_ge(proj_raw, t + 1)
                v.scalar_tensor_tensor(out=nt[:, i, :], in0=nt[:, i, :], scalar=-3.0, in1=rn[:, i, :],
                                       op0=ALU.add, op1=ALU.mult).then_inc(refined, 1)
                d.wait_ge(refined, t + 1)
                v.scalar_tensor_tensor(out=qk_raw[:, i, :], in0=qk_raw[:, i, :], scalar=qk_gain[:, i:i + 1],
                                       in1=nt[:, i, :], op0=ALU.mult, op1=ALU.mult).then_inc(hat_ready, 1)

            def hat_lo(t, i):
                d.wait_ge(qk_hi_ready, t + 1)
                v.tensor_tensor(qk_lo[:, i, :], qk_raw[:, i, :], r32(qk_hi[:, i, :]), ALU.subtract)\
                    .then_inc(qk_lo_ready, 1)

            lo(N_QK0 + 2, 0)
            lo(N_QK0 + 3, 1)
            lo(N_VB + 2, 0)
            hat(0, 0, None)
            hat(1, 1, None)
            lo(N_VB + 3, 1)
            hat_lo(0, 0)
            hat_lo(1, 1)
            lo(N_VB + 4, 0)
            lo(N_VB + 5, 1)

            def logits_wait(s, h, first):
                hh = s * 2 + h
                d.wait_ge(s_done, hh + 1)
                d.wait_ge(bias_ready, hh + 1)
                if not first:
                    d.wait_ge(t_done, hh)

            def softmax_logits(s, h):
                hh = s * 2 + h
                for qt, c, n in segs():
                    src = ps[:, X0:X0 + 3, :].rearrange("p b c -> p (b c)")[:, c:c + n]
                    bb = bias_rev[:, h, n - 1::-1]
                    last = v.tensor_tensor_reduce(out=pa[:, c:c + n], in0=src, in1=bb, scale=0.125, scalar=MASKED,
                                                  op0=ALU.add, op1=ALU.max, accum_out=hstat[:, 0, qt:qt + 1])
                last.then_inc(rowmax_done, 1)
                d.wait_ge(rowmax_done, hh + 1)
                v.tensor_scalar(hstat[:, 1, :], hstat[:, 0, :], -1.0, None, ALU.mult).then_inc(negmax_ready, 1)

            def softmax_scale(s, h):
                hh = s * 2 + h
                d.wait_ge(exp_done, hh + 1)
                v.reciprocal(hstat[:, 3, :], hstat[:, 2, :]).then_inc(recip_done, 1)
                d.wait_ge(recip_done, hh + 1)
                for qt, c, n in segs():
                    last = v.tensor_scalar(pa[:, c:c + n], pa[:, c:c + n], hstat[:, 3, qt:qt + 1], None, ALU.mult)
                last.then_inc(p_ready, 1)

            def sticks(s, h):
                hh = s * 2 + h
                d.wait_ge(sig_done, hh - 7)
                d.wait_ge(t_done, hh)
                for qt, c, n in segs():
                    e = seg2(qt)
                    last = v.tensor_tensor_scan(rev(suffix, e, n), rev(keep, c, n), rev(keep, c, n), 1.0,
                                                ALU.mult, ALU.bypass)
                last.then_inc(scan_done, 1)
                d.wait_ge(scan_done, hh - 7)
                for qt, c, n in segs():
                    e = seg2(qt)
                    last = v.tensor_tensor(pa[:, c:c + n], beta[:, c:c + n], suffix[:, e + 1:e + 1 + n], ALU.mult)
                last.then_inc(p_ready, 1)

            def rev(buf, c, n):
                return buf[:, c:c + n][:, ::-1]

            def vp_split_lo(s, vv, pair):
                cols = slice(pair * P, pair * P + P) if isinstance(pair, int) else bass.ds(pair * P, P)
                v.tensor_tensor(vp_lo[:, :, :], vv[:, :, cols], r32(vp_hi[:, :, :]), ALU.subtract)\
                    .then_inc(vp_lo_ready, 1)

            def pt_split_lo(s, h, bank):
                d.wait_ge(pt_hi_ready, s * 2 + h + 1)
                flat = ps[:, bank:bank + 3, :].rearrange("p b c -> p (b c)")[:, 0:SCORES]
                v.tensor_tensor(pt_lo[:, :], flat, r32(pt_hi[:, :]), ALU.subtract).then_inc(pt_lo_ready, 1)

            def o_split_lo(s, h):
                d.wait_ge(o_hi_ready, s * 2 + h + 1)
                rw = slice(HD * h, HD * h + HD)
                at = s
                v.tensor_tensor(o_lo[rw, at, :], ps[rw, Y0, :], r32(o_hi[rw, at, :]), ALU.subtract)\
                    .then_inc(o_lo_ready, 1)

            def raw_lo(t, i):
                d.wait_ge(qk_hi_ready, t + 1)
                v.tensor_tensor(qk_lo[:, i, :], ps[:, PROJ[i], :], r32(qk_hi[:, i, :]), ALU.subtract)\
                    .then_inc(qk_lo_ready, 1)

            def slot(s, attn, proj):
                b = s * 4 + N_SLOT
                first = isinstance(s, int) and s == 0
                vv, pair = (v_a, s) if attn == "A" else (v_b, s - 4)
                t = s * 2 + 2
                if attn == "A":
                    d.wait_ge(vp_hi_ready, s + 1)
                    logits_wait(s, 0, first)
                    vp_split_lo(s, vv, pair)
                    softmax_logits(s, 0)
                    softmax_scale(s, 0)
                else:
                    d.wait_ge(vp_hi_ready, s + 1)
                    vp_split_lo(s, vv, pair)
                    sticks(s, 0)
                if proj == "B":
                    raw_lo(t, 0)
                if attn == "A":
                    logits_wait(s, 1, False)
                lo(b + 2, 0)
                if attn == "A":
                    softmax_logits(s, 1)
                pt_split_lo(s, 0, Y0)
                if attn == "A":
                    softmax_scale(s, 1)
                else:
                    sticks(s, 1)
                if proj == "B":
                    raw_lo(t + 1, 1)
                lo(b + 3, 1)
                o_split_lo(s, 0)
                pt_split_lo(s, 1, X0)
                if proj == "A":
                    hat(t, 0, None)
                lo(b + 4, 0)
                if proj == "A":
                    hat(t + 1, 1, None)
                    hat_lo(t, 0)
                    hat_lo(t + 1, 1)
                o_split_lo(s, 1)
                lo(b + 5, 1)

            slot(0, "A", "A")
            with d.Fori(1, 3) as s:
                slot(s, "A", "A")
            slot(3, "A", "B")
            d.wait_ge(qk_lo_ready, 8)
            for qt in range(TT):
                c = seg2(qt) + P * (qt + 1)
                last = v.memset(suffix[:, c:c + 1], 1.0)
            last.then_inc(suffix_init, 1)
            d.wait_ge(suffix_init, 1)
            with d.Fori(4, 7) as s:
                slot(s, "B", "B")

            s, b = 7, N_SLOT + 28
            d.wait_ge(vp_hi_ready, 8)
            vp_split_lo(s, v_b, 3)
            v.memset(u_pad[:, :, 0:16], 0.0).then_inc(u_init, 1)
            sticks(s, 0)
            lo(b + 2, 0)
            pt_split_lo(s, 0, Y0)
            sticks(s, 1)
            lo(b + 3, 1)
            v.memset(inv[:, 0, :], 1.0).then_inc(inv_step, 1)
            d.wait_ge(inv_step, 1)
            v.tensor_tensor_scan(inv[:, 1, :], inv[:, 0, :], inv[:, 0, :], 0.0, ALU.add, ALU.bypass).then_inc(inv_step, 1)
            d.wait_ge(inv_step, 2)
            v.reciprocal(inv[:, 2, :], inv[:, 1, :]).then_inc(inv_step, 1)
            d.wait_ge(wp_hi_ready, 1)
            v.tensor_tensor(wp_lo[:, :, :], wp_raw[:, :, :], r32(wp_hi[:, :, :]), ALU.subtract).then_inc(wp_lo_ready, 1)
            o_split_lo(s, 0)
            pt_split_lo(s, 1, X0)
            lo(b + 4, 0)
            o_split_lo(s, 1)
            lo(b + 5, 1)
            d.wait_ge(inv_step, 3)
            step = [0]

            def pooled(g):
                w = WINDOWS[g]
                d.wait_ge(win_ready, g + 1)
                if g:
                    d.wait_ge(pl_lo_ready, g)
                sums = win[:, g % 2, :]
                v.scalar_tensor_tensor(out=pl[:, :], in0=sums[:, 16:], scalar=1.0 / w, in1=u_pad[:, g, 16:],
                                       op0=ALU.mult, op1=ALU.subtract).then_inc(pl_step, 1)
                d.wait_ge(pl_step, 2 * g + 1)
                v.tensor_tensor(pl[:, 0:w - 1], sums[:, 16:15 + w], inv[:, 2, 0:w - 1], ALU.mult).then_inc(pl_step, 1)
                d.wait_ge(pl_step, 2 * g + 2)
                v.tensor_tensor(pl[:, 0:w - 1], pl[:, 0:w - 1], u_pad[:, g, 16:15 + w], ALU.subtract)\
                    .then_inc(pl_ready, 1)
                d.wait_ge(pl_hi_ready, g + 1)
                v.tensor_tensor(pl_lo[:, g % 2, :], pl[:, :], r32(pl_hi[:, g % 2, :]), ALU.subtract)\
                    .then_inc(pl_lo_ready, 1)

            def oc_split_lo(g):
                d.wait_ge(oc_hi_ready, g + 1)
                v.scalar_tensor_tensor(out=oc_lo[:, g, :], in0=ps[:, 2 + g, :], scalar=pcol(PSC, g),
                                       in1=r32(oc_hi[:, g, :]), op0=ALU.mult, op1=ALU.subtract).then_inc(oc_lo_ready, 1)

            pooled(0)
            pooled(1)
            lo(b + 6, 0)
            lo(b + 7, 1)
            pooled(2)
            oc_split_lo(0)
            pooled(3)
            oc_split_lo(1)
            oc_split_lo(2)
            oc_split_lo(3)

            def merge(mm, i, first):
                m = mm * 2 + i
                n = mm * 6 + (N_MERGE + 3 * i)
                bank = 4 * i
                gm = [gates[:, m + KD * br, :] for br in range(2)]
                lo(n + 2, i)
                if not first:
                    d.wait_ge(m_lo_ready, m)
                d.wait_ge(sig_ab, m + 1)
                d.wait_ge(unit_done, n + 1)
                v.tensor_tensor(mg[:, 0, :], ps[:, bank, :], gm[0], ALU.mult)
                v.tensor_tensor(mg[:, 1, :], ps[:, bank + 1, :], gm[1], ALU.mult).then_inc(mg_step, 1)
                d.wait_ge(mg_step, m * 3 + 1)
                v.tensor_tensor(mg[:, 0, :], mg[:, 0, :], mg[:, 1, :], ALU.add).then_inc(mg_step, 1)
                lo(n + 3, 1 - i)
                d.wait_ge(sig_c, m + 1)
                d.wait_ge(unit_done, n + 3)
                v.tensor_tensor(mg[:, 2, :], ps[:, bank + 3, :], mg[:, 3, :], ALU.mult).then_inc(mg_step, 1)
                d.wait_ge(mg_step, m * 3 + 3)
                v.tensor_tensor(mg[:, 0, :], mg[:, 0, :], mg[:, 2, :], ALU.add).then_inc(mg_ready, 1)
                lo(n + 4, i)
                d.wait_ge(m_hi_ready, m + 1)
                at = m
                v.tensor_tensor(m_lo[:, at, :], mg[:, 0, :], r32(m_hi[:, at, :]), ALU.subtract).then_inc(m_lo_ready, 1)

            merge(0, 0, True)
            merge(0, 1, False)
            with d.Fori(1, KD // 2) as mm:
                merge(mm, 0, False)
                merge(mm, 1, False)

            def out_tile(m, bank):
                d.wait_ge(unit_done, m + (N_OUT + 1))
                at = m
                v.tensor_tensor(x1_t[:, at, :], ps[:, bank, :], x_t[:, at, :], ALU.add).then_inc(x1_ready, 1)

            def h2_split_lo(m):
                d.wait_ge(h2_hi, m + 1)
                at = m
                v.scalar_tensor_tensor(out=h_lo[:, at, :], in0=x1_t[:, at, :], scalar=pcol(GF, m),
                                       in1=r32(h_hi[:, at, :]), op0=ALU.mult, op1=ALU.subtract).then_inc(h2_lo, 1)

            lo(N_OUT + 2, 0)
            d.wait_ge(xt_stored, 8)
            out_tile(0, 0)
            lo(N_OUT + 3, 1)
            out_tile(1, 1)
            h2_split_lo(0)
            h2_split_lo(1)
            with d.Fori(1, KD // 2) as mm:
                for i in range(2):
                    lo(mm * 2 + (N_OUT + i + 2), i)
                    out_tile(mm * 2 + i, i)
                    h2_split_lo(mm * 2 + i)
            d.wait_ge(x1_exp, 1)
            v.tensor_tensor(ffn_t[:, 1, :], r_ffn[:, :], r_ffn[:, :], ALU.mult).then_inc(ffn_step, 1)
            d.wait_ge(ffn_step, 1)
            v.tensor_tensor(ffn_t[:, 1, :], ffn_t[:, 1, :], ffn_t[:, 0, :], ALU.mult).then_inc(ffn_step, 1)
            d.wait_ge(ffn_step, 2)
            v.tensor_scalar(ffn_t[:, 1, :], ffn_t[:, 1, :], -0.5, 1.5, ALU.mult, ALU.add).then_inc(ffn_step, 1)
            d.wait_ge(ffn_step, 3)
            v.tensor_tensor(r_ffn[:, :], r_ffn[:, :], ffn_t[:, 1, :], ALU.mult).then_inc(r_ready, 1)
            v.memset(conv_in[:, :, 0:2], 0.0).then_inc(cin_zero, 1)
            d.wait_ge(r_ready, 1)
            d.wait_ge(cin_zero, 1)

            def taps(jj, i, gv):
                j, e = jj * 2 + i, 2 * i + gv
                count = jj * 4 + (e + 1)
                d.wait_ge(tap_init, count)
                v.scalar_tensor_tensor(out=conv_out[:, e, :], in0=conv_in[:, e, 1:1 + S], scalar=pcol(CW1, j + KF * gv),
                                       in1=conv_out[:, e, :], op0=ALU.mult, op1=ALU.add).then_inc(tap1_done, 1)
                d.wait_ge(tap1_done, count)
                v.scalar_tensor_tensor(out=conv_out[:, e, :], in0=conv_in[:, e, 0:S], scalar=pcol(CW0, j + KF * gv),
                                       in1=conv_out[:, e, :], op0=ALU.mult, op1=ALU.add).then_inc(conv_done, 1)

            def up(jj):
                for i in range(2):
                    n = jj * 4 + (N_UP + 2 * i)
                    for gv in range(2):
                        e = 2 * i + gv
                        d.wait_ge(unit_done, n + gv + 1)
                        v.tensor_tensor(conv_in[:, e, 2:2 + S], ps[:, e, :], r_ffn[:, :], ALU.mult)\
                            .then_inc(cin_ready, 1)
                        lo(n + gv + 2, gv)
                        taps(jj, i, gv)

            with d.Fori(0, KF // 2) as jj:
                up(jj)

            def a_split(k, slot):
                d.wait_ge(a_hi_ready, k + 1)
                src = act_sb[:, k, :]
                v.tensor_tensor(a_lo[:, slot, :], src, r32(a_hi[:, slot, :]), ALU.subtract).then_inc(a_lo_ready, 1)

            a_split(0, 0)
            a_split(1, 1)
            with d.Fori(0, KF // 2 - 1) as kk:
                for i in range(2):
                    lo(kk * 2 + (N_DOWN + i + 2), i)
                    a_split(kk * 2 + (i + 2), i)
            for b8 in range(8):
                d.wait_ge(bank_done, b8 + 1)
                h = b8 % 2
                v.tensor_tensor(out_sb[:, b8, :], ps[:, b8, :], x1[:, b8 // 2, h * S:h * S + S], ALU.add)\
                    .then_inc(out_ready, 1)

        @block.tensor
        def _(pe):
            mm3 = nc.tensor.matmul

            def product(dst, l_hi, l_lo, r_hi, r_lo, start, stop, **kw):
                mm3(dst, l_hi, r_lo, start=start, stop=False, **kw)
                mm3(dst, l_lo, r_hi, start=False, stop=False, **kw)
                return mm3(dst, l_hi, r_hi, start=False, stop=stop, **kw)

            def tile_of(n, slot, bank):
                pe.wait_ge(lo_ready, n + 1)
                for k in range(KD):
                    c = slice(k * P, k * P + P)
                    last = product(ps[:, bank, :], w_hi[:, slot, c], w_lo[:, slot, c], h_hi[:, k, :], h_lo[:, k, :],
                                   k == 0, k == KD - 1)
                last.then_inc(unit_done, 1)

            pe.wait_ge(const_ready, 1)
            pe.wait_ge(rows_landed, 12 * 16)
            for t in range(2):
                last = nc.tensor.transpose(ps[:, 0, t * P:t * P + P], rows[:, t, :], ident[:, :])
            last.then_inc(par_in_psum, 1)
            pe.wait_ge(par_ready, 1)
            for t in range(TT):
                pe.wait_ge(xs_ready, t + 1)
                for k in range(KD):
                    last = nc.tensor.transpose(ps[:, k, t * P:t * P + P], x_scaled[:, t % 2, k * P:k * P + P],
                                               ident[:, :])
                last.then_inc(xs_used, 1)

            def values(n0, free_banks):
                for u in range(4):
                    pe.wait_ge(lo_ready, n0 + u + 1)
                    if u == 0:
                        free_banks()
                    for kk in range(2):
                        k = 2 * u + kk
                        if n0 == N_VA:
                            pe.wait_ge(h_lo_ready, max(k + 1, TT))
                        for t in range(TT):
                            c = slice(kk * WB, kk * WB + WB)
                            tk = slice(t * P, t * P + P)
                            last = product(ps[:, t, :], h_hi[:, k, tk], h_lo[:, k, tk], w_hi[:, u % 2, c],
                                           w_lo[:, u % 2, c], k == 0, k == KD - 1)
                    last.then_inc(unit_done, 1)
                    yield

            for _ in values(N_VA, lambda: None):
                pass
            pe.wait_ge(h_lo_ready, KD)
            tile_of(N_QK0, 0, 4)
            tile_of(N_QK0 + 1, 1, 5)

            def sumsq(t, i, bank):
                pe.wait_ge(proj_sq, t + 1)
                mm3(ps[:, bank, :], ones_heads[:, :], sq[:, i, :], start=True, stop=True).then_inc(ss_done, 1)

            for u, _ in enumerate(values(N_VB, lambda: pe.wait_ge(v_stored, 2))):
                if u == 0:
                    sumsq(0, 0, 6)
                    sumsq(1, 1, 7)

            def scores(s, h, attn):
                hh = s * 2 + h
                r = slice(HD * h, HD * h + HD)
                for qt, c, n in segs():
                    dst = ps[:, X0:X0 + 3, :].rearrange("p b c -> p (b c)")[:, c:c + n]
                    q = slice(qt * P, qt * P + P)
                    last = product(dst, qk_hi[r, 0, q], qk_lo[r, 0, q], qk_hi[r, 1, 0:n], qk_lo[r, 1, 0:n], True, attn == "A")
                    if attn == "B":
                        last = mm3(dst[:, qt * P:n], ident_b[:, :], causal_b[:, :], start=False, stop=True)
                last.then_inc(s_done, 1)

            def transposes(s, h, bank):
                hh = s * 2 + h
                pe.wait_ge(p_ready, hh + 1)
                flat = ps[:, bank:bank + 3, :].rearrange("p b c -> p (b c)")
                for kt in range(TT):
                    for qt in range(kt, TT):
                        c = T_OFF[kt] + P * (qt - kt)
                        last = nc.tensor.transpose(flat[:, c:c + P], pa[:, S_OFF[qt] + kt * P:S_OFF[qt] + kt * P + P],
                                                   ident[:, :])
                last.then_inc(t_done, 1)

            def output(s, h):
                hh = s * 2 + h
                if h == 0:
                    pe.wait_ge(vp_lo_ready, s + 1)
                pe.wait_ge(pt_lo_ready, hh + 1)
                for kt in range(TT):
                    n = S - P * kt
                    c = slice(T_OFF[kt], T_OFF[kt] + n)
                    last = product(ps[:, Y0, P * kt:S], vp_hi[:, kt, :], vp_lo[:, kt, :], pt_hi[:, c], pt_lo[:, c],
                                   kt == 0, kt == TT - 1)
                last.then_inc(pv_done, 1)

            def slot(s, attn, proj):
                b = s * 4 + N_SLOT
                t = s * 2 + 2
                first = isinstance(s, int) and s == 0
                pe.wait_ge(qk_lo_ready, s * 2 + 2)
                if not first:
                    pe.wait_ge(pt_lo_ready, s * 2)
                scores(s, 0, attn)
                if first:
                    pe.wait_ge(v_stored, 4)
                else:
                    pe.wait_ge(gate_stored, s * 2)
                tile_of(b, 0, PROJ[0])
                if not first:
                    pe.wait_ge(o_lo_ready, s * 2)
                transposes(s, 0, Y0)
                if attn == "B":
                    pe.wait_ge(sig_done, s * 2 - 7)
                else:
                    pe.wait_ge(rowmax_done, s * 2 + 1)
                scores(s, 1, attn)
                tile_of(b + 1, 1, PROJ[1])
                output(s, 0)
                if proj == "A":
                    sumsq(t, 0, Y0 + 1)
                if attn == "B":
                    pe.wait_ge(sig_done, s * 2 - 6)
                transposes(s, 1, X0)
                if proj == "A":
                    sumsq(t + 1, 1, Y0 + 2)
                    pe.wait_ge(proj_raw, t + 1)
                elif proj == "B":
                    pe.wait_ge(qk_lo_ready, s * 2 + 3)
                else:
                    pe.wait_ge(u_stored, 1)
                tile_of(b + 2, 0, PROJ[0])
                pe.wait_ge(o_lo_ready, s * 2 + 1)
                output(s, 1)
                if proj == "A":
                    pe.wait_ge(proj_sq, t + 2)
                elif proj == "B":
                    pe.wait_ge(qk_lo_ready, s * 2 + 4)
                else:
                    pe.wait_ge(u_stored, 2)
                tile_of(b + 3, 1, PROJ[1])

            slot(0, "A", "A")
            with pe.Fori(1, 3) as s:
                slot(s, "A", "A")
            slot(3, "A", "B")
            with pe.Fori(4, 7) as s:
                slot(s, "B", "B")
            slot(7, "B", "U")
            b = N_SLOT + 28
            for i in range(2):
                pe.wait_ge(u_stored, 3 + i)
                tile_of(b + 4 + i, i, PROJ[i])

            pe.wait_ge(wp_lo_ready, 1)
            pe.wait_ge(o_lo_ready, 16)
            pe.wait_ge(pt_lo_ready, 16)
            for g in range(4):
                pe.wait_ge(pl_lo_ready, g + 1)
                product(ps[:, 2 + g, :], wp_hi[:, g, :], wp_lo[:, g, :], pl_hi[:, g % 2, :], pl_lo[:, g % 2, :],
                        True, True).then_inc(mix_done, 1)

            def merge(mm, i, first):
                m = mm * 2 + i
                n = mm * 6 + (N_MERGE + 3 * i)
                bank = 4 * i
                sl = (i, 1 - i, i)
                pe.wait_ge(lo_ready, n + 1)
                if not first:
                    pe.wait_ge(mg_ready, m - 1)
                else:
                    pe.wait_ge(gate_stored, 2 * KD)
                    if i:
                        pe.wait_ge(oc_lo_ready, 4)
                for br in range(2):
                    for k in range(KB):
                        c = slice((KB * br + k) * P, (KB * br + k) * P + P)
                        last = product(ps[:, bank + br, :], w_hi[:, sl[0], c], w_lo[:, sl[0], c],
                                       o_hi[:, KB * br + k, :], o_lo[:, KB * br + k, :], k == 0, k == KB - 1)
                last.then_inc(unit_done, 1)
                if first:
                    pe.wait_ge(oc_lo_ready, 4)
                tile_of(n + 1, sl[1], bank + 2)
                pe.wait_ge(lo_ready, n + 3)
                for k in range(KB):
                    c = slice(k * P, k * P + P)
                    last = product(ps[:, bank + 3, :], w_hi[:, sl[2], c], w_lo[:, sl[2], c], oc_hi[:, k, :],
                                   oc_lo[:, k, :], k == 0, k == KB - 1)
                last.then_inc(unit_done, 1)

            merge(0, 0, True)
            merge(0, 1, True)
            with pe.Fori(1, KD // 2) as mm:
                merge(mm, 0, False)
                merge(mm, 1, False)

            def x_half(half_no):
                pe.wait_ge(xre_landed[half_no], 16)
                if half_no == 0:
                    pe.wait_ge(mg_ready, KD)
                else:
                    pe.wait_ge(xt_stored, 4)
                for k in range(KD):
                    for t in range(2):
                        c = (k % 2) * 256 + t * P
                        last = nc.tensor.transpose(ps[:, 4 + k // 2, c:c + P], x_re[:, t, k * P:k * P + P], ident[:, :])
                last.then_inc(xre_t_done, 1)

            def out_tile(n, slot, bank):
                pe.wait_ge(lo_ready, n + 1)
                for k in range(KD):
                    c = slice(k * P, k * P + P)
                    last = product(ps[:, bank, :], w_hi[:, slot, c], w_lo[:, slot, c], m_hi[:, k, :], m_lo[:, k, :],
                                   k == 0, k == KD - 1)
                last.then_inc(unit_done, 1)

            def x1_sumsq(m, i, start, stop):
                pe.wait_ge(x1_sq, m + 1)
                mm3(ps[:, 2, :], ones_all[:, :], sq_x1[:, i, :], start=start, stop=stop).then_inc(x1_ss, 1)

            x_half(0)
            pe.wait_ge(m_lo_ready, KD)
            out_tile(N_OUT, 0, 0)
            x_half(1)
            out_tile(N_OUT + 1, 1, 1)
            pe.wait_ge(x1_ready, 1)
            out_tile(N_OUT + 2, 0, 0)
            x1_sumsq(0, 0, True, False)
            pe.wait_ge(x1_ready, 2)
            out_tile(N_OUT + 3, 1, 1)
            x1_sumsq(1, 1, False, False)
            with pe.Fori(1, KD // 2 - 1) as mm:
                for i in range(2):
                    pe.wait_ge(x1_ready, mm * 2 + (i + 1))
                    out_tile(mm * 2 + (N_OUT + i + 2), i, i)
                    x1_sumsq(mm * 2 + i, i, False, False)
            x1_sumsq(KD - 2, 0, False, False)

            def x1_back(half_no):
                for k in range(4):
                    for t in range(TT):
                        last = nc.tensor.transpose(ps[:, 4 + t, k * P:k * P + P],
                                                   x1_t[:, 4 * half_no + k, t * P:t * P + P], ident[:, :])
                last.then_inc(x1n_t_done, 1)

            x1_back(0)
            x1_sumsq(KD - 1, 1, False, True)
            pe.wait_ge(x1n_stored, 1)
            x1_back(1)
            pe.wait_ge(h2_lo, KD)

            def up(jj, first):
                for i in range(2):
                    for gv in range(2):
                        e = 2 * i + gv
                        if not first:
                            pe.wait_ge(cin_ready, jj * 4 + (e - 3))
                        elif e == 2:
                            pe.wait_ge(x1_ms, 1)
                        tile_of(jj * 4 + (N_UP + e), gv, e)

            up(0, True)
            with pe.Fori(1, KF // 2) as jj:
                up(jj, False)

            pe.wait_ge(cin_ready, 2 * KF)
            pe.wait_ge(x1n_stored, 2)

            def down(k, slot, start):
                pe.wait_ge(lo_ready, k + (N_DOWN + 1))
                pe.wait_ge(a_lo_ready, k + 1)
                for b8 in range(8):
                    t, h = b8 // 2, b8 % 2
                    tk, c = slice(t * P, t * P + P), slice(h * S, h * S + S)
                    last = product(ps[:, b8, :], a_hi[:, slot, tk], a_lo[:, slot, tk], w_hi[:, slot, c],
                                   w_lo[:, slot, c], start, False)
                last.then_inc(unit_done, 1)

            down(0, 0, True)
            down(1, 1, False)
            with pe.Fori(1, KF // 2 - 1) as kk:
                down(kk * 2, 0, False)
                down(kk * 2 + 1, 1, False)
            for k, slot in ((KF - 2, 0), (KF - 1, 1)):
                pe.wait_ge(lo_ready, k + N_DOWN + 1)
                pe.wait_ge(a_lo_ready, k + 1)
            for b8 in range(8):
                t, h = b8 // 2, b8 % 2
                tk, c = slice(t * P, t * P + P), slice(h * S, h * S + S)
                for slot in range(2):
                    last = product(ps[:, b8, :], a_hi[:, slot, tk], a_lo[:, slot, tk], w_hi[:, slot, c],
                                   w_lo[:, slot, c], False, slot == 1)
                last.then_inc(bank_done, 1)


_INS = ["x", "norm_mix", "w_in", "b_gate", "q_norm_a", "k_norm_a", "rel_bias_a", "w_pool", "pool_scale",
        "w_branch_a", "w_branch_b", "w_branch_c", "w_out", "norm_ffn", "w_up", "conv_w", "conv_b", "w_down"]


def kernel(**inputs):
    import numpy as _np
    import concourse.bacc as _bacc
    from concourse import mybir as _mybir
    from concourse.bass_utils import run_bass_kernel_spmd as _run

    nc = _bacc.Bacc("TRN2", target_bir_lowering=False, num_devices=1)
    arrays, args = {}, []
    for name in _INS:
        a = _np.ascontiguousarray(inputs[name])
        arrays[f"in_{name}_dram"] = a
        args.append(nc.dram_tensor(f"in_{name}_dram", a.shape, _mybir.dt.from_np(a.dtype), kind="ExternalInput").ap())
    args.append(nc.dram_tensor("out_0_dram", (1, S, D), _mybir.dt.float32, kind="ExternalOutput").ap())
    build(nc, *args)
    r = _run(nc, [arrays], core_ids=[0])
    return r.results[0]["out_0_dram"]
```

```python
import concourse.bass as bass
from concourse import mybir
from contextlib import ExitStack

FP32 = mybir.dt.float32
F32R = mybir.dt.float32r
ACT = mybir.ActivationFunctionType
ALU = mybir.AluOpType

P = 128
S = 512
TT = S // P
D = 1024
KD = D // P
HD = 64
PAIRS = 4
WB = 512
KB = WB // P
FF = 2816
KF = FF // P
EPS = 1e-6
REL = 192
REL_ROW = 640
MASKED = -1e30
WINDOWS = (2, 4, 8, 16)
UNIT = KD * P

Q_A, K_A, V_A, Q_B, K_B, V_B, U_C, GATE = 0, 4, 8, 12, 16, 20, 24, 28

N_QK0 = 0
N_VA = 2
N_VB = 6
N_SLOT = 10
N_MERGE = N_SLOT + 4 * 8 + 2  
N_OUT = N_MERGE + 3 * KD
N_UP = N_OUT + KD
N_DOWN = N_UP + 2 * KF
N_END = N_DOWN + KF

S_OFF = (896, 1024, 512, 0)
T_OFF = (0, 512, 1024, 896)
SCORES = 1280

PROJ = (0, 1)
HEAD = (5, 2)
V_A_BANKS = (2, 3, 4, 5)
V_B_BANKS = (0, 1, 6, 7)
PAR_BANK = 6
MIX = 4


def build(nc, x, norm_mix, w_in, b_gate, q_norm_a, k_norm_a, rel_bias_a, w_pool, pool_scale,
          w_branch_a, w_branch_b, w_branch_c, w_out, norm_ffn, w_up, conv_w, conv_b, w_down, out):
    ctx = ExitStack()
    with ctx:
        def sb(name, shape, dt=FP32):
            return ctx.enter_context(nc.sbuf_tensor(name, shape, dt))

        def sem(name):
            return ctx.enter_context(nc.semaphore(name))

        def region(kb, *specs):
            with ExitStack() as scope:
                if kb:
                    scope.enter_context(nc.sbuf_tensor(f"below_{specs[0][0]}", [P, 256 * kb], FP32))
                return [scope.enter_context(nc.sbuf_tensor(n, s, d)) for n, s, d in specs]

        w_raw = sb("w_raw", [P, 2, UNIT])
        w_hi = sb("w_hi", [P, 2, UNIT], F32R)
        w_lo = sb("w_lo", [P, 2, UNIT], F32R)
        h_hi = sb("h_hi", [P, KD, S], F32R)
        h_lo = sb("h_lo", [P, KD, S], F32R)
        ident = sb("ident", [P, P])
        ones_heads = sb("ones_heads", [P, P])
        ones_all = sb("ones_all", [P, P])
        g_row = sb("g_row", [KD, P])
        g_mix = sb("g_mix", [P, KD])
        rows = sb("rows", [P, 2, P])
        par = sb("par", [P, 2, P])
        eps = sb("eps", [P, 1])
        tok = sb("tok", [P, 6, TT])
        hstat = sb("hstat", [P, 2, 3, TT])
        qk_gain = sb("qk_gain", [P, 2])
        masked = sb("masked", [P, 2, HD])
        ident_b = sb("ident_b", [P, P], mybir.dt.bfloat16)
        causal_b = sb("causal_b", [P, P], mybir.dt.bfloat16)
        inv = sb("inv", [P, 3, 16])
        CW0, CW1, BG, GM, GF = (0, 0), (0, 44), (0, 88), (0, 112), (0, 120)
        CW2, CB, PSC, GQ, GK = (1, 0), (1, 44), (1, 88), (1, 92), (1, 93)

        def pcol(where, i):
            t, c = where
            return par[:, t, c + i:c + i + 1] if isinstance(i, int) else par[:, t, bass.ds(i + c, 1)]

        x_scaled, squares = region(0, ("x_scaled", [P, TT, D], FP32), ("squares", [P, TT, D], FP32))
        x_in, = region(64, ("x_in", [P, TT, D], FP32))
        frow, = region(32, ("frow", [8, 2, REL_ROW], FP32))
        o_hi, o_lo, gates = region(0, ("o_hi", [P, 2 * KB, S], F32R), ("o_lo", [P, 2 * KB, S], F32R),
                                   ("gates", [P, 2 * KD, S], FP32))
        (v_a, v_b, bias_rev, pa1, qk_hi, qk_lo, pt_hi, pt_lo, vp_hi, vp_lo, pa0, qk_raw, sq, rn, nt) = region(
            64, ("v_a", [P, TT, WB], FP32), ("v_b", [P, TT, WB], FP32), ("bias_rev", [P, 2, S], FP32),
            ("pa1", [P, 3 * P * 8], FP32),
            ("qk_hi", [P, 2, S], F32R), ("qk_lo", [P, 2, S], F32R),
            ("pt_hi", [P, SCORES], F32R), ("pt_lo", [P, SCORES], F32R),
            ("vp_hi", [P, TT, P], F32R), ("vp_lo", [P, TT, P], F32R),
            ("pa0", [P, SCORES], FP32),
            ("qk_raw", [P, 2, S], FP32), ("sq", [P, 2, S], FP32), ("rn", [P, 2, S], FP32), ("nt", [P, 2, S], FP32))
        pa = (pa0, pa1)
        keep0, keep1, suffix = region(64 + 59, ("keep0", [P, SCORES], FP32), ("keep1", [P, SCORES], FP32),
                                    ("suffix", [P, SCORES + TT], FP32))
        keep = (keep0, keep1)
        u_pad, = region(64, ("u_pad", [P, 4, 16 + S], FP32))
        win, = region(73, ("win", [P, 2, 16 + S], FP32))
        pl_hi, = region(80, ("pl_hi", [P, 2, S], F32R))
        wp_hi, wp_lo, wp_raw = region(89, ("wp_hi", [P, 4, P], F32R), ("wp_lo", [P, 4, P], F32R),
                                      ("wp_raw", [P, 4, P], FP32))
        pl_lo, pl = region(96, ("pl_lo", [P, 2, S], F32R), ("pl", [P, S], FP32))
        m_hi, m_lo, oc_hi, oc_lo, x_re, mg = region(
            80, ("m_hi", [P, KD, S], F32R), ("m_lo", [P, KD, S], F32R),
            ("oc_hi", [P, KB, S], F32R), ("oc_lo", [P, KB, S], F32R),
            ("x_re", [P, 2, D], FP32), ("mg", [P, 4, S], FP32))
        x_t, x1_t, act_sb = region(0, ("x_t", [P, KD, S], FP32), ("x1_t", [P, KD, S], FP32),
                                ("act", [P, KF, S], FP32))
        x1, conv_in, conv_out, sg, r_ffn, ffn_t = region(
            76, ("x1", [P, TT, D], FP32), ("conv_in", [P, 4, 2 + S], FP32), ("conv_out", [P, 4, S], FP32),
            ("sg", [P, 2, S], FP32), ("r_ffn", [P, S], FP32), ("ffn_t", [P, 2, S], FP32))
        sq_x1, ss_x1 = region(132, ("sq_x1", [P, 2, S], FP32), ("ss_x1", [P, S], FP32))
        a_hi, a_lo = region(124, ("a_hi", [P, 2, S], F32R), ("a_lo", [P, 2, S], F32R))
        out_sb, = region(92, ("out_sb", [P, 8, S], FP32))

        ps = ctx.enter_context(nc.psum_tensor("ps", [P, 8, S], FP32))
        frow_dram = nc.dram_tensor("rel_bias_rows", (8, REL_ROW), FP32, kind="Internal").ap()

        x_landed = [sem(f"x_landed{t}") for t in range(TT)]
        gmix_landed, gmix_in_psum, gmix_ready = sem("gmix_landed"), sem("gmix_in_psum"), sem("gmix_ready")
        rows_landed, rel_landed, bias_landed, frow_stored = (sem("rows_landed"), sem("rel_landed"),
                                                             sem("bias_landed"), sem("frow_stored"))
        wp_landed = sem("wp_landed")
        xre_landed = [sem("xre_landed0"), sem("xre_landed1")]
        w_landed = [sem("w_landed0"), sem("w_landed1")]
        hi_ready, lo_ready, unit_done = sem("hi_ready"), sem("lo_ready"), sem("unit_done")
        const_step, const_ready, rows_zero = sem("const_step"), sem("const_ready"), sem("rows_zero")
        par_in_psum, par_ready = sem("par_in_psum"), sem("par_ready")
        ssq_done, ln_done, exp0_done, tok_step, rstd_ready = (sem("ssq_done"), sem("ln_done"), sem("exp0_done"),
                                                              sem("tok_step"), sem("rstd_ready"))
        xs_ready, xs_used, h_hi_ready, h_lo_ready = sem("xs_ready"), sem("xs_used"), sem("h_hi_ready"), sem("h_lo_ready")
        frow_step, frow_ready, bias_ready = sem("frow_step"), sem("frow_ready"), sem("bias_ready")
        v_stored = sem("v_stored")
        proj_raw, proj_sq = sem("proj_raw"), sem("proj_sq")
        ss_done, ms_done, lnq_done, expq_done, newton_step, rn_ready = (
            sem("ss_done"), sem("ms_done"), sem("lnq_done"), sem("expq_done"), sem("newton_step"), sem("rn_ready"))
        heads_step = sem("heads_step")
        refined, gain_ready = sem("refined"), sem("gain_ready")
        hat_ready, qk_hi_ready, qk_lo_ready = sem("hat_ready"), sem("qk_hi_ready"), sem("qk_lo_ready")
        s_done, negmax_ready, exp_done, recip_done, p_ready = (
            sem("s_done"), sem("negmax_ready"), sem("exp_done"), sem("recip_done"), sem("p_ready"))
        keep_done, beta_done, scan_done = sem("keep_done"), sem("beta_done"), sem("scan_done")
        suffix_init = sem("suffix_init")
        t_done, pt_hi_ready, pt_lo_ready = sem("t_done"), sem("pt_hi_ready"), sem("pt_lo_ready")
        vp_hi_ready, vp_lo_ready = sem("vp_hi_ready"), sem("vp_lo_ready")
        pv_done, o_hi_ready, o_lo_ready = sem("pv_done"), sem("o_hi_ready"), sem("o_lo_ready")
        gate_stored = sem("gate_stored")
        u_init, u_stored, win_step, pl_step, pl_ready = (sem("u_init"), sem("u_stored"), sem("win_step"),
                                                         sem("pl_step"), sem("pl_ready"))
        inv_step = sem("inv_step")
        win_ready = sem("win_ready")
        pl_hi_ready, pl_lo_ready, wp_hi_ready, wp_lo_ready = (sem("pl_hi_ready"), sem("pl_lo_ready"),
                                                              sem("wp_hi_ready"), sem("wp_lo_ready"))
        mix_done, oc_hi_ready, oc_lo_ready = sem("mix_done"), sem("oc_hi_ready"), sem("oc_lo_ready")
        sig_ab, sig_c, mg_step, mg_ready = sem("sig_ab"), sem("sig_c"), sem("mg_step"), sem("mg_ready")
        m_hi_ready, m_lo_ready = sem("m_hi_ready"), sem("m_lo_ready")
        xre_t_done, xt_stored = sem("xre_t_done"), sem("xt_stored")
        x1_total = sem("x1_total")
        x1_ready, x1_sq, x1_ss, h2_hi, h2_lo = (sem("x1_ready"), sem("x1_sq"), sem("x1_ss"), sem("h2_hi"), sem("h2_lo"))
        x1_ln, x1_exp, x1_ms, ffn_step, r_ready = (sem("x1_ln"), sem("x1_exp"), sem("x1_ms"), sem("ffn_step"), sem("r_ready"))
        x1n_t_done, x1n_stored = sem("x1n_t_done"), sem("x1n_stored")
        cin_zero, cin_ready, tap_init, tap1_done, conv_done = (sem("cin_zero"), sem("cin_ready"), sem("tap_init"),
                                                    sem("tap1_done"), sem("conv_done"))
        sg_ready, silu_ready, act_ready = sem("sg_ready"), sem("silu_ready"), sem("act_ready")
        a_hi_ready, a_lo_ready = sem("a_hi_ready"), sem("a_lo_ready")
        bank_done, out_ready, out_stored = sem("bank_done"), sem("out_ready"), sem("out_stored")

        block = ctx.enter_context(nc.Block())

        def r32(ap):
            return ap.bitcast(FP32)

        def segs():
            return [(qt, S_OFF[qt], P * (qt + 1)) for qt in (3, 2, 0, 1)]

        def seg2(qt):
            return S_OFF[qt] + (0, 1, 2, 3)[(3, 2, 0, 1).index(qt)]

        xw = x[0].rearrange("(t p) d -> p t d", p=P)
        win_v = w_in[0].rearrange("(k p) (j c) -> p k j c", p=P, c=P)
        win_c = w_in[0].rearrange("(k p) c -> p k c", p=P)
        wa_v, wb_v, wc_v = (w[0].rearrange("(k p) (j c) -> p k j c", p=P, c=P)
                            for w in (w_branch_a, w_branch_b, w_branch_c))
        wo_v = w_out[0].rearrange("(k p) (j c) -> p k j c", p=P, c=P)
        wu_v = w_up[0].rearrange("(k p) (j c) -> p k j c", p=P, c=P)
        wd_v = w_down[0].rearrange("(k p) (h c) -> p k h c", p=P, h=2)
        out_v = out[0].rearrange("(t p) (h d) -> p t h d", p=P, h=2)

        @block.sync
        def _(sp):
            for t in range(TT):
                sp.dma_start(x_in[:, t, :], xw[:, t, :]).then_inc(x_landed[t], 16)

            def load(n, slot, halves):
                if not (isinstance(n, int) and n < 2):
                    sp.wait_ge(lo_ready, n - 1)
                for i, src in enumerate(halves):
                    k, c = src.shape[1], src.shape[-1]
                    dst = w_raw[:, slot, i * k * c:(i + 1) * k * c].rearrange("p (k c) -> p k c", k=k)
                    sp.dma_start(dst, src).then_inc(w_landed[slot], 16)

            def cols(n, slot, view, j):
                load(n, slot, [view[:, 0:4, j, :], view[:, 4:8, j, :]])

            def values(n0, c0):
                for u in range(4):
                    load(n0 + u, u % 2, [win_c[:, 2 * u + i:2 * u + i + 1, c0:c0 + WB] for i in range(2)])

            cols(N_QK0, 0, win_v, Q_A)
            cols(N_QK0 + 1, 1, win_v, K_A)
            values(N_VA, V_A * P)
            values(N_VB, V_B * P)

            def slot(s, qj, kj):
                b = N_SLOT + 4 * s
                cols(b, 0, win_v, qj)
                cols(b + 1, 1, win_v, kj)
                cols(b + 2, 0, win_v, GATE + 2 * s)
                cols(b + 3, 1, win_v, GATE + 2 * s + 1)

            slot(0, Q_A + 1, K_A + 1)
            with sp.Fori(1, 3) as s:
                slot(s, s + (Q_A + 1), s + (K_A + 1))
            slot(3, Q_B, K_B)
            with sp.Fori(4, 7) as s:
                slot(s, s + (Q_B - 3), s + (K_B - 3))
            b = N_SLOT + 28
            for i in range(4):
                cols(b + i, i % 2, win_v, U_C + i)
            sp.wait_ge(negmax_ready, 8 * TT)
            sp.dma_start(wp_raw[:, :, :], w_pool[0].rearrange("g c e -> c g e")).then_inc(wp_landed, 16)
            for i in range(2):
                cols(b + 4 + i, i, win_v, GATE + 14 + i)
            with sp.Fori(0, KD // 2) as mm:
                for i in range(2):
                    m = mm * 2 + i
                    n = mm * 6 + (N_MERGE + 3 * i)
                    load(n, i, [wa_v[:, :, m, :], wb_v[:, :, m, :]])
                    cols(n + 1, 1 - i, win_v, m + (GATE + 2 * KD))
                    load(n + 2, i, [wc_v[:, 0:2, m, :], wc_v[:, 2:4, m, :]])
            sp.dma_start(x_re[:, :, :], xw[:, 0:2, :]).then_inc(xre_landed[0], 16)
            cols(N_OUT, 0, wo_v, 0)
            cols(N_OUT + 1, 1, wo_v, 1)
            sp.wait_ge(xre_t_done, 1)
            sp.dma_start(x_re[:, :, :], xw[:, 2:4, :]).then_inc(xre_landed[1], 16)
            with sp.Fori(1, KD // 2) as mm:
                for i in range(2):
                    cols(mm * 2 + (N_OUT + i), i, wo_v, mm * 2 + i)
            with sp.Fori(0, KF) as j:
                cols(j * 2 + N_UP, 0, wu_v, j)
                cols(j * 2 + (N_UP + 1), 1, wu_v, j + KF)
            with sp.Fori(0, KF // 2) as kk:
                for i in range(2):
                    load(kk * 2 + (N_DOWN + i), i, [wd_v[:, bass.ds(kk * 2 + i, 1), h, :] for h in range(2)])
            for b8 in range(8):
                sp.wait_ge(out_ready, b8 + 1)
                sp.dma_start(out_v[:, b8 // 2, b8 % 2, :], out_sb[:, b8, :]).then_inc(out_stored, 16)
            sp.wait_ge(out_stored, 8 * 16)

        @block.gpsimd
        def _(pool):
            pool.memset(rows[:, :, :], 0.0).then_inc(rows_zero, 1)
            pool.memset(ident[:, :], 0.0).then_inc(const_step, 1)
            pool.memset(ones_all[:, :], 1.0)
            pool.memset(eps[:, :], EPS)
            pool.memset(masked[:, 0, :], MASKED)
            pool.memset(masked[:, 1, :], 0.0)
            pool.memset(ident_b[:, :], 0.0)
            pool.memset(causal_b[:, :], 0.0).then_inc(const_step, 1)
            pool.wait_ge(const_step, 2)
            pool.affine_select(out=ident_b[:, :], in_=ident_b[:, :], compare_op=ALU.not_equal, fill=1.0, base=0,
                               pattern=[[-1, P]], channel_multiplier=1)
            pool.affine_select(out=causal_b[:, :], in_=causal_b[:, :], compare_op=ALU.is_gt, fill=MASKED, base=0,
                               pattern=[[-1, P]], channel_multiplier=1)
            pool.affine_select(out=ident[:, :], in_=ident[:, :], compare_op=ALU.not_equal, fill=1.0, base=0,
                               pattern=[[-1, P]], channel_multiplier=1).then_inc(const_ready, 1)
            pool.wait_ge(frow_ready, 3)
            pool.dma_start(frow_dram[:, :], frow[:, 0, :]).then_inc(frow_stored, 16)
            pool.wait_ge(frow_stored, 16)
            windows = bass.AP(frow_dram.tensor, 0, [[REL_ROW, 8], [1, P], [1, S]])

            def bias_load(hh, h):
                if not (isinstance(hh, int) and hh < 2):
                    pool.wait_ge(negmax_ready, hh * 4 - 4)
                pool.dma_start(bias_rev[:, h, :], windows[hh, :, :]).then_inc(bias_landed, 16)
                pool.wait_ge(bias_landed, hh * 16 + 16)
                pool.tensor_tensor(bias_rev[0:HD, h, 0:HD], masked[0:HD, 0, :], masked[0:HD, 1, :], ALU.add)\
                    .then_inc(bias_ready, 1)

            bias_load(0, 0)
            bias_load(1, 1)

            def newton(t, i):
                pool.wait_ge(expq_done, t + 1)
                pool.tensor_tensor(nt[:, i, :], rn[:, i, :], rn[:, i, :], ALU.mult).then_inc(newton_step, 1)
                pool.wait_ge(newton_step, t + 1)
                pool.tensor_tensor(nt[:, i, :], nt[:, i, :], sq[:, i, :], ALU.mult).then_inc(rn_ready, 1)

            newton(0, 0)
            newton(1, 1)
            with pool.Fori(0, 3) as s:
                bias_load(s * 2 + 2, 0)
                newton(s * 2 + 2, 0)
                bias_load(s * 2 + 3, 1)
                newton(s * 2 + 3, 1)

            step = 0
            for g, w in enumerate(WINDOWS):
                pool.wait_ge(u_stored, g + 1)
                src, width, n = u_pad[:, g, :], 1, 0
                if g >= 1:
                    pool.wait_ge(pl_ready, g)
                while width < w:
                    lo = 2 * width - 1
                    dst = win[:, n % 2, :]
                    ins = pool.tensor_tensor(dst[:, lo:16 + S], src[:, lo:16 + S],
                                             src[:, lo - width:16 + S - width], ALU.add)
                    src, width, n = dst, 2 * width, n + 1
                    if width < w:
                        step += 1
                        ins.then_inc(win_step, 1)
                        pool.wait_ge(win_step, step)
                ins.then_inc(win_ready, 1)

            def x1_sum(m, i):
                pool.wait_ge(x1_sq, m + 1)
                pool.tensor_tensor(ss_x1[:, :], sq_x1[:, (i + 1) % 2, :] if isinstance(m, int) and m == 1
                                   else ss_x1[:, :], sq_x1[:, i, :], ALU.add).then_inc(x1_ss, 1)

            x1_sum(1, 1)
            for m in range(2, 4):
                pool.wait_ge(x1_ss, m - 1)
                x1_sum(m, m % 2)
            with pool.Fori(2, KD // 2) as mm:
                for i in range(2):
                    pool.wait_ge(x1_ss, mm * 2 + (i - 1))
                    x1_sum(mm * 2 + i, i)

            with pool.Fori(0, KF // 2) as jj:
                for i in range(2):
                    j = jj * 2 + i
                    pool.wait_ge(sg_ready, j + 1)
                    pool.tensor_tensor(sg[:, i, :], sg[:, i, :], conv_out[:, 2 * i, :], ALU.mult).then_inc(silu_ready, 1)
                    pool.wait_ge(silu_ready, j + 1)
                    pool.wait_ge(conv_done, j * 2 + 2)
                    pool.tensor_tensor(act_sb[:, j, :],
                                       sg[:, i, :], conv_out[:, 2 * i + 1, :], ALU.mult).then_inc(act_ready, 1)

        @block.scalar
        def _(act_e):
            a = act_e
            act = nc.scalar.activation
            a.dma_start(g_row[:, :], norm_mix[0].rearrange("(k c) -> k c", c=P)).then_inc(gmix_landed, 16)
            a.wait_ge(rows_zero, 1)
            for src, (t, c), n in ((conv_w[0, 0], CW0, 44), (conv_w[0, 1], CW1, 44), (b_gate[0], BG, 24),
                                   (norm_ffn[0], GF, 8), (conv_w[0, 2], CW2, 44),
                                   (conv_b[0], CB, 44), (pool_scale[0], PSC, 4)):
                a.dma_start(rows[c:c + n, t, :], src.rearrange("(r c) -> r c", c=P)).then_inc(rows_landed, 16)
            for src, (t, c) in ((q_norm_a, GQ), (k_norm_a, GK)):
                for i in range(2):
                    a.dma_start(rows[c:c + 1, t, i * HD:(i + 1) * HD], src[:, :]).then_inc(rows_landed, 16)
            a.dma_start(frow[:, 1, 0:REL], rel_bias_a[0]).then_inc(rel_landed, 16)

            def hi(n, slot):
                a.wait_ge(w_landed[slot], ((n // 2 + 1) * 32) if isinstance(n, int) else 0)
                if not (isinstance(n, int) and n < 2):
                    a.wait_ge(unit_done, n - 1)
                act(w_hi[:, slot, :], w_raw[:, slot, :], ACT.Copy).then_inc(hi_ready, 1)

            def hi_at(n, slot, half):
                a.wait_ge(w_landed[slot], half * 32 + 32)
                a.wait_ge(unit_done, n - 1)
                act(w_hi[:, slot, :], w_raw[:, slot, :], ACT.Copy).then_inc(hi_ready, 1)

            a.preload_act_table_set("natural_log_exp_and_others")
            a.wait_ge(const_ready, 1)
            for t in range(TT):
                a.wait_ge(x_landed[t], 16)
                act(squares[:, t, :], x_in[:, t, :], ACT.Square, accum_out=tok[:, 0, t:t + 1]).then_inc(ssq_done, 1)
                a.wait_ge(ssq_done, t + 1)
                act(tok[:, 2, t:t + 1], tok[:, 0, t:t + 1], ACT.Ln, scale=1.0 / D, bias=eps[:, :]).then_inc(ln_done, 1)
                a.wait_ge(ln_done, t + 1)
                act(tok[:, 3, t:t + 1], tok[:, 2, t:t + 1], ACT.Exp, scale=-0.5).then_inc(exp0_done, 1)
            hi(0, 0)
            a.wait_ge(gmix_ready, 1)
            a.wait_ge(xs_used, TT)
            for k in range(KD):
                act(h_hi[:, k, :], ps[:, k, :], ACT.Copy, scale=g_mix[:, k:k + 1]).then_inc(h_hi_ready, 1)
            hi(1, 1)

            def after(n):
                hi(n + 2, n % 2)

            def proj_a(t, i, bank, used, prev):
                a.wait_ge(unit_done, used)
                if prev:
                    a.wait_ge(qk_lo_ready, t - 1)
                act(qk_raw[:, i, :], ps[:, bank, :], ACT.Copy).then_inc(proj_raw, 1)
                act(sq[:, i, :], ps[:, bank, :], ACT.Square).then_inc(proj_sq, 1)

            def norm_a(t, i, bank):
                a.wait_ge(ss_done, t + 1)
                act(sq[:, i, :], ps[:, bank, :], ACT.Identity, scale=1.0 / HD, bias=eps[:, :]).then_inc(ms_done, 1)
                a.wait_ge(ms_done, t + 1)
                act(rn[:, i, :], sq[:, i, :], ACT.Ln).then_inc(lnq_done, 1)
                a.wait_ge(lnq_done, t + 1)
                act(rn[:, i, :], rn[:, i, :], ACT.Exp, scale=-0.5).then_inc(expq_done, 1)

            def hat_hi(t, i):
                a.wait_ge(hat_ready, t + 1)
                act(qk_hi[:, i, :], qk_raw[:, i, :], ACT.Copy).then_inc(qk_hi_ready, 1)

            proj_a(0, 0, 0, N_QK0 + 1, False)
            after(N_QK0)
            proj_a(1, 1, 1, N_QK0 + 2, False)
            after(N_QK0 + 1)
            after(N_VA)
            norm_a(0, 0, 6)
            norm_a(1, 1, 7)
            after(N_VA + 1)
            hat_hi(0, 0)
            hat_hi(1, 1)
            after(N_VA + 2)
            after(N_VA + 3)
            act(v_a[:, :, :], ps[:, V_A_BANKS[0]:V_A_BANKS[0] + 4, :], ACT.Copy).then_inc(v_stored, 1)
            for u in range(3):
                after(N_VB + u)
            a.wait_ge(unit_done, N_VB + 4)
            act(v_b[:, 0:2, :], ps[:, V_B_BANKS[0]:V_B_BANKS[0] + 2, :], ACT.Copy).then_inc(v_stored, 1)
            after(N_VB + 3)
            a.wait_ge(par_ready, 1)
            a.wait_ge(v_stored, 3)

            def attn_probs(s, h, branch):
                hh = s * 2 + h
                if branch == "A":
                    for i, (qt, c, n) in enumerate(segs()):
                        a.wait_ge(negmax_ready, hh * 4 + (i + 1))
                        act(pa[h][:, c:c + n], pa[h][:, c:c + n], ACT.Exp, scale=-1.0, bias=hstat[:, h, 0, qt:qt + 1],
                            accum_out=hstat[:, h, 1, qt:qt + 1]).then_inc(exp_done, 1)
                else:
                    a.wait_ge(s_done, s + 1)
                    a.wait_ge(t_done, hh - 1)
                    flat = ps[:, HEAD[h]:HEAD[h] + 3, :].rearrange("p b c -> p (b c)")[:, 0:SCORES]
                    act(keep[h][:, :], flat, ACT.Sigmoid, scale=-0.125).then_inc(keep_done, 1)
                    act(pa[h][:, 0:SCORES], flat, ACT.Sigmoid, scale=0.125).then_inc(beta_done, 1)

            def vp_split_hi(s, v, pair, first):
                if not first:
                    a.wait_ge(pv_done, s * 2)
                cols = slice(pair * P, pair * P + P) if isinstance(pair, int) else bass.ds(pair * P, P)
                act(vp_hi[:, :, :], v[:, :, cols], ACT.Copy).then_inc(vp_hi_ready, 1)

            def pt_split_hi(s, h, first):
                a.wait_ge(t_done, s * 2 + h + 1)
                if not first:
                    a.wait_ge(pv_done, s * 2 + h)
                flat = ps[:, HEAD[h]:HEAD[h] + 3, :].rearrange("p b c -> p (b c)")[:, 0:SCORES]
                act(pt_hi[:, :], flat, ACT.Copy).then_inc(pt_hi_ready, 1)

            def o_split_hi(s, h):
                a.wait_ge(pv_done, s * 2 + h + 1)
                rowsl = slice(HD * h, HD * h + HD)
                dst = o_hi[rowsl, s, :]
                act(dst, ps[rowsl, HEAD[h], :], ACT.Copy).then_inc(o_hi_ready, 1)

            def gate_store(g, bank, used):
                a.wait_ge(unit_done, used)
                dst = gates[:, g, :]
                act(dst, ps[:, bank, :], ACT.Identity, bias=pcol(BG, g)).then_inc(gate_stored, 1)

            def slot(s, attn, proj):
                b = s * 4 + N_SLOT
                half = s * 2 + N_SLOT // 2
                first = isinstance(s, int) and s == 0
                if attn == "A":
                    vp_split_hi(s, v_a, s, first)
                    attn_probs(s, 0, attn)
                    attn_probs(s, 1, attn)
                else:
                    attn_probs(s, 0, attn)
                    attn_probs(s, 1, attn)
                    vp_split_hi(s, v_b, s - 4, False)
                t = s * 2 + 2
                if proj == "A":
                    proj_a(t, 0, PROJ[0], b + 1, True)
                elif proj == "B":
                    a.wait_ge(unit_done, b + 1)
                    act(qk_hi[:, 0, :], ps[:, PROJ[0], :], ACT.Copy).then_inc(qk_hi_ready, 1)
                hi_at(b + 2, 0, half + 1)
                pt_split_hi(s, 0, first)
                if proj == "A":
                    proj_a(t + 1, 1, PROJ[1], b + 2, True)
                    norm_a(t, 0, HEAD[0] + 1)
                elif proj == "B":
                    a.wait_ge(unit_done, b + 2)
                    act(qk_hi[:, 1, :], ps[:, PROJ[1], :], ACT.Copy).then_inc(qk_hi_ready, 1)
                hi_at(b + 3, 1, half + 1)
                o_split_hi(s, 0)
                pt_split_hi(s, 1, False)
                if proj == "A":
                    norm_a(t + 1, 1, HEAD[0] + 2)
                hi_at(b + 4, 0, half + 2)
                gate_store(s * 2, PROJ[0], b + 3)
                if proj == "A":
                    hat_hi(t, 0)
                    hat_hi(t + 1, 1)
                o_split_hi(s, 1)
                hi_at(b + 5, 1, half + 2)
                gate_store(s * 2 + 1, PROJ[1], b + 4)

            slot(0, "A", "A")
            a.preload_act_table_set("natural_log_exp_and_others")
            with a.Fori(1, 3) as s:
                slot(s, "A", "A")
            slot(3, "A", "B")
            a.preload_act_table(ACT.Sigmoid)
            with a.Fori(4, 7) as s:
                slot(s, "B", "B")

            s, b = 7, N_SLOT + 28
            half = b // 2
            attn_probs(s, 0, "B")
            attn_probs(s, 1, "B")
            vp_split_hi(s, v_b, 3, False)

            def u_store(i, bank):
                a.wait_ge(unit_done, b + i + 1)
                if i == 0:
                    a.wait_ge(u_init, 1)
                act(u_pad[:, i, 16:16 + S], ps[:, bank, :], ACT.Copy).then_inc(u_stored, 1)

            u_store(0, PROJ[0])
            hi_at(b + 2, 0, half + 1)
            pt_split_hi(s, 0, False)
            u_store(1, PROJ[1])
            hi_at(b + 3, 1, half + 1)
            a.wait_ge(wp_landed, 16)
            act(wp_hi[:, :, :], wp_raw[:, :, :], ACT.Copy).then_inc(wp_hi_ready, 1)
            o_split_hi(s, 0)
            pt_split_hi(s, 1, False)
            hi_at(b + 4, 0, half + 2)
            u_store(2, PROJ[0])
            o_split_hi(s, 1)
            hi_at(b + 5, 1, half + 2)
            u_store(3, PROJ[1])

            def pl_hi_split(g):
                a.wait_ge(pl_ready, g + 1)
                if g >= 2:
                    a.wait_ge(mix_done, g - 1)
                act(pl_hi[:, g % 2, :], pl[:, :], ACT.Copy).then_inc(pl_hi_ready, 1)

            def oc_split_hi(g):
                a.wait_ge(mix_done, g + 1)
                act(oc_hi[:, g, :], ps[:, MIX + g, :], ACT.Copy, scale=pcol(PSC, g)).then_inc(oc_hi_ready, 1)

            pl_hi_split(0)
            pl_hi_split(1)
            hi(b + 6, 0)
            gate_store(14, PROJ[0], b + 5)
            hi(b + 7, 1)
            gate_store(15, PROJ[1], b + 6)
            pl_hi_split(2)
            pl_hi_split(3)

            a.wait_ge(gate_stored, 2 * KD)

            def merge(mm, i, first):
                m = mm * 2 + i
                n = mm * 6 + (N_MERGE + 3 * i)
                h3 = mm * 3
                for br in range(2):
                    g = gates[:, m + KD * br, :]
                    last = act(g, g, ACT.Sigmoid)
                last.then_inc(sig_ab, 1)
                hi_at(n + 2, i, h3 + ((N_MERGE + 3 * i + 2) // 2))
                hi_at(n + 3, 1 - i, h3 + ((N_MERGE + 3 * i + 3) // 2))
                a.wait_ge(unit_done, n + 2)
                act(mg[:, 3, :], ps[:, 4 * i + 2, :], ACT.Sigmoid, bias=pcol(BG, m + 2 * KD)).then_inc(sig_c, 1)
                if first:
                    for g in range(4):
                        oc_split_hi(g)
                hi_at(n + 4, i, h3 + ((N_MERGE + 3 * i + 4) // 2))
                a.wait_ge(mg_ready, m + 1)
                act(m_hi[:, m, :], mg[:, 0, :], ACT.Copy).then_inc(m_hi_ready, 1)

            merge(0, 0, True)
            merge(0, 1, False)
            with a.Fori(1, KD // 2) as mm:
                merge(mm, 0, False)
                merge(mm, 1, False)

            a.preload_act_table_set("natural_log_exp_and_others")

            def xt_store(half_no):
                a.wait_ge(xre_t_done, half_no + 1)
                for i in range(4):
                    src = ps[:, 4 + i, :].rearrange("p (k t) -> p k t", k=2)
                    act(x_t[:, 2 * i:2 * i + 2, half_no * 256:half_no * 256 + 256], src, ACT.Copy)\
                        .then_inc(xt_stored, 1)

            def out_tile(m, i, h2):
                a.wait_ge(x1_ready, m + 1)
                x1m = x1_t[:, m, :]
                if not (isinstance(m, int) and m < 2):
                    a.wait_ge(x1_ss, m - 1)
                act(sq_x1[:, i, :], x1m, ACT.Square).then_inc(x1_sq, 1)
                hm = h_hi[:, m, :]
                act(hm, x1m, ACT.Copy, scale=pcol(GF, m)).then_inc(h2_hi, 1)

            xt_store(0)
            hi(N_OUT + 2, 0)
            xt_store(1)
            hi(N_OUT + 3, 1)
            out_tile(0, 0, None)
            out_tile(1, 1, None)
            with a.Fori(1, KD // 2) as mm:
                for i in range(2):
                    n = mm * 2 + (N_OUT + i)
                    hi_at(n + 2, i, mm + (N_OUT // 2 + 1))
                    out_tile(mm * 2 + i, i, None)
            a.wait_ge(x1_total, 1)
            act(ffn_t[:, 0, :], ps[:, 2, :], ACT.Identity, scale=1.0 / D, bias=eps[:, :]).then_inc(x1_ms, 1)
            a.wait_ge(x1_ms, 1)
            act(ffn_t[:, 1, :], ffn_t[:, 0, :], ACT.Ln).then_inc(x1_ln, 1)
            a.wait_ge(x1_ln, 1)
            act(r_ffn[:, :], ffn_t[:, 1, :], ACT.Exp, scale=-0.5).then_inc(x1_exp, 1)
            def x1_store(half_no):
                a.wait_ge(x1n_t_done, half_no + 1)
                for t in range(TT):
                    last = act(x1[:, t, half_no * S:half_no * S + S], ps[:, 4 + t, :], ACT.Copy)
                last.then_inc(x1n_stored, 1)

            x1_store(0)

            a.preload_act_table(ACT.Sigmoid)

            def up(jj, first):
                for i in range(2):
                    j = jj * 2 + i
                    n = jj * 4 + (N_UP + 2 * i)
                    for gv in range(2):
                        e = 2 * i + gv
                        hi_at(n + gv + 2, gv, jj * 2 + (N_UP // 2 + i + 1))
                        a.wait_ge(cin_ready, jj * 4 + (e + 1))
                        if not first:
                            a.wait_ge(act_ready, jj * 2 + (i - 1))
                        act(conv_out[:, e, :], conv_in[:, e, 2:2 + S], ACT.Identity, scale=pcol(CW2, j + KF * gv),
                            bias=pcol(CB, j + KF * gv)).then_inc(tap_init, 1)
                    a.wait_ge(conv_done, jj * 4 + (2 * i + 1))
                    act(sg[:, i, :], conv_out[:, 2 * i, :], ACT.Sigmoid).then_inc(sg_ready, 1)

            def a_split(k, slot, first):
                a.wait_ge(act_ready, k + 1)
                if not first:
                    a.wait_ge(unit_done, k + (N_DOWN - 1))
                act(a_hi[:, slot, :], act_sb[:, k, :], ACT.Copy).then_inc(a_hi_ready, 1)

            up(0, True)
            x1_store(1)
            with a.Fori(1, KF // 2 - 1) as jj:
                up(jj, False)
            a_split(0, 0, True)
            a_split(1, 1, True)
            up(KF // 2 - 1, False)

            with a.Fori(0, KF // 2 - 1) as kk:
                for i in range(2):
                    hi_at(kk * 2 + (N_DOWN + i + 2), i, kk + (N_DOWN // 2 + 1))
                    a_split(kk * 2 + (i + 2), i, False)

        @block.vector
        def _(d):
            v = nc.vector

            def lo(n, slot):
                d.wait_ge(hi_ready, n + 1)
                v.tensor_tensor(w_lo[:, slot, :], w_raw[:, slot, :], r32(w_hi[:, slot, :]), ALU.subtract)\
                    .then_inc(lo_ready, 1)

            v.memset(ones_heads[:, :], 0.0).then_inc(heads_step, 1)
            d.wait_ge(heads_step, 1)
            v.memset(ones_heads[0:HD, 0:HD], 1.0)
            v.memset(ones_heads[HD:P, HD:P], 1.0).then_inc(heads_step, 1)
            d.wait_ge(gmix_in_psum, 1)
            v.tensor_copy(g_mix[:, :], ps[:, 0, 0:KD]).then_inc(gmix_ready, 1)
            for t in range(TT):
                ms, r, c = tok[:, 1, t:t + 1], tok[:, 3, t:t + 1], tok[:, 4, t:t + 1]
                d.wait_ge(ssq_done, t + 1)
                v.tensor_scalar(ms, tok[:, 0, t:t + 1], 1.0 / D, EPS, ALU.mult, ALU.add).then_inc(tok_step, 1)
                d.wait_ge(exp0_done, t + 1)
                d.wait_ge(tok_step, 2 * t + 1)
                v.scalar_tensor_tensor(out=c, in0=r, scalar=ms, in1=r, op0=ALU.mult, op1=ALU.mult).then_inc(tok_step, 1)
                d.wait_ge(tok_step, 2 * t + 2)
                v.tensor_scalar(c, c, -0.5, 1.5, ALU.mult, ALU.add).then_inc(rstd_ready, 1)
                d.wait_ge(rstd_ready, t + 1)
                v.tensor_scalar(x_scaled[:, t, :], x_in[:, t, :], r, c, ALU.mult, ALU.mult).then_inc(xs_ready, 1)
            lo(N_QK0, 0)
            d.wait_ge(gmix_ready, 1)
            for k in range(KD):
                d.wait_ge(h_hi_ready, k + 1)
                v.scalar_tensor_tensor(out=h_lo[:, k, :], in0=ps[:, k, :], scalar=g_mix[:, k:k + 1],
                                       in1=r32(h_hi[:, k, :]), op0=ALU.mult, op1=ALU.subtract).then_inc(h_lo_ready, 1)
            lo(N_QK0 + 1, 1)
            d.wait_ge(rel_landed, 16)
            v.tensor_scalar(frow[:, 0, 64:64 + REL], frow[:, 1, 0:REL], 8.0, None, ALU.mult).then_inc(frow_ready, 1)
            d.wait_ge(frow_ready, 1)
            v.tensor_copy(frow[:, 0, 0:64], frow[:, 0, 64:65].to_broadcast([8, 64])).then_inc(frow_ready, 1)
            v.tensor_copy(frow[:, 0, 64 + REL:], frow[:, 0, 63 + REL:64 + REL].to_broadcast([8, REL_ROW - 64 - REL]))\
                .then_inc(frow_ready, 1)

            def hat(t, i):
                d.wait_ge(rn_ready, t + 1)
                d.wait_ge(proj_raw, t + 1)
                v.scalar_tensor_tensor(out=nt[:, i, :], in0=nt[:, i, :], scalar=-3.0, in1=rn[:, i, :],
                                       op0=ALU.add, op1=ALU.mult).then_inc(refined, 1)
                d.wait_ge(refined, t + 1)
                v.scalar_tensor_tensor(out=qk_raw[:, i, :], in0=qk_raw[:, i, :], scalar=qk_gain[:, i:i + 1],
                                       in1=nt[:, i, :], op0=ALU.mult, op1=ALU.mult).then_inc(hat_ready, 1)

            def hat_lo(t, i):
                d.wait_ge(qk_hi_ready, t + 1)
                v.tensor_tensor(qk_lo[:, i, :], qk_raw[:, i, :], r32(qk_hi[:, i, :]), ALU.subtract)\
                    .then_inc(qk_lo_ready, 1)

            lo(N_VA, 0)
            d.wait_ge(par_in_psum, 1)
            v.tensor_copy(par[:, :, :], ps[:, PAR_BANK, 0:2 * P].rearrange("p (t c) -> p t c", t=2)).then_inc(par_ready, 1)
            d.wait_ge(par_ready, 1)
            v.tensor_scalar(qk_gain[:, :], par[:, GQ[0], GQ[1]:GQ[1] + 2], -0.5, None, ALU.mult).then_inc(gain_ready, 1)
            d.wait_ge(gain_ready, 1)
            lo(N_VA + 1, 1)
            lo(N_VA + 2, 0)
            hat(0, 0)
            hat(1, 1)
            lo(N_VA + 3, 1)
            hat_lo(0, 0)
            hat_lo(1, 1)
            for u in range(5):
                lo(N_VB + u, u % 2)
            d.wait_ge(unit_done, N_VB + 4)
            v.tensor_copy(v_b[:, 2:4, :], ps[:, V_B_BANKS[2]:V_B_BANKS[2] + 2, :]).then_inc(v_stored, 1)
            lo(N_VB + 5, 1)

            def scores_of(h, c, n):
                return ps[:, HEAD[h]:HEAD[h] + 3, :].rearrange("p b c -> p (b c)")[:, c:c + n]

            def softmax_logits(s, h):
                for qt, c, n in segs():
                    v.tensor_tensor_reduce(out=pa[h][:, c:c + n], in0=scores_of(h, c, n), in1=bias_rev[:, h, n - 1::-1],
                                           scale=-0.125, scalar=-MASKED, op0=ALU.add, op1=ALU.min,
                                           accum_out=hstat[:, h, 0, qt:qt + 1]).then_inc(negmax_ready, 1)

            def softmax_scale(s, h):
                hh = s * 2 + h
                d.wait_ge(exp_done, hh * 4 + 4)
                v.reciprocal(hstat[:, h, 2, :], hstat[:, h, 1, :]).then_inc(recip_done, 1)
                d.wait_ge(recip_done, hh + 1)
                for qt, c, n in segs():
                    last = v.tensor_scalar(pa[h][:, c:c + n], pa[h][:, c:c + n], hstat[:, h, 2, qt:qt + 1], None, ALU.mult)
                last.then_inc(p_ready, 1)

            def sticks(s, h):
                hh = s * 2 + h
                d.wait_ge(keep_done, hh - 7)
                d.wait_ge(p_ready, hh)
                for qt, c, n in segs():
                    e = seg2(qt)
                    last = v.tensor_tensor_scan(rev(suffix, e, n), rev(keep[h], c, n), rev(keep[h], c, n), 1.0,
                                                ALU.mult, ALU.bypass)
                last.then_inc(scan_done, 1)
                d.wait_ge(scan_done, hh - 7)
                d.wait_ge(beta_done, hh - 7)
                for qt, c, n in segs():
                    e = seg2(qt)
                    last = v.tensor_tensor(pa[h][:, c:c + n], pa[h][:, c:c + n], suffix[:, e + 1:e + 1 + n], ALU.mult)
                last.then_inc(p_ready, 1)

            def rev(buf, c, n):
                return buf[:, c:c + n][:, ::-1]

            def vp_split_lo(s, vv, pair):
                d.wait_ge(vp_hi_ready, s + 1)
                cols = slice(pair * P, pair * P + P) if isinstance(pair, int) else bass.ds(pair * P, P)
                v.tensor_tensor(vp_lo[:, :, :], vv[:, :, cols], r32(vp_hi[:, :, :]), ALU.subtract)\
                    .then_inc(vp_lo_ready, 1)

            def pt_split_lo(s, h):
                d.wait_ge(pt_hi_ready, s * 2 + h + 1)
                v.tensor_tensor(pt_lo[:, :], scores_of(h, 0, SCORES), r32(pt_hi[:, :]), ALU.subtract).then_inc(pt_lo_ready, 1)

            def o_split_lo(s, h):
                d.wait_ge(o_hi_ready, s * 2 + h + 1)
                rw = slice(HD * h, HD * h + HD)
                at = s
                v.tensor_tensor(o_lo[rw, at, :], ps[rw, HEAD[h], :], r32(o_hi[rw, at, :]), ALU.subtract)\
                    .then_inc(o_lo_ready, 1)

            def raw_lo(t, i):
                d.wait_ge(qk_hi_ready, t + 1)
                v.tensor_tensor(qk_lo[:, i, :], ps[:, PROJ[i], :], r32(qk_hi[:, i, :]), ALU.subtract)\
                    .then_inc(qk_lo_ready, 1)

            def slot(s, attn, proj):
                b = s * 4 + N_SLOT
                first = isinstance(s, int) and s == 0
                t = s * 2 + 2
                if attn == "A":
                    d.wait_ge(s_done, s + 1)
                    d.wait_ge(bias_ready, s * 2 + 2)
                    if not first:
                        d.wait_ge(t_done, s * 2)
                    vp_split_lo(s, v_a, s)
                    softmax_logits(s, 0)
                    softmax_scale(s, 0)
                    softmax_logits(s, 1)
                else:
                    sticks(s, 0)
                    vp_split_lo(s, v_b, s - 4)
                if proj == "B":
                    raw_lo(t, 0)
                lo(b + 2, 0)
                pt_split_lo(s, 0)
                if attn == "A":
                    softmax_scale(s, 1)
                else:
                    sticks(s, 1)
                if proj == "B":
                    raw_lo(t + 1, 1)
                lo(b + 3, 1)
                o_split_lo(s, 0)
                pt_split_lo(s, 1)
                if proj == "A":
                    hat(t, 0)
                lo(b + 4, 0)
                if proj == "A":
                    hat(t + 1, 1)
                    hat_lo(t, 0)
                    hat_lo(t + 1, 1)
                o_split_lo(s, 1)
                lo(b + 5, 1)

            slot(0, "A", "A")
            with d.Fori(1, 3) as s:
                slot(s, "A", "A")
            slot(3, "A", "B")
            d.wait_ge(qk_lo_ready, 8)
            for qt in range(TT):
                c = seg2(qt) + P * (qt + 1)
                last = v.memset(suffix[:, c:c + 1], 1.0)
            last.then_inc(suffix_init, 1)
            d.wait_ge(suffix_init, 1)
            with d.Fori(4, 7) as s:
                slot(s, "B", "B")

            s, b = 7, N_SLOT + 28
            sticks(s, 0)
            vp_split_lo(s, v_b, 3)
            v.memset(u_pad[:, :, 0:16], 0.0).then_inc(u_init, 1)
            lo(b + 2, 0)
            pt_split_lo(s, 0)
            sticks(s, 1)
            lo(b + 3, 1)
            v.memset(inv[:, 0, :], 1.0).then_inc(inv_step, 1)
            d.wait_ge(inv_step, 1)
            v.tensor_tensor_scan(inv[:, 1, :], inv[:, 0, :], inv[:, 0, :], 0.0, ALU.add, ALU.bypass).then_inc(inv_step, 1)
            d.wait_ge(inv_step, 2)
            v.reciprocal(inv[:, 2, :], inv[:, 1, :]).then_inc(inv_step, 1)
            d.wait_ge(wp_hi_ready, 1)
            v.tensor_tensor(wp_lo[:, :, :], wp_raw[:, :, :], r32(wp_hi[:, :, :]), ALU.subtract).then_inc(wp_lo_ready, 1)
            o_split_lo(s, 0)
            pt_split_lo(s, 1)
            lo(b + 4, 0)
            o_split_lo(s, 1)
            lo(b + 5, 1)
            d.wait_ge(inv_step, 3)
            step = [0]

            def pooled(g):
                w = WINDOWS[g]
                d.wait_ge(win_ready, g + 1)
                if g:
                    d.wait_ge(pl_lo_ready, g)
                sums = win[:, g % 2, :]
                v.scalar_tensor_tensor(out=pl[:, :], in0=sums[:, 16:], scalar=1.0 / w, in1=u_pad[:, g, 16:],
                                       op0=ALU.mult, op1=ALU.subtract).then_inc(pl_step, 1)
                d.wait_ge(pl_step, 2 * g + 1)
                v.tensor_tensor(pl[:, 0:w - 1], sums[:, 16:15 + w], inv[:, 2, 0:w - 1], ALU.mult).then_inc(pl_step, 1)
                d.wait_ge(pl_step, 2 * g + 2)
                v.tensor_tensor(pl[:, 0:w - 1], pl[:, 0:w - 1], u_pad[:, g, 16:15 + w], ALU.subtract)\
                    .then_inc(pl_ready, 1)
                d.wait_ge(pl_hi_ready, g + 1)
                v.tensor_tensor(pl_lo[:, g % 2, :], pl[:, :], r32(pl_hi[:, g % 2, :]), ALU.subtract)\
                    .then_inc(pl_lo_ready, 1)

            def oc_split_lo(g):
                d.wait_ge(oc_hi_ready, g + 1)
                v.scalar_tensor_tensor(out=oc_lo[:, g, :], in0=ps[:, MIX + g, :], scalar=pcol(PSC, g),
                                       in1=r32(oc_hi[:, g, :]), op0=ALU.mult, op1=ALU.subtract).then_inc(oc_lo_ready, 1)

            pooled(0)
            pooled(1)
            lo(b + 6, 0)
            lo(b + 7, 1)
            pooled(2)
            pooled(3)

            def merge(mm, i, first):
                m = mm * 2 + i
                n = mm * 6 + (N_MERGE + 3 * i)
                bank = 4 * i
                gm = [gates[:, m + KD * br, :] for br in range(2)]
                lo(n + 2, i)
                if not first:
                    d.wait_ge(m_lo_ready, m)
                d.wait_ge(sig_ab, m + 1)
                d.wait_ge(unit_done, n + 1)
                v.tensor_tensor(mg[:, 0, :], ps[:, bank, :], gm[0], ALU.mult)
                v.tensor_tensor(mg[:, 1, :], ps[:, bank + 1, :], gm[1], ALU.mult).then_inc(mg_step, 1)
                d.wait_ge(mg_step, m * 3 + 1)
                v.tensor_tensor(mg[:, 0, :], mg[:, 0, :], mg[:, 1, :], ALU.add).then_inc(mg_step, 1)
                lo(n + 3, 1 - i)
                if first:
                    for g in range(4):
                        oc_split_lo(g)
                d.wait_ge(sig_c, m + 1)
                d.wait_ge(unit_done, n + 3)
                v.tensor_tensor(mg[:, 2, :], ps[:, bank + 3, :], mg[:, 3, :], ALU.mult).then_inc(mg_step, 1)
                d.wait_ge(mg_step, m * 3 + 3)
                v.tensor_tensor(mg[:, 0, :], mg[:, 0, :], mg[:, 2, :], ALU.add).then_inc(mg_ready, 1)
                lo(n + 4, i)
                d.wait_ge(m_hi_ready, m + 1)
                at = m
                v.tensor_tensor(m_lo[:, at, :], mg[:, 0, :], r32(m_hi[:, at, :]), ALU.subtract).then_inc(m_lo_ready, 1)

            merge(0, 0, True)
            merge(0, 1, False)
            with d.Fori(1, KD // 2) as mm:
                merge(mm, 0, False)
                merge(mm, 1, False)

            def out_tile(m, bank):
                d.wait_ge(unit_done, m + (N_OUT + 1))
                at = m
                v.tensor_tensor(x1_t[:, at, :], ps[:, bank, :], x_t[:, at, :], ALU.add).then_inc(x1_ready, 1)

            def h2_split_lo(m):
                d.wait_ge(h2_hi, m + 1)
                at = m
                v.scalar_tensor_tensor(out=h_lo[:, at, :], in0=x1_t[:, at, :], scalar=pcol(GF, m),
                                       in1=r32(h_hi[:, at, :]), op0=ALU.mult, op1=ALU.subtract).then_inc(h2_lo, 1)

            lo(N_OUT + 2, 0)
            d.wait_ge(xt_stored, 8)
            out_tile(0, 0)
            lo(N_OUT + 3, 1)
            out_tile(1, 1)
            h2_split_lo(0)
            h2_split_lo(1)
            with d.Fori(1, KD // 2) as mm:
                for i in range(2):
                    lo(mm * 2 + (N_OUT + i + 2), i)
                    out_tile(mm * 2 + i, i)
                    h2_split_lo(mm * 2 + i)
            d.wait_ge(x1_exp, 1)
            v.tensor_tensor(ffn_t[:, 1, :], r_ffn[:, :], r_ffn[:, :], ALU.mult).then_inc(ffn_step, 1)
            d.wait_ge(ffn_step, 1)
            v.tensor_tensor(ffn_t[:, 1, :], ffn_t[:, 1, :], ffn_t[:, 0, :], ALU.mult).then_inc(ffn_step, 1)
            d.wait_ge(ffn_step, 2)
            v.tensor_scalar(ffn_t[:, 1, :], ffn_t[:, 1, :], -0.5, 1.5, ALU.mult, ALU.add).then_inc(ffn_step, 1)
            d.wait_ge(ffn_step, 3)
            v.tensor_tensor(r_ffn[:, :], r_ffn[:, :], ffn_t[:, 1, :], ALU.mult).then_inc(r_ready, 1)
            v.memset(conv_in[:, :, 0:2], 0.0).then_inc(cin_zero, 1)
            d.wait_ge(r_ready, 1)
            d.wait_ge(cin_zero, 1)

            def taps(jj, i, gv):
                j, e = jj * 2 + i, 2 * i + gv
                count = jj * 4 + (e + 1)
                d.wait_ge(tap_init, count)
                v.scalar_tensor_tensor(out=conv_out[:, e, :], in0=conv_in[:, e, 1:1 + S], scalar=pcol(CW1, j + KF * gv),
                                       in1=conv_out[:, e, :], op0=ALU.mult, op1=ALU.add).then_inc(tap1_done, 1)
                d.wait_ge(tap1_done, count)
                v.scalar_tensor_tensor(out=conv_out[:, e, :], in0=conv_in[:, e, 0:S], scalar=pcol(CW0, j + KF * gv),
                                       in1=conv_out[:, e, :], op0=ALU.mult, op1=ALU.add).then_inc(conv_done, 1)

            def up(jj):
                for i in range(2):
                    n = jj * 4 + (N_UP + 2 * i)
                    for gv in range(2):
                        e = 2 * i + gv
                        d.wait_ge(unit_done, n + gv + 1)
                        v.tensor_tensor(conv_in[:, e, 2:2 + S], ps[:, e, :], r_ffn[:, :], ALU.mult)\
                            .then_inc(cin_ready, 1)
                        lo(n + gv + 2, gv)
                        taps(jj, i, gv)

            def a_split(k, slot):
                d.wait_ge(a_hi_ready, k + 1)
                src = act_sb[:, k, :]
                v.tensor_tensor(a_lo[:, slot, :], src, r32(a_hi[:, slot, :]), ALU.subtract).then_inc(a_lo_ready, 1)

            with d.Fori(0, KF // 2 - 1) as jj:
                up(jj)
            a_split(0, 0)
            a_split(1, 1)
            up(KF // 2 - 1)

            with d.Fori(0, KF // 2 - 1) as kk:
                for i in range(2):
                    lo(kk * 2 + (N_DOWN + i + 2), i)
                    a_split(kk * 2 + (i + 2), i)
            for b8 in range(8):
                d.wait_ge(bank_done, b8 + 1)
                h = b8 % 2
                v.tensor_tensor(out_sb[:, b8, :], ps[:, b8, :], x1[:, b8 // 2, h * S:h * S + S], ALU.add)\
                    .then_inc(out_ready, 1)

        @block.tensor
        def _(pe):
            mm3 = nc.tensor.matmul

            def product(dst, l_hi, l_lo, r_hi, r_lo, start, stop, **kw):
                mm3(dst, l_hi, r_lo, start=start, stop=False, **kw)
                mm3(dst, l_lo, r_hi, start=False, stop=False, **kw)
                return mm3(dst, l_hi, r_hi, start=False, stop=stop, **kw)

            def tile_of(n, slot, bank, channels_ready=None, midway=None):
                pe.wait_ge(lo_ready, n + 1)
                for k in range(KD):
                    c = slice(k * P, k * P + P)
                    if channels_ready is not None:
                        pe.wait_ge(channels_ready, k + 1)
                    if midway is not None and k == KD // 2:
                        midway()
                    last = product(ps[:, bank, :], w_hi[:, slot, c], w_lo[:, slot, c], h_hi[:, k, :], h_lo[:, k, :],
                                   k == 0, k == KD - 1)
                last.then_inc(unit_done, 1)

            pe.wait_ge(const_ready, 1)
            pe.wait_ge(gmix_landed, 16)
            nc.tensor.transpose(ps[:, 0, 0:KD], g_row[:, :], ident[0:KD, 0:KD]).then_inc(gmix_in_psum, 1)
            pe.wait_ge(gmix_ready, 1)
            for t in range(TT):
                pe.wait_ge(xs_ready, t + 1)
                for k in range(KD):
                    last = nc.tensor.transpose(ps[:, k, t * P:t * P + P], x_scaled[:, t, k * P:k * P + P], ident[:, :])
                last.then_inc(xs_used, 1)

            tile_of(N_QK0, 0, PROJ[0], channels_ready=h_lo_ready)
            tile_of(N_QK0 + 1, 1, PROJ[1])
            pe.wait_ge(rows_landed, 11 * 16)
            for t in range(2):
                last = nc.tensor.transpose(ps[:, PAR_BANK, t * P:t * P + P], rows[:, t, :], ident[:, :])
            last.then_inc(par_in_psum, 1)

            def values(n0, banks, u):
                pe.wait_ge(lo_ready, n0 + u + 1)
                for kk in range(2):
                    k = 2 * u + kk
                    for t in range(TT):
                        c = slice(kk * WB, kk * WB + WB)
                        tk = slice(t * P, t * P + P)
                        last = product(ps[:, banks[t], :], h_hi[:, k, tk], h_lo[:, k, tk], w_hi[:, u % 2, c],
                                       w_lo[:, u % 2, c], k == 0, k == KD - 1)
                last.then_inc(unit_done, 1)

            def sumsq(t, i, bank):
                pe.wait_ge(proj_sq, t + 1)
                mm3(ps[:, bank, :], ones_heads[:, :], sq[:, i, :], start=True, stop=True).then_inc(ss_done, 1)

            values(N_VA, V_A_BANKS, 0)
            pe.wait_ge(par_ready, 1)
            sumsq(0, 0, 6)
            sumsq(1, 1, 7)
            for u in range(1, 4):
                values(N_VA, V_A_BANKS, u)
            pe.wait_ge(ms_done, 2)
            for u in range(4):
                values(N_VB, V_B_BANKS, u)

            def scores(s, attn):
                for qt, c, n in segs():
                    q = slice(qt * P, qt * P + P)
                    dst = [ps[:, HEAD[h]:HEAD[h] + 3, :].rearrange("p b c -> p (b c)")[:, c:c + n] for h in range(2)]
                    for i, (a_q, a_k) in enumerate(((qk_hi, qk_lo), (qk_lo, qk_hi), (qk_hi, qk_hi))):
                        for h in range(2):
                            r = slice(HD * h, HD * h + HD)
                            last = mm3(dst[h], a_q[r, 0, q], a_k[r, 1, 0:n], start=i == 0, stop=i == 2 and attn == "A")
                    if attn == "B":
                        for h in range(2):
                            last = mm3(dst[h][:, qt * P:n], ident_b[:, :], causal_b[:, :], start=False, stop=True)
                last.then_inc(s_done, 1)

            def transposes(s, h):
                pe.wait_ge(p_ready, s * 2 + h + 1)
                flat = ps[:, HEAD[h]:HEAD[h] + 3, :].rearrange("p b c -> p (b c)")
                for kt in range(TT):
                    for qt in range(kt, TT):
                        c = T_OFF[kt] + P * (qt - kt)
                        last = nc.tensor.transpose(flat[:, c:c + P],
                                                   pa[h][:, S_OFF[qt] + kt * P:S_OFF[qt] + kt * P + P], ident[:, :])
                last.then_inc(t_done, 1)

            def output(s, h):
                if h == 0:
                    pe.wait_ge(vp_lo_ready, s + 1)
                pe.wait_ge(pt_lo_ready, s * 2 + h + 1)
                for kt in range(TT):
                    n = S - P * kt
                    c = slice(T_OFF[kt], T_OFF[kt] + n)
                    last = product(ps[:, HEAD[h], P * kt:S], vp_hi[:, kt, :], vp_lo[:, kt, :], pt_hi[:, c], pt_lo[:, c],
                                   kt == 0, kt == TT - 1)
                last.then_inc(pv_done, 1)

            def slot(s, attn, proj):
                b = s * 4 + N_SLOT
                t = s * 2 + 2
                pe.wait_ge(qk_lo_ready, s * 2 + 2)
                if isinstance(s, int) and s == 0:
                    pe.wait_ge(v_stored, 3)
                else:
                    pe.wait_ge(o_lo_ready, s * 2)
                scores(s, attn)
                if not (isinstance(s, int) and s == 0):
                    pe.wait_ge(gate_stored, s * 2)
                tile_of(b, 0, PROJ[0])
                transposes(s, 0)
                tile_of(b + 1, 1, PROJ[1])
                output(s, 0)
                if proj == "A":
                    sumsq(t, 0, HEAD[0] + 1)
                transposes(s, 1)
                if proj == "A":
                    sumsq(t + 1, 1, HEAD[0] + 2)
                elif proj == "B":
                    pe.wait_ge(qk_lo_ready, s * 2 + 3)
                else:
                    pe.wait_ge(u_stored, 1)
                tile_of(b + 2, 0, PROJ[0])
                output(s, 1)
                if proj == "B":
                    pe.wait_ge(qk_lo_ready, s * 2 + 4)
                elif proj == "U":
                    pe.wait_ge(u_stored, 2)
                tile_of(b + 3, 1, PROJ[1])

            slot(0, "A", "A")
            with pe.Fori(1, 3) as s:
                slot(s, "A", "A")
            slot(3, "A", "B")
            with pe.Fori(4, 7) as s:
                slot(s, "B", "B")
            slot(7, "B", "U")
            b = N_SLOT + 28
            for i in range(2):
                pe.wait_ge(u_stored, 3 + i)
                tile_of(b + 4 + i, i, PROJ[i])

            def mix(g):
                pe.wait_ge(pl_lo_ready, g + 1)
                product(ps[:, MIX + g, :], wp_hi[:, g, :], wp_lo[:, g, :], pl_hi[:, g % 2, :], pl_lo[:, g % 2, :],
                        True, True).then_inc(mix_done, 1)

            def merge(mm, i, first):
                m = mm * 2 + i
                n = mm * 6 + (N_MERGE + 3 * i)
                bank = 4 * i
                sl = (i, 1 - i, i)
                pe.wait_ge(lo_ready, n + 1)
                if not first:
                    pe.wait_ge(mg_ready, m - 1)
                else:
                    pe.wait_ge(gate_stored, 2 * KD)
                for br in range(2):
                    for k in range(KB):
                        c = slice((KB * br + k) * P, (KB * br + k) * P + P)
                        last = product(ps[:, bank + br, :], w_hi[:, sl[0], c], w_lo[:, sl[0], c],
                                       o_hi[:, KB * br + k, :], o_lo[:, KB * br + k, :], k == 0, k == KB - 1)
                last.then_inc(unit_done, 1)
                if first and i == 0:
                    pe.wait_ge(wp_lo_ready, 1)
                    pe.wait_ge(o_lo_ready, 16)
                    mix(0)
                    mix(1)
                tile_of(n + 1, sl[1], bank + 2)
                if first and i == 0:
                    mix(2)
                    mix(3)
                    pe.wait_ge(oc_lo_ready, 4)
                pe.wait_ge(lo_ready, n + 3)
                for k in range(KB):
                    c = slice(k * P, k * P + P)
                    last = product(ps[:, bank + 3, :], w_hi[:, sl[2], c], w_lo[:, sl[2], c], oc_hi[:, k, :],
                                   oc_lo[:, k, :], k == 0, k == KB - 1)
                last.then_inc(unit_done, 1)

            merge(0, 0, True)
            merge(0, 1, True)
            with pe.Fori(1, KD // 2) as mm:
                merge(mm, 0, False)
                merge(mm, 1, False)

            def x_half(half_no):
                pe.wait_ge(xre_landed[half_no], 16)
                if half_no == 0:
                    pe.wait_ge(mg_ready, KD)
                else:
                    pe.wait_ge(xt_stored, 4)
                for k in range(KD):
                    for t in range(2):
                        c = (k % 2) * 256 + t * P
                        last = nc.tensor.transpose(ps[:, 4 + k // 2, c:c + P], x_re[:, t, k * P:k * P + P], ident[:, :])
                last.then_inc(xre_t_done, 1)

            def out_tile(n, slot, bank):
                pe.wait_ge(lo_ready, n + 1)
                for k in range(KD):
                    c = slice(k * P, k * P + P)
                    last = product(ps[:, bank, :], w_hi[:, slot, c], w_lo[:, slot, c], m_hi[:, k, :], m_lo[:, k, :],
                                   k == 0, k == KD - 1)
                last.then_inc(unit_done, 1)

            x_half(0)
            pe.wait_ge(m_lo_ready, KD)
            out_tile(N_OUT, 0, 0)
            x_half(1)
            out_tile(N_OUT + 1, 1, 1)
            with pe.Fori(1, KD // 2) as mm:
                for i in range(2):
                    pe.wait_ge(x1_ready, mm * 2 + (i - 1))
                    out_tile(mm * 2 + (N_OUT + i), i, i)

            def x1_back(half_no):
                for k in range(4):
                    for t in range(TT):
                        last = nc.tensor.transpose(ps[:, 4 + t, k * P:k * P + P],
                                                   x1_t[:, 4 * half_no + k, t * P:t * P + P], ident[:, :])
                last.then_inc(x1n_t_done, 1)

            def x1_sum_channels():
                pe.wait_ge(x1_ss, KD - 1)
                mm3(ps[:, 2, :], ones_all[:, :], ss_x1[:, :], start=True, stop=True).then_inc(x1_total, 1)

            x1_back(0)
            pe.wait_ge(x1_ready, KD)

            def up(jj, first):
                for i in range(2):
                    for gv in range(2):
                        e = 2 * i + gv
                        if not first:
                            pe.wait_ge(cin_ready, jj * 4 + (e - 3))
                        elif e == 2:
                            pe.wait_ge(x1_ms, 1)
                        begins = first and e == 0
                        tile_of(jj * 4 + (N_UP + e), gv, e, channels_ready=h2_lo if begins else None,
                                midway=x1_sum_channels if begins else None)

            up(0, True)
            pe.wait_ge(x1n_stored, 1)
            x1_back(1)
            with pe.Fori(1, KF // 2) as jj:
                up(jj, False)

            pe.wait_ge(x1n_stored, 2)

            def down(k, slot, start):
                pe.wait_ge(lo_ready, k + (N_DOWN + 1))
                pe.wait_ge(a_lo_ready, k + 1)
                for b8 in ((4, 5, 6, 7, 0, 1, 2, 3) if start else range(8)):
                    t, h = b8 // 2, b8 % 2
                    if start and b8 == 0:
                        pe.wait_ge(cin_ready, 2 * KF)
                    tk, c = slice(t * P, t * P + P), slice(h * S, h * S + S)
                    last = product(ps[:, b8, :], a_hi[:, slot, tk], a_lo[:, slot, tk], w_hi[:, slot, c],
                                   w_lo[:, slot, c], start, False)
                last.then_inc(unit_done, 1)

            down(0, 0, True)
            down(1, 1, False)
            with pe.Fori(1, KF // 2 - 1) as kk:
                down(kk * 2, 0, False)
                down(kk * 2 + 1, 1, False)
            down(KF - 2, 0, False)
            pe.wait_ge(lo_ready, N_END)
            pe.wait_ge(a_lo_ready, KF)
            for b8 in range(8):
                t, h = b8 // 2, b8 % 2
                tk, c = slice(t * P, t * P + P), slice(h * S, h * S + S)
                product(ps[:, b8, :], a_hi[:, 1, tk], a_lo[:, 1, tk], w_hi[:, 1, c], w_lo[:, 1, c], False, True)\
                    .then_inc(bank_done, 1)


_INS = ["x", "norm_mix", "w_in", "b_gate", "q_norm_a", "k_norm_a", "rel_bias_a", "w_pool", "pool_scale",
        "w_branch_a", "w_branch_b", "w_branch_c", "w_out", "norm_ffn", "w_up", "conv_w", "conv_b", "w_down"]


def kernel(**inputs):
    import numpy as _np
    import concourse.bacc as _bacc
    from concourse import mybir as _mybir
    from concourse.bass_utils import run_bass_kernel_spmd as _run

    nc = _bacc.Bacc("TRN2", target_bir_lowering=False, num_devices=1)
    arrays, args = {}, []
    for name in _INS:
        a = _np.ascontiguousarray(inputs[name])
        arrays[f"in_{name}_dram"] = a
        args.append(nc.dram_tensor(f"in_{name}_dram", a.shape, _mybir.dt.from_np(a.dtype), kind="ExternalInput").ap())
    args.append(nc.dram_tensor("out_0_dram", (1, S, D), _mybir.dt.float32, kind="ExternalOutput").ap())
    build(nc, *args)
    r = _run(nc, [arrays], core_ids=[0])
    return r.results[0]["out_0_dram"]
```

```python
import concourse.bass as bass
from concourse import mybir
from contextlib import ExitStack

FP32 = mybir.dt.float32
F32R = mybir.dt.float32r
ACT = mybir.ActivationFunctionType
ALU = mybir.AluOpType

P = 128
S = 512
TT = S // P
D = 1024
KD = D // P
HD = 64
WB = 512
KB = WB // P
FF = 2816
KF = FF // P
EPS = 1e-6
REL = 192
REL_ROW = 640
MASKED = -1e30
WINDOWS = (2, 4, 8, 16)
GROUPS = (3, 2, 1, 0)
UNIT = KD * P

Q_A, K_A, V_A, Q_B, K_B, V_B, U_C, GATE = 0, 4, 8, 12, 16, 20, 24, 28

N_QK0 = 0
N_VA = 2
N_VB = 6
N_SLOT = 10
N_MERGE = N_SLOT + 4 * 8 + 2
N_OUT = N_MERGE + 3 * KD
N_UP = N_OUT + KD
N_DOWN = N_UP + 2 * KF
N_END = N_DOWN + KF

S_OFF = (896, 1024, 512, 0)
T_OFF = (0, 512, 1024, 896)
SCORES = 1280

PROJ = (0, 1)
HEAD = (5, 2)
V_A_BANKS = (2, 3, 4, 5)
V_B_BANKS = (6, 7, 0, 1)
PAR_BANK = 6
MIX = 4


def build(nc, x, norm_mix, w_in, b_gate, q_norm_a, k_norm_a, rel_bias_a, w_pool, pool_scale,
          w_branch_a, w_branch_b, w_branch_c, w_out, norm_ffn, w_up, conv_w, conv_b, w_down, out):
    ctx = ExitStack()
    with ctx:
        def sb(name, shape, dt=FP32):
            return ctx.enter_context(nc.sbuf_tensor(name, shape, dt))

        def sem(name):
            return ctx.enter_context(nc.semaphore(name))

        def region(kb, *specs):
            with ExitStack() as scope:
                if kb:
                    scope.enter_context(nc.sbuf_tensor(f"below_{specs[0][0]}", [P, 256 * kb], FP32))
                return [scope.enter_context(nc.sbuf_tensor(n, s, d)) for n, s, d in specs]

        w_raw = sb("w_raw", [P, 2, UNIT])
        w_hi = sb("w_hi", [P, 2, UNIT], F32R)
        w_lo = sb("w_lo", [P, 2, UNIT], F32R)
        h_hi = sb("h_hi", [P, KD, S], F32R)
        h_lo = sb("h_lo", [P, KD, S], F32R)
        ident = sb("ident", [P, P])
        ones_heads = sb("ones_heads", [P, P])
        ones_all = sb("ones_all", [P, P])
        g_row = sb("g_row", [KD, P])
        g_mix = sb("g_mix", [P, KD])
        rows = sb("rows", [P, 2, P])
        par = sb("par", [P, 2, P])
        eps = sb("eps", [P, 1])
        tok = sb("tok", [P, 6, TT])
        hstat = sb("hstat", [P, 2, 3, TT])
        qk_gain = sb("qk_gain", [P, 2])
        masked = sb("masked", [P, 2, HD])
        ident_b = sb("ident_b", [P, P], mybir.dt.bfloat16)
        causal_b = sb("causal_b", [P, P], mybir.dt.bfloat16)
        inv = sb("inv", [P, 3, 16])
        CW0, CW1, BG, GF = (0, 0), (0, 44), (0, 88), (0, 120)
        CW2, CB, PSC, GQ, GK = (1, 0), (1, 44), (1, 88), (1, 92), (1, 93)

        def pcol(where, i):
            t, c = where
            return par[:, t, c + i:c + i + 1] if isinstance(i, int) else par[:, t, bass.ds(i + c, 1)]

        x_scaled, squares = region(0, ("x_scaled", [P, TT, D], FP32), ("squares", [P, TT, D], FP32))
        x_in, = region(64, ("x_in", [P, TT, D], FP32))
        frow, = region(32, ("frow", [8, 2, REL_ROW], FP32))
        o_hi, o_lo, gates = region(0, ("o_hi", [P, 2 * KB, S], F32R), ("o_lo", [P, 2 * KB, S], F32R),
                                   ("gates", [P, 2 * KD, S], FP32))
        (v_a, v_b, bias_rev, pa1, qk_hi, qk_lo, pt_hi, pt_lo, v_st, pa0, qk_raw, sq, rn, nt, o_sum) = region(
            64, ("v_a", [P, TT, WB], FP32), ("v_b", [P, TT, WB], FP32), ("bias_rev", [P, 2, S], FP32),
            ("pa1", [P, 3 * P * 8], FP32),
            ("qk_hi", [P, 2, S], F32R), ("qk_lo", [P, 2, S], F32R),
            ("pt_hi", [P, SCORES], F32R), ("pt_lo", [P, SCORES], F32R),
            ("v_st", [P, 2, TT, P], F32R),
            ("pa0", [P, SCORES], FP32),
            ("qk_raw", [P, 2, S], FP32), ("sq", [P, 2, S], FP32), ("rn", [P, 2, S], FP32), ("nt", [P, 2, S], FP32),
            ("o_sum", [P, S], FP32))
        pa = (pa0, pa1)
        keep0, keep1, suffix = region(64 + 59, ("keep0", [P, SCORES], FP32), ("keep1", [P, SCORES], FP32),
                                    ("suffix", [P, SCORES + TT], FP32))
        keep = (keep0, keep1)
        u_pad, = region(64, ("u_pad", [P, 4, 16 + S], FP32))
        win, = region(73, ("win", [P, 2, 16 + S], FP32))
        pl_hi, = region(80, ("pl_hi", [P, 2, S], F32R))
        wp_hi, wp_lo, wp_raw = region(89, ("wp_hi", [P, 4, P], F32R), ("wp_lo", [P, 4, P], F32R),
                                      ("wp_raw", [P, 4, P], FP32))
        pl_lo, pl = region(96, ("pl_lo", [P, 2, S], F32R), ("pl", [P, S], FP32))
        m_hi, m_lo, oc_hi, oc_lo, x_re, mg = region(
            80, ("m_hi", [P, KD, S], F32R), ("m_lo", [P, KD, S], F32R),
            ("oc_hi", [P, KB, S], F32R), ("oc_lo", [P, KB, S], F32R),
            ("x_re", [P, 2, D], FP32), ("mg", [P, 4, S], FP32))
        x_t, x1_t, act_sb = region(0, ("x_t", [P, KD, S], FP32), ("x1_t", [P, KD, S], FP32),
                                ("act", [P, KF, S], FP32))
        x1, conv_in, conv_out, sg, r_ffn, ffn_t = region(
            76, ("x1", [P, TT, D], FP32), ("conv_in", [P, 4, 2 + S], FP32), ("conv_out", [P, 4, S], FP32),
            ("sg", [P, 2, S], FP32), ("r_ffn", [P, S], FP32), ("ffn_t", [P, 2, S], FP32))
        sq_x1, ss_x1 = region(132, ("sq_x1", [P, 2, S], FP32), ("ss_x1", [P, S], FP32))
        a_hi, a_lo = region(124, ("a_hi", [P, 2, S], F32R), ("a_lo", [P, 2, S], F32R))
        out_sb, = region(92, ("out_sb", [P, 8, S], FP32))

        ps = ctx.enter_context(nc.psum_tensor("ps", [P, 8, S], FP32))
        frow_dram = nc.dram_tensor("rel_bias_rows", (8, REL_ROW), FP32, kind="Internal").ap()

        x_landed = [sem(f"x_landed{t}") for t in range(TT)]
        gmix_landed, gmix_in_psum, gmix_ready = sem("gmix_landed"), sem("gmix_in_psum"), sem("gmix_ready")
        rows_landed, rel_landed, bias_landed, frow_stored = (sem("rows_landed"), sem("rel_landed"),
                                                             sem("bias_landed"), sem("frow_stored"))
        wp_landed = sem("wp_landed")
        xre_landed = [sem("xre_landed0"), sem("xre_landed1")]
        w_landed = [sem("w_landed0"), sem("w_landed1")]
        hi_ready, lo_ready, unit_done = sem("hi_ready"), sem("lo_ready"), sem("unit_done")
        const_step, const_ready, rows_zero = sem("const_step"), sem("const_ready"), sem("rows_zero")
        par_in_psum, par_ready = sem("par_in_psum"), sem("par_ready")
        ssq_done, ln_done, exp0_done, tok_step, rstd_ready = (sem("ssq_done"), sem("ln_done"), sem("exp0_done"),
                                                              sem("tok_step"), sem("rstd_ready"))
        xs_ready, xs_used, h_hi_ready, h_lo_ready = sem("xs_ready"), sem("xs_used"), sem("h_hi_ready"), sem("h_lo_ready")
        frow_ready, bias_ready = sem("frow_ready"), sem("bias_ready")
        v_b_half = sem("v_b_half")
        v_stored, v_b_stored = sem("v_stored"), sem("v_b_stored")
        proj_raw, proj_sq = sem("proj_raw"), sem("proj_sq")
        ss_done, ms_done, lnq_done, expq_done, newton_step, rn_ready = (
            sem("ss_done"), sem("ms_done"), sem("lnq_done"), sem("expq_done"), sem("newton_step"), sem("rn_ready"))
        newton_q = sem("newton_q")
        heads_step = sem("heads_step")
        refined, gain_ready = sem("refined"), sem("gain_ready")
        hat_ready, qk_hi_ready, qk_lo_ready = sem("hat_ready"), sem("qk_hi_ready"), sem("qk_lo_ready")
        s_done, negmax_ready, exp_done, recip_done, p_ready = (
            sem("s_done"), sem("negmax_ready"), sem("exp_done"), sem("recip_done"), sem("p_ready"))
        keep_done, beta_done, scan_done = sem("keep_done"), sem("beta_done"), sem("scan_done")
        suffix_init = sem("suffix_init")
        t_done, pt_hi_ready, pt_lo_ready = sem("t_done"), sem("pt_hi_ready"), sem("pt_lo_ready")
        v_hi_ready, v_lo_ready = sem("v_hi_ready"), sem("v_lo_ready")
        pv_done, o_part_ready, o_sum_ready, o_hi_ready, o_lo_ready = (sem("pv_done"), sem("o_part_ready"), sem("o_sum_ready"), sem("o_hi_ready"),
                                                        sem("o_lo_ready"))
        gate_stored = sem("gate_stored")
        u_init, u_stored, win_step, pl_step, pl_ready = (sem("u_init"), sem("u_stored"), sem("win_step"),
                                                         sem("pl_step"), sem("pl_ready"))
        inv_step = sem("inv_step")
        win_ready = sem("win_ready")
        pl_hi_ready, pl_lo_ready, wp_hi_ready, wp_lo_ready = (sem("pl_hi_ready"), sem("pl_lo_ready"),
                                                              sem("wp_hi_ready"), sem("wp_lo_ready"))
        mix_done, oc_hi_ready, oc_lo_ready = sem("mix_done"), sem("oc_hi_ready"), sem("oc_lo_ready")
        sig_ab, sig_c, mg_step, mg_ready = sem("sig_ab"), sem("sig_c"), sem("mg_step"), sem("mg_ready")
        m_hi_ready, m_lo_ready = sem("m_hi_ready"), sem("m_lo_ready")
        xre_t_done, xt_stored = sem("xre_t_done"), sem("xt_stored")
        x1_total = sem("x1_total")
        x1_ready, x1_sq, x1_ss, h2_hi, h2_lo = (sem("x1_ready"), sem("x1_sq"), sem("x1_ss"), sem("h2_hi"), sem("h2_lo"))
        x1_ln, x1_exp, x1_ms, ffn_step, r_ready = (sem("x1_ln"), sem("x1_exp"), sem("x1_ms"), sem("ffn_step"), sem("r_ready"))
        x1n_t_done, x1n_stored = sem("x1n_t_done"), sem("x1n_stored")
        cin_zero, cin_ready, tap_init, tap1_done, conv_done = (sem("cin_zero"), sem("cin_ready"), sem("tap_init"),
                                                    sem("tap1_done"), sem("conv_done"))
        sg_ready, silu_ready, act_ready = sem("sg_ready"), sem("silu_ready"), sem("act_ready")
        a_hi_ready, a_lo_ready = sem("a_hi_ready"), sem("a_lo_ready")
        bank_done, out_ready, out_stored = sem("bank_done"), sem("out_ready"), sem("out_stored")

        block = ctx.enter_context(nc.Block())

        def r32(ap):
            return ap.bitcast(FP32)

        def own(h):
            return slice(HD * h, HD * h + HD)

        def segs():
            return [(qt, S_OFF[qt], P * (qt + 1)) for qt in (3, 2, 1, 0)]

        def seg2(qt):
            return S_OFF[qt] + (0, 1, 2, 3)[(3, 2, 0, 1).index(qt)]

        xw = x[0].rearrange("(t p) d -> p t d", p=P)
        win_v = w_in[0].rearrange("(k p) (j c) -> p k j c", p=P, c=P)
        win_c = w_in[0].rearrange("(k p) c -> p k c", p=P)
        wa_v, wb_v, wc_v = (w[0].rearrange("(k p) (j c) -> p k j c", p=P, c=P)
                            for w in (w_branch_a, w_branch_b, w_branch_c))
        wo_v = w_out[0].rearrange("(k p) (j c) -> p k j c", p=P, c=P)
        wu_v = w_up[0].rearrange("(k p) (j c) -> p k j c", p=P, c=P)
        wd_v = w_down[0].rearrange("(k p) (h c) -> p k h c", p=P, h=2)
        out_v = out[0].rearrange("(t p) (h d) -> p t h d", p=P, h=2)

        @block.sync
        def _(sp):
            for t in range(TT):
                sp.dma_start(x_in[:, t, :], xw[:, t, :]).then_inc(x_landed[t], 16)
                if t == 0:
                    sp.dma_start(g_row[:, :], norm_mix[0].rearrange("(k c) -> k c", c=P)).then_inc(gmix_landed, 16)

            def load(n, slot, halves):
                if not (isinstance(n, int) and n < 2):
                    sp.wait_ge(lo_ready, n - 1)
                for i, src in enumerate(halves):
                    k, c = src.shape[1], src.shape[-1]
                    dst = w_raw[:, slot, i * k * c:(i + 1) * k * c].rearrange("p (k c) -> p k c", k=k)
                    sp.dma_start(dst, src).then_inc(w_landed[slot], 16)

            def cols(n, slot, view, j):
                load(n, slot, [view[:, 0:4, j, :], view[:, 4:8, j, :]])

            def values(n0, c0):
                for u in range(4):
                    load(n0 + u, u % 2, [win_c[:, 2 * u + i:2 * u + i + 1, c0:c0 + WB] for i in range(2)])

            cols(N_QK0, 0, win_v, Q_A)
            cols(N_QK0 + 1, 1, win_v, K_A)
            sp.wait_ge(rows_zero, 1)
            for src, (t, c), n in ((conv_w[0, 0], CW0, 44), (conv_w[0, 1], CW1, 44), (b_gate[0], BG, 24),
                                   (norm_ffn[0], GF, 8), (conv_w[0, 2], CW2, 44),
                                   (conv_b[0], CB, 44), (pool_scale[0], PSC, 4)):
                sp.dma_start(rows[c:c + n, t, :], src.rearrange("(r c) -> r c", c=P)).then_inc(rows_landed, 16)
            for src, (t, c) in ((q_norm_a, GQ), (k_norm_a, GK)):
                for i in range(2):
                    sp.dma_start(rows[c:c + 1, t, i * HD:(i + 1) * HD], src[:, :]).then_inc(rows_landed, 16)
            sp.dma_start(frow[:, 1, 0:REL], rel_bias_a[0]).then_inc(rel_landed, 16)
            values(N_VA, V_A * P)
            values(N_VB, V_B * P)

            def slot(s, qj, kj):
                b = N_SLOT + 4 * s
                cols(b, 0, win_v, qj)
                cols(b + 1, 1, win_v, kj)
                cols(b + 2, 0, win_v, GATE + 2 * s)
                cols(b + 3, 1, win_v, GATE + 2 * s + 1)

            slot(0, Q_A + 1, K_A + 1)
            with sp.Fori(1, 3) as s:
                slot(s, s + (Q_A + 1), s + (K_A + 1))
            slot(3, Q_B, K_B)
            with sp.Fori(4, 7) as s:
                slot(s, s + (Q_B - 3), s + (K_B - 3))
            b = N_SLOT + 28
            for i, g in enumerate(GROUPS):
                cols(b + i, i % 2, win_v, U_C + g)
            sp.wait_ge(negmax_ready, 8 * TT)
            sp.dma_start(wp_raw[:, :, :], w_pool[0].rearrange("g c e -> c g e")).then_inc(wp_landed, 16)
            for i in range(2):
                cols(b + 4 + i, i, win_v, GATE + 14 + i)
            sp.wait_ge(p_ready, 16)
            sp.dma_start(x_re[:, :, :], xw[:, 0:2, :]).then_inc(xre_landed[0], 16)
            with sp.Fori(0, KD // 2) as mm:
                for i in range(2):
                    m = mm * 2 + i
                    n = mm * 6 + (N_MERGE + 3 * i)
                    load(n, i, [wa_v[:, :, m, :], wb_v[:, :, m, :]])
                    cols(n + 1, 1 - i, win_v, m + (GATE + 2 * KD))
                    load(n + 2, i, [wc_v[:, 0:2, m, :], wc_v[:, 2:4, m, :]])
            for m in range(4):
                cols(N_OUT + m, m % 2, wo_v, m)
            sp.wait_ge(xre_t_done, 1)
            sp.dma_start(x_re[:, :, :], xw[:, 2:4, :]).then_inc(xre_landed[1], 16)
            with sp.Fori(2, KD // 2) as mm:
                for i in range(2):
                    cols(mm * 2 + (N_OUT + i), i, wo_v, mm * 2 + i)
            with sp.Fori(0, KF) as j:
                cols(j * 2 + N_UP, 0, wu_v, j)
                cols(j * 2 + (N_UP + 1), 1, wu_v, j + KF)
            with sp.Fori(0, KF // 2) as kk:
                for i in range(2):
                    load(kk * 2 + (N_DOWN + i), i, [wd_v[:, bass.ds(kk * 2 + i, 1), h, :] for h in range(2)])
            for b8 in range(8):
                sp.wait_ge(out_ready, b8 + 1)
                sp.dma_start(out_v[:, b8 // 2, b8 % 2, :], out_sb[:, b8, :]).then_inc(out_stored, 16)
            sp.wait_ge(out_stored, 8 * 16)

        @block.gpsimd
        def _(pool):
            pool.memset(rows[:, :, :], 0.0).then_inc(rows_zero, 1)
            pool.memset(ident[:, :], 0.0).then_inc(const_step, 1)
            pool.memset(ones_all[:, :], 1.0)
            pool.memset(eps[:, :], EPS)
            pool.memset(masked[:, 0, :], MASKED)
            pool.memset(masked[:, 1, :], 0.0)
            pool.memset(ident_b[:, :], 0.0)
            pool.memset(causal_b[:, :], 0.0).then_inc(const_step, 1)
            pool.wait_ge(const_step, 2)
            pool.affine_select(out=ident_b[:, :], in_=ident_b[:, :], compare_op=ALU.not_equal, fill=1.0, base=0,
                               pattern=[[-1, P]], channel_multiplier=1)
            pool.affine_select(out=causal_b[:, :], in_=causal_b[:, :], compare_op=ALU.is_gt, fill=MASKED, base=0,
                               pattern=[[-1, P]], channel_multiplier=1)
            pool.affine_select(out=ident[:, :], in_=ident[:, :], compare_op=ALU.not_equal, fill=1.0, base=0,
                               pattern=[[-1, P]], channel_multiplier=1).then_inc(const_ready, 1)
            pool.wait_ge(hi_ready, N_QK0 + 2)
            pool.wait_ge(lo_ready, N_QK0 + 1)
            pool.tensor_tensor(w_lo[:, 1, :], w_raw[:, 1, :], r32(w_hi[:, 1, :]), ALU.subtract).then_inc(lo_ready, 1)
            pool.wait_ge(frow_ready, 3)
            pool.dma_start(frow_dram[:, :], frow[:, 0, :]).then_inc(frow_stored, 16)
            pool.wait_ge(frow_stored, 16)
            windows = bass.AP(frow_dram.tensor, 0, [[REL_ROW, 8], [1, P], [1, S]])

            def bias_load(hh, h):
                if not (isinstance(hh, int) and hh < 2):
                    pool.wait_ge(negmax_ready, hh * 4 - 4)
                pool.dma_start(bias_rev[:, h, :], windows[hh, :, :]).then_inc(bias_landed, 16)
                pool.wait_ge(bias_landed, hh * 16 + 16)
                pool.tensor_tensor(bias_rev[0:HD, h, 0:HD], masked[0:HD, 0, :], masked[0:HD, 1, :], ALU.add)\
                    .then_inc(bias_ready, 1)

            bias_load(0, 0)
            bias_load(1, 1)

            def newton_k(pair):
                pool.wait_ge(expq_done, pair * 2 + 2)
                pool.tensor_tensor(nt[:, 1, :], rn[:, 1, :], rn[:, 1, :], ALU.mult).then_inc(newton_step, 1)
                pool.wait_ge(newton_step, pair + 1)
                pool.tensor_tensor(nt[:, 1, :], nt[:, 1, :], sq[:, 1, :], ALU.mult).then_inc(rn_ready, 1)

            def o_split_lo(s, h):
                pool.wait_ge(o_hi_ready, s * 2 + h + 1)
                pool.tensor_tensor(o_lo[own(h), s, :], o_sum[own(h), :], r32(o_hi[own(h), s, :]), ALU.subtract)\
                    .then_inc(o_lo_ready, 1)
                pool.wait_ge(o_lo_ready, s * 2 + h + 1)

            newton_k(0)
            with pool.Fori(0, 3) as s:
                bias_load(s * 2 + 2, 0)
                bias_load(s * 2 + 3, 1)
                newton_k(s + 1)
                pool.wait_ge(rn_ready, s + 2)
                o_split_lo(s, 0)
                o_split_lo(s, 1)
            with pool.Fori(3, 7) as s:
                o_split_lo(s, 0)
                o_split_lo(s, 1)

            step = 0
            for i, g in enumerate(GROUPS):
                w = WINDOWS[g]
                pool.wait_ge(u_stored, i + 1)
                src, width, n = u_pad[:, g, :], 1, 0
                if i >= 1:
                    pool.wait_ge(pl_ready, i)
                while width < w:
                    lo = 2 * width - 1
                    dst = win[:, n % 2, :]
                    ins = pool.tensor_tensor(dst[:, lo:16 + S], src[:, lo:16 + S],
                                             src[:, lo - width:16 + S - width], ALU.add)
                    src, width, n = dst, 2 * width, n + 1
                    if width < w:
                        step += 1
                        ins.then_inc(win_step, 1)
                        pool.wait_ge(win_step, step)
                ins.then_inc(win_ready, 1)
                if i < 2:
                    pool.wait_ge(win_ready, i + 1)
                    o_split_lo(7, i)

            def x1_sum(m, i):
                pool.wait_ge(x1_sq, m + 1)
                pool.tensor_tensor(ss_x1[:, :], sq_x1[:, (i + 1) % 2, :] if isinstance(m, int) and m == 1
                                   else ss_x1[:, :], sq_x1[:, i, :], ALU.add).then_inc(x1_ss, 1)

            x1_sum(1, 1)
            for m in range(2, 4):
                pool.wait_ge(x1_ss, m - 1)
                x1_sum(m, m % 2)
            with pool.Fori(2, KD // 2) as mm:
                for i in range(2):
                    pool.wait_ge(x1_ss, mm * 2 + (i - 1))
                    x1_sum(mm * 2 + i, i)

            with pool.Fori(0, KF // 2) as jj:
                for i in range(2):
                    j = jj * 2 + i
                    pool.wait_ge(sg_ready, j + 1)
                    pool.tensor_tensor(sg[:, i, :], sg[:, i, :], conv_out[:, 2 * i, :], ALU.mult).then_inc(silu_ready, 1)
                    pool.wait_ge(silu_ready, j + 1)
                    pool.wait_ge(conv_done, j * 2 + 2)
                    pool.tensor_tensor(act_sb[:, j, :],
                                       sg[:, i, :], conv_out[:, 2 * i + 1, :], ALU.mult).then_inc(act_ready, 1)

        @block.scalar
        def _(act_e):
            a = act_e
            act = nc.scalar.activation
            def hi(n, slot):
                a.wait_ge(w_landed[slot], ((n // 2 + 1) * 32) if isinstance(n, int) else 0)
                if not (isinstance(n, int) and n < 2):
                    a.wait_ge(unit_done, n - 1)
                act(w_hi[:, slot, :], w_raw[:, slot, :], ACT.Copy).then_inc(hi_ready, 1)

            def hi_at(n, slot, half):
                a.wait_ge(w_landed[slot], half * 32 + 32)
                a.wait_ge(unit_done, n - 1)
                act(w_hi[:, slot, :], w_raw[:, slot, :], ACT.Copy).then_inc(hi_ready, 1)

            a.preload_act_table_set("natural_log_exp_and_others")
            a.wait_ge(const_ready, 1)
            for t in range(TT):
                a.wait_ge(x_landed[t], 16)
                act(squares[:, t, :], x_in[:, t, :], ACT.Square, accum_out=tok[:, 0, t:t + 1]).then_inc(ssq_done, 1)
                a.wait_ge(ssq_done, t + 1)
                act(tok[:, 2, t:t + 1], tok[:, 0, t:t + 1], ACT.Ln, scale=1.0 / D, bias=eps[:, :]).then_inc(ln_done, 1)
                a.wait_ge(ln_done, t + 1)
                act(tok[:, 3, t:t + 1], tok[:, 2, t:t + 1], ACT.Exp, scale=-0.5).then_inc(exp0_done, 1)
            hi(0, 0)
            hi(1, 1)
            a.wait_ge(gmix_ready, 1)
            for k in range(KD):
                a.wait_ge(xs_used, k + 1)
                act(h_hi[:, k, :], ps[:, k, :], ACT.Copy, scale=g_mix[:, k:k + 1]).then_inc(h_hi_ready, 1)

            def after(n):
                hi(n + 2, n % 2)

            def proj_a(t, i, bank, used, prev):
                a.wait_ge(unit_done, used)
                if prev:
                    a.wait_ge(qk_lo_ready, t - 1)
                act(qk_raw[:, i, :], ps[:, bank, :], ACT.Copy).then_inc(proj_raw, 1)
                act(sq[:, i, :], ps[:, bank, :], ACT.Square).then_inc(proj_sq, 1)

            def norms_a(t, bank):
                for i in range(2):
                    a.wait_ge(ss_done, t + (i + 1))
                    act(sq[:, i, :], ps[:, bank + i, :], ACT.Identity, scale=1.0 / HD, bias=eps[:, :])\
                        .then_inc(ms_done, 1)
                for i in range(2):
                    a.wait_ge(ms_done, t + (i + 1))
                    act(rn[:, i, :], sq[:, i, :], ACT.Ln).then_inc(lnq_done, 1)
                for i in range(2):
                    a.wait_ge(lnq_done, t + (i + 1))
                    act(rn[:, i, :], rn[:, i, :], ACT.Exp, scale=-0.5).then_inc(expq_done, 1)

            def hat_hi(t, i):
                a.wait_ge(hat_ready, t + 1)
                act(qk_hi[:, i, :], qk_raw[:, i, :], ACT.Copy).then_inc(qk_hi_ready, 1)

            proj_a(0, 0, 0, N_QK0 + 1, False)
            after(N_QK0)
            proj_a(1, 1, 1, N_QK0 + 2, False)
            after(N_QK0 + 1)
            after(N_VA)
            norms_a(0, 6)
            after(N_VA + 1)
            hat_hi(0, 0)
            hat_hi(1, 1)
            after(N_VA + 2)
            after(N_VA + 3)
            act(v_a[:, :, :], ps[:, V_A_BANKS[0]:V_A_BANKS[0] + 4, :], ACT.Copy).then_inc(v_stored, 1)
            for u in range(3):
                after(N_VB + u)
            a.wait_ge(unit_done, N_VB + 4)
            act(v_b[:, 2:4, :], ps[:, V_B_BANKS[2]:V_B_BANKS[2] + 2, :], ACT.Copy).then_inc(v_stored, 1)
            after(N_VB + 3)
            a.wait_ge(par_ready, 1)
            a.wait_ge(v_stored, 2)

            def attn_probs(s, h, branch):
                hh = s * 2 + h
                if branch == "A":
                    for i, (qt, c, n) in enumerate(segs()):
                        a.wait_ge(negmax_ready, hh * 4 + (i + 1))
                        act(pa[h][:, c:c + n], pa[h][:, c:c + n], ACT.Exp, scale=-1.0, bias=hstat[:, h, 0, qt:qt + 1],
                            accum_out=hstat[:, h, 1, qt:qt + 1]).then_inc(exp_done, 1)
                else:
                    a.wait_ge(s_done, s + 1)
                    a.wait_ge(t_done, hh - 1)
                    flat = ps[:, HEAD[h]:HEAD[h] + 3, :].rearrange("p b c -> p (b c)")[:, 0:SCORES]
                    act(keep[h][:, :], flat, ACT.Sigmoid, scale=-0.125).then_inc(keep_done, 1)
                    act(pa[h][:, 0:SCORES], flat, ACT.Sigmoid, scale=0.125).then_inc(beta_done, 1)

            def v_split_hi(s, v, pair, first):
                if not first:
                    a.wait_ge(pv_done, s * 2)
                for h in range(2):
                    last = act(v_st[:, h, :, own(h)], v[:, :, bass.ds(pair * P + h * HD, HD)], ACT.Copy)
                last.then_inc(v_hi_ready, 1)

            def pt_split_hi(s, h, first):
                a.wait_ge(t_done, s * 2 + h + 1)
                if not first:
                    a.wait_ge(pv_done, s * 2 + h)
                flat = ps[:, HEAD[h]:HEAD[h] + 3, :].rearrange("p b c -> p (b c)")[:, 0:SCORES]
                act(pt_hi[:, :], flat, ACT.Copy).then_inc(pt_hi_ready, 1)

            def o_part(s, h):
                a.wait_ge(pv_done, s * 2 + h + 1)
                if not (isinstance(s, int) and s + h == 0):
                    a.wait_ge(o_lo_ready, s * 2 + h)
                act(o_sum[own(1 - h), :], ps[own(1 - h), HEAD[h], :], ACT.Copy).then_inc(o_part_ready, 1)

            def o_split_hi(s, h):
                a.wait_ge(o_sum_ready, s * 2 + h + 1)
                act(o_hi[own(h), s, :], o_sum[own(h), :], ACT.Copy).then_inc(o_hi_ready, 1)

            def gate_store(g, bank, used):
                a.wait_ge(unit_done, used)
                act(gates[:, g, :], ps[:, bank, :], ACT.Identity, bias=pcol(BG, g)).then_inc(gate_stored, 1)

            def slot(s, attn, proj):
                b = s * 4 + N_SLOT
                half = s * 2 + N_SLOT // 2
                first = isinstance(s, int) and s == 0
                if attn == "A":
                    v_split_hi(s, v_a, s, first)
                    attn_probs(s, 0, attn)
                    attn_probs(s, 1, attn)
                else:
                    attn_probs(s, 0, attn)
                    attn_probs(s, 1, attn)
                    v_split_hi(s, v_b, s - 4, False)
                t = s * 2 + 2
                if attn == "A":
                    pt_split_hi(s, 0, first)
                if proj == "A":
                    proj_a(t, 0, PROJ[0], b + 1, True)
                elif proj == "B":
                    a.wait_ge(unit_done, b + 1)
                    act(qk_hi[:, 0, :], ps[:, PROJ[0], :], ACT.Copy).then_inc(qk_hi_ready, 1)
                if attn == "B":
                    pt_split_hi(s, 0, first)
                hi_at(b + 2, 0, half + 1)
                if proj == "A":
                    proj_a(t + 1, 1, PROJ[1], b + 2, True)
                    norms_a(t, HEAD[0] + 1)
                elif proj == "B":
                    a.wait_ge(unit_done, b + 2)
                    act(qk_hi[:, 1, :], ps[:, PROJ[1], :], ACT.Copy).then_inc(qk_hi_ready, 1)
                pt_split_hi(s, 1, False)
                hi_at(b + 3, 1, half + 1)
                o_part(s, 0)
                hi_at(b + 4, 0, half + 2)
                gate_store(s * 2, PROJ[0], b + 3)
                if proj == "A":
                    hat_hi(t, 0)
                o_split_hi(s, 0)
                if proj == "A":
                    hat_hi(t + 1, 1)
                o_part(s, 1)
                o_split_hi(s, 1)
                hi_at(b + 5, 1, half + 2)
                gate_store(s * 2 + 1, PROJ[1], b + 4)

            slot(0, "A", "A")
            a.preload_act_table_set("natural_log_exp_and_others")
            with a.Fori(1, 3) as s:
                slot(s, "A", "A")
            slot(3, "A", "B")
            a.preload_act_table(ACT.Sigmoid)
            with a.Fori(4, 7) as s:
                slot(s, "B", "B")

            s, b = 7, N_SLOT + 28
            half = b // 2
            attn_probs(s, 0, "B")
            attn_probs(s, 1, "B")
            v_split_hi(s, v_b, 3, False)

            def u_store(i, bank):
                a.wait_ge(unit_done, b + i + 1)
                if i == 0:
                    a.wait_ge(u_init, 1)
                act(u_pad[:, GROUPS[i], 16:16 + S], ps[:, bank, :], ACT.Copy).then_inc(u_stored, 1)

            u_store(0, PROJ[0])
            pt_split_hi(s, 0, False)
            hi_at(b + 2, 0, half + 1)
            u_store(1, PROJ[1])
            pt_split_hi(s, 1, False)
            hi_at(b + 3, 1, half + 1)
            a.wait_ge(wp_landed, 16)
            act(wp_hi[:, :, :], wp_raw[:, :, :], ACT.Copy).then_inc(wp_hi_ready, 1)

            def pl_hi_split(i):
                a.wait_ge(pl_ready, i + 1)
                if i >= 2:
                    a.wait_ge(mix_done, i - 1)
                act(pl_hi[:, i % 2, :], pl[:, :], ACT.Copy).then_inc(pl_hi_ready, 1)

            def oc_split_hi(i):
                a.wait_ge(mix_done, i + 1)
                g = GROUPS[i]
                act(oc_hi[:, g, :], ps[:, MIX + i, :], ACT.Copy, scale=pcol(PSC, g)).then_inc(oc_hi_ready, 1)

            o_part(s, 0)
            o_split_hi(s, 0)
            pl_hi_split(0)
            hi_at(b + 4, 0, half + 2)
            u_store(2, PROJ[0])
            o_part(s, 1)
            o_split_hi(s, 1)
            pl_hi_split(1)
            hi_at(b + 5, 1, half + 2)
            u_store(3, PROJ[1])
            pl_hi_split(2)
            pl_hi_split(3)
            hi(b + 6, 0)
            gate_store(14, PROJ[0], b + 5)
            for i in range(3):
                oc_split_hi(i)
            hi(b + 7, 1)
            gate_store(15, PROJ[1], b + 6)
            oc_split_hi(3)

            a.wait_ge(gate_stored, 2 * KD)

            with a.Fori(0, KD // 2) as mm:
                for i in range(2):
                    m = mm * 2 + i
                    n = mm * 6 + (N_MERGE + 3 * i)
                    h3 = mm * 3
                    for br in range(2):
                        g = gates[:, m + KD * br, :]
                        last = act(g, g, ACT.Sigmoid)
                    last.then_inc(sig_ab, 1)
                    hi_at(n + 2, i, h3 + ((N_MERGE + 3 * i + 2) // 2))
                    hi_at(n + 3, 1 - i, h3 + ((N_MERGE + 3 * i + 3) // 2))
                    a.wait_ge(unit_done, n + 2)
                    act(mg[:, 3, :], ps[:, 4 * i + 2, :], ACT.Sigmoid, bias=pcol(BG, m + 2 * KD)).then_inc(sig_c, 1)
                    hi_at(n + 4, i, h3 + ((N_MERGE + 3 * i + 4) // 2))
                    a.wait_ge(mg_ready, m + 1)
                    act(m_hi[:, m, :], mg[:, 0, :], ACT.Copy).then_inc(m_hi_ready, 1)

            a.preload_act_table_set("natural_log_exp_and_others")

            def xt_store(half_no):
                a.wait_ge(xre_t_done, half_no + 1)
                for i in range(4):
                    src = ps[:, 4 + i, :].rearrange("p (k t) -> p k t", k=2)
                    act(x_t[:, 2 * i:2 * i + 2, half_no * 256:half_no * 256 + 256], src, ACT.Copy)\
                        .then_inc(xt_stored, 1)

            def out_tile(m, i):
                a.wait_ge(x1_ready, m + 1)
                x1m = x1_t[:, m, :]
                if not (isinstance(m, int) and m < 2):
                    a.wait_ge(x1_ss, m - 1)
                act(sq_x1[:, i, :], x1m, ACT.Square).then_inc(x1_sq, 1)
                hm = h_hi[:, m, :]
                act(hm, x1m, ACT.Copy, scale=pcol(GF, m)).then_inc(h2_hi, 1)

            hi(N_OUT + 2, 0)
            xt_store(0)
            hi(N_OUT + 3, 1)
            xt_store(1)
            out_tile(0, 0)
            out_tile(1, 1)
            with a.Fori(1, KD // 2) as mm:
                for i in range(2):
                    n = mm * 2 + (N_OUT + i)
                    hi_at(n + 2, i, mm + (N_OUT // 2 + 1))
                    out_tile(mm * 2 + i, i)
            a.wait_ge(x1_total, 1)
            act(ffn_t[:, 0, :], ps[:, 2, :], ACT.Identity, scale=1.0 / D, bias=eps[:, :]).then_inc(x1_ms, 1)
            a.wait_ge(x1_ms, 1)
            act(ffn_t[:, 1, :], ffn_t[:, 0, :], ACT.Ln).then_inc(x1_ln, 1)
            a.wait_ge(x1_ln, 1)
            act(r_ffn[:, :], ffn_t[:, 1, :], ACT.Exp, scale=-0.5).then_inc(x1_exp, 1)
            def x1_store(half_no):
                a.wait_ge(x1n_t_done, half_no + 1)
                for t in range(TT):
                    last = act(x1[:, t, half_no * S:half_no * S + S], ps[:, 4 + t, :], ACT.Copy)
                last.then_inc(x1n_stored, 1)

            x1_store(0)

            a.preload_act_table(ACT.Sigmoid)

            def up(jj, first):
                for i in range(2):
                    j = jj * 2 + i
                    n = jj * 4 + (N_UP + 2 * i)
                    for gv in range(2):
                        e = 2 * i + gv
                        hi_at(n + gv + 2, gv, jj * 2 + (N_UP // 2 + i + 1))
                        a.wait_ge(cin_ready, jj * 4 + (e + 1))
                        if not first:
                            a.wait_ge(act_ready, jj * 2 + (i - 1))
                        act(conv_out[:, e, :], conv_in[:, e, 2:2 + S], ACT.Identity, scale=pcol(CW2, j + KF * gv),
                            bias=pcol(CB, j + KF * gv)).then_inc(tap_init, 1)
                    a.wait_ge(conv_done, jj * 4 + (2 * i + 1))
                    act(sg[:, i, :], conv_out[:, 2 * i, :], ACT.Sigmoid).then_inc(sg_ready, 1)

            def a_split(k, slot, first):
                a.wait_ge(act_ready, k + 1)
                if not first:
                    a.wait_ge(unit_done, k + (N_DOWN - 1))
                act(a_hi[:, slot, :], act_sb[:, k, :], ACT.Copy).then_inc(a_hi_ready, 1)

            up(0, True)
            x1_store(1)
            with a.Fori(1, KF // 2 - 1) as jj:
                up(jj, False)
            a_split(0, 0, True)
            a_split(1, 1, True)
            up(KF // 2 - 1, False)

            with a.Fori(0, KF // 2 - 1) as kk:
                for i in range(2):
                    hi_at(kk * 2 + (N_DOWN + i + 2), i, kk + (N_DOWN // 2 + 1))
                    a_split(kk * 2 + (i + 2), i, False)

        @block.vector
        def _(d):
            v = nc.vector

            def lo(n, slot):
                d.wait_ge(hi_ready, n + 1)
                v.tensor_tensor(w_lo[:, slot, :], w_raw[:, slot, :], r32(w_hi[:, slot, :]), ALU.subtract)\
                    .then_inc(lo_ready, 1)

            v.memset(ones_heads[:, :], 0.0).then_inc(heads_step, 1)
            d.wait_ge(heads_step, 1)
            v.memset(ones_heads[0:HD, 0:HD], 1.0)
            v.memset(ones_heads[HD:P, HD:P], 1.0).then_inc(heads_step, 1)
            d.wait_ge(gmix_in_psum, 1)
            v.tensor_copy(g_mix[:, :], ps[:, 0, 0:KD]).then_inc(gmix_ready, 1)
            for t in range(TT):
                ms, r, c = tok[:, 1, t:t + 1], tok[:, 3, t:t + 1], tok[:, 4, t:t + 1]
                d.wait_ge(ssq_done, t + 1)
                v.tensor_scalar(ms, tok[:, 0, t:t + 1], 1.0 / D, EPS, ALU.mult, ALU.add).then_inc(tok_step, 1)
                d.wait_ge(exp0_done, t + 1)
                d.wait_ge(tok_step, 2 * t + 1)
                v.scalar_tensor_tensor(out=c, in0=r, scalar=ms, in1=r, op0=ALU.mult, op1=ALU.mult).then_inc(tok_step, 1)
                d.wait_ge(tok_step, 2 * t + 2)
                v.tensor_scalar(c, c, -0.5, 1.5, ALU.mult, ALU.add).then_inc(rstd_ready, 1)
                d.wait_ge(rstd_ready, t + 1)
                v.tensor_scalar(x_scaled[:, t, :], x_in[:, t, :], r, c, ALU.mult, ALU.mult).then_inc(xs_ready, 1)
            lo(N_QK0, 0)
            d.wait_ge(gmix_ready, 1)
            for k in range(KD):
                d.wait_ge(h_hi_ready, k + 1)
                v.scalar_tensor_tensor(out=h_lo[:, k, :], in0=ps[:, k, :], scalar=g_mix[:, k:k + 1],
                                       in1=r32(h_hi[:, k, :]), op0=ALU.mult, op1=ALU.subtract).then_inc(h_lo_ready, 1)
            d.wait_ge(rel_landed, 16)
            v.tensor_scalar(frow[:, 0, 64:64 + REL], frow[:, 1, 0:REL], 8.0, None, ALU.mult).then_inc(frow_ready, 1)
            d.wait_ge(frow_ready, 1)
            v.tensor_copy(frow[:, 0, 0:64], frow[:, 0, 64:65].to_broadcast([8, 64])).then_inc(frow_ready, 1)
            v.tensor_copy(frow[:, 0, 64 + REL:], frow[:, 0, 63 + REL:64 + REL].to_broadcast([8, REL_ROW - 64 - REL]))\
                .then_inc(frow_ready, 1)

            def newton_half_q(pair):
                d.wait_ge(expq_done, pair * 2 + 1)
                v.tensor_tensor(nt[:, 0, :], rn[:, 0, :], rn[:, 0, :], ALU.mult).then_inc(newton_q, 1)
                d.wait_ge(newton_q, pair * 2 + 1)
                v.tensor_tensor(nt[:, 0, :], nt[:, 0, :], sq[:, 0, :], ALU.mult).then_inc(newton_q, 1)

            def hat(pair, i):
                t = pair * 2 + i
                if i == 0:
                    d.wait_ge(newton_q, t + 2)
                else:
                    d.wait_ge(rn_ready, pair + 1)
                d.wait_ge(proj_raw, t + 1)
                v.scalar_tensor_tensor(out=nt[:, i, :], in0=nt[:, i, :], scalar=-3.0, in1=rn[:, i, :],
                                       op0=ALU.add, op1=ALU.mult).then_inc(refined, 1)
                d.wait_ge(refined, t + 1)
                v.scalar_tensor_tensor(out=qk_raw[:, i, :], in0=qk_raw[:, i, :], scalar=qk_gain[:, i:i + 1],
                                       in1=nt[:, i, :], op0=ALU.mult, op1=ALU.mult).then_inc(hat_ready, 1)

            def hat_lo(t, i):
                d.wait_ge(qk_hi_ready, t + 1)
                v.tensor_tensor(qk_lo[:, i, :], qk_raw[:, i, :], r32(qk_hi[:, i, :]), ALU.subtract)\
                    .then_inc(qk_lo_ready, 1)

            d.wait_ge(lo_ready, N_VA)
            lo(N_VA, 0)
            d.wait_ge(par_in_psum, 1)
            v.tensor_copy(par[:, :, :], ps[:, PAR_BANK, 0:2 * P].rearrange("p (t c) -> p t c", t=2)).then_inc(par_ready, 1)
            d.wait_ge(par_ready, 1)
            v.tensor_scalar(qk_gain[:, :], par[:, GQ[0], GQ[1]:GQ[1] + 2], -0.5, None, ALU.mult).then_inc(gain_ready, 1)
            d.wait_ge(gain_ready, 1)
            lo(N_VA + 1, 1)
            lo(N_VA + 2, 0)
            newton_half_q(0)
            hat(0, 0)
            hat(0, 1)
            lo(N_VA + 3, 1)
            hat_lo(0, 0)
            hat_lo(1, 1)
            for u in range(5):
                lo(N_VB + u, u % 2)
            d.wait_ge(v_b_half, 1)
            v.tensor_copy(v_b[:, 0:2, :], ps[:, V_B_BANKS[0]:V_B_BANKS[0] + 2, :]).then_inc(v_b_stored, 1)
            lo(N_VB + 5, 1)

            def scores_of(h, c, n):
                return ps[:, HEAD[h]:HEAD[h] + 3, :].rearrange("p b c -> p (b c)")[:, c:c + n]

            def softmax_logits(s, h):
                for qt, c, n in segs():
                    v.tensor_tensor_reduce(out=pa[h][:, c:c + n], in0=scores_of(h, c, n), in1=bias_rev[:, h, n - 1::-1],
                                           scale=-0.125, scalar=-MASKED, op0=ALU.add, op1=ALU.min,
                                           accum_out=hstat[:, h, 0, qt:qt + 1]).then_inc(negmax_ready, 1)

            def softmax_scale(s, h):
                hh = s * 2 + h
                for i, (qt, c, n) in enumerate(segs()):
                    d.wait_ge(exp_done, hh * 4 + (i + 1))
                    v.reciprocal(hstat[:, h, 2, qt:qt + 1], hstat[:, h, 1, qt:qt + 1]).then_inc(recip_done, 1)
                    d.wait_ge(recip_done, hh * 4 + (i + 1))
                    last = v.tensor_scalar(pa[h][:, c:c + n], pa[h][:, c:c + n], hstat[:, h, 2, qt:qt + 1], None, ALU.mult)
                last.then_inc(p_ready, 1)

            def sticks(s, h):
                hh = s * 2 + h
                d.wait_ge(keep_done, hh - 7)
                d.wait_ge(p_ready, hh)
                for qt, c, n in segs():
                    e = seg2(qt)
                    last = v.tensor_tensor_scan(rev(suffix, e, n), rev(keep[h], c, n), rev(keep[h], c, n), 1.0,
                                                ALU.mult, ALU.bypass)
                last.then_inc(scan_done, 1)
                d.wait_ge(scan_done, hh - 7)
                d.wait_ge(beta_done, hh - 7)
                for qt, c, n in segs():
                    e = seg2(qt)
                    last = v.tensor_tensor(pa[h][:, c:c + n], pa[h][:, c:c + n], suffix[:, e + 1:e + 1 + n], ALU.mult)
                last.then_inc(p_ready, 1)

            def rev(buf, c, n):
                return buf[:, c:c + n][:, ::-1]

            def v_split_lo(s, vv, pair):
                d.wait_ge(v_hi_ready, s + 1)
                for h in range(2):
                    last = v.tensor_tensor(v_st[:, h, :, own(1 - h)], vv[:, :, bass.ds(pair * P + h * HD, HD)],
                                           r32(v_st[:, h, :, own(h)]), ALU.subtract)
                last.then_inc(v_lo_ready, 1)

            def pt_split_lo(s, h):
                d.wait_ge(pt_hi_ready, s * 2 + h + 1)
                v.tensor_tensor(pt_lo[:, :], scores_of(h, 0, SCORES), r32(pt_hi[:, :]), ALU.subtract).then_inc(pt_lo_ready, 1)

            def o_sum_up(s, h):
                d.wait_ge(o_part_ready, s * 2 + h + 1)
                v.tensor_tensor(o_sum[own(h), :], ps[own(h), HEAD[h], :], o_sum[own(1 - h), :], ALU.add)\
                    .then_inc(o_sum_ready, 1)

            def raw_lo(t, i):
                d.wait_ge(qk_hi_ready, t + 1)
                v.tensor_tensor(qk_lo[:, i, :], ps[:, PROJ[i], :], r32(qk_hi[:, i, :]), ALU.subtract)\
                    .then_inc(qk_lo_ready, 1)

            def slot(s, attn, proj):
                b = s * 4 + N_SLOT
                first = isinstance(s, int) and s == 0
                t = s * 2 + 2
                if attn == "A":
                    d.wait_ge(s_done, s + 1)
                    d.wait_ge(bias_ready, s * 2 + 2)
                    if not first:
                        d.wait_ge(t_done, s * 2)
                    v_split_lo(s, v_a, s)
                    softmax_logits(s, 0)
                    softmax_scale(s, 0)
                    softmax_logits(s, 1)
                else:
                    sticks(s, 0)
                    v_split_lo(s, v_b, s - 4)
                    sticks(s, 1)
                pt_split_lo(s, 0)
                if attn == "A":
                    softmax_scale(s, 1)
                if proj == "B":
                    raw_lo(t, 0)
                lo(b + 2, 0)
                if proj == "B":
                    raw_lo(t + 1, 1)
                if proj == "A":
                    newton_half_q(s + 1)
                pt_split_lo(s, 1)
                lo(b + 3, 1)
                o_sum_up(s, 0)
                if proj == "A":
                    hat(s + 1, 0)
                    hat(s + 1, 1)
                    hat_lo(t, 0)
                    hat_lo(t + 1, 1)
                o_sum_up(s, 1)
                lo(b + 4, 0)
                lo(b + 5, 1)

            slot(0, "A", "A")
            with d.Fori(1, 3) as s:
                slot(s, "A", "A")
            slot(3, "A", "B")
            d.wait_ge(qk_lo_ready, 8)
            for qt in range(TT):
                c = seg2(qt) + P * (qt + 1)
                last = v.memset(suffix[:, c:c + 1], 1.0)
            last.then_inc(suffix_init, 1)
            d.wait_ge(suffix_init, 1)
            with d.Fori(4, 7) as s:
                slot(s, "B", "B")

            s, b = 7, N_SLOT + 28
            sticks(s, 0)
            v_split_lo(s, v_b, 3)
            v.memset(u_pad[:, :, 0:16], 0.0).then_inc(u_init, 1)
            sticks(s, 1)
            pt_split_lo(s, 0)
            lo(b + 2, 0)
            pt_split_lo(s, 1)
            lo(b + 3, 1)
            v.memset(inv[:, 0, :], 1.0).then_inc(inv_step, 1)
            d.wait_ge(inv_step, 1)
            v.tensor_tensor_scan(inv[:, 1, :], inv[:, 0, :], inv[:, 0, :], 0.0, ALU.add, ALU.bypass).then_inc(inv_step, 1)
            d.wait_ge(inv_step, 2)
            v.reciprocal(inv[:, 2, :], inv[:, 1, :]).then_inc(inv_step, 1)
            d.wait_ge(wp_hi_ready, 1)
            v.tensor_tensor(wp_lo[:, :, :], wp_raw[:, :, :], r32(wp_hi[:, :, :]), ALU.subtract).then_inc(wp_lo_ready, 1)
            d.wait_ge(inv_step, 3)

            def pooled(i):
                g = GROUPS[i]
                w = WINDOWS[g]
                d.wait_ge(win_ready, i + 1)
                if i:
                    d.wait_ge(pl_lo_ready, i)
                sums = win[:, g % 2, :]
                v.scalar_tensor_tensor(out=pl[:, :], in0=sums[:, 16:], scalar=1.0 / w, in1=u_pad[:, g, 16:],
                                       op0=ALU.mult, op1=ALU.subtract).then_inc(pl_step, 1)
                d.wait_ge(pl_step, 2 * i + 1)
                v.tensor_tensor(pl[:, 0:w - 1], sums[:, 16:15 + w], inv[:, 2, 0:w - 1], ALU.mult).then_inc(pl_step, 1)
                d.wait_ge(pl_step, 2 * i + 2)
                v.tensor_tensor(pl[:, 0:w - 1], pl[:, 0:w - 1], u_pad[:, g, 16:15 + w], ALU.subtract)\
                    .then_inc(pl_ready, 1)
                d.wait_ge(pl_hi_ready, i + 1)
                v.tensor_tensor(pl_lo[:, i % 2, :], pl[:, :], r32(pl_hi[:, i % 2, :]), ALU.subtract)\
                    .then_inc(pl_lo_ready, 1)

            def oc_split_lo(i):
                g = GROUPS[i]
                d.wait_ge(oc_hi_ready, i + 1)
                v.scalar_tensor_tensor(out=oc_lo[:, g, :], in0=ps[:, MIX + i, :], scalar=pcol(PSC, g),
                                       in1=r32(oc_hi[:, g, :]), op0=ALU.mult, op1=ALU.subtract).then_inc(oc_lo_ready, 1)

            o_sum_up(s, 0)
            pooled(0)
            lo(b + 4, 0)
            o_sum_up(s, 1)
            pooled(1)
            lo(b + 5, 1)
            pooled(2)
            pooled(3)
            lo(b + 6, 0)
            for i in range(3):
                oc_split_lo(i)
            lo(b + 7, 1)
            oc_split_lo(3)

            def merge(mm, i, first):
                m = mm * 2 + i
                n = mm * 6 + (N_MERGE + 3 * i)
                bank = 4 * i
                gm = [gates[:, m + KD * br, :] for br in range(2)]
                lo(n + 2, i)
                if not first:
                    d.wait_ge(m_lo_ready, m)
                d.wait_ge(sig_ab, m + 1)
                d.wait_ge(unit_done, n + 1)
                v.tensor_tensor(mg[:, 0, :], ps[:, bank, :], gm[0], ALU.mult)
                v.tensor_tensor(mg[:, 1, :], ps[:, bank + 1, :], gm[1], ALU.mult).then_inc(mg_step, 1)
                d.wait_ge(mg_step, m * 3 + 1)
                v.tensor_tensor(mg[:, 0, :], mg[:, 0, :], mg[:, 1, :], ALU.add).then_inc(mg_step, 1)
                lo(n + 3, 1 - i)
                d.wait_ge(sig_c, m + 1)
                d.wait_ge(unit_done, n + 3)
                v.tensor_tensor(mg[:, 2, :], ps[:, bank + 3, :], mg[:, 3, :], ALU.mult).then_inc(mg_step, 1)
                d.wait_ge(mg_step, m * 3 + 3)
                v.tensor_tensor(mg[:, 0, :], mg[:, 0, :], mg[:, 2, :], ALU.add).then_inc(mg_ready, 1)
                lo(n + 4, i)
                d.wait_ge(m_hi_ready, m + 1)
                v.tensor_tensor(m_lo[:, m, :], mg[:, 0, :], r32(m_hi[:, m, :]), ALU.subtract).then_inc(m_lo_ready, 1)

            merge(0, 0, True)
            merge(0, 1, False)
            with d.Fori(1, KD // 2) as mm:
                merge(mm, 0, False)
                merge(mm, 1, False)

            def out_tile(m, bank):
                d.wait_ge(unit_done, m + (N_OUT + 1))
                v.tensor_tensor(x1_t[:, m, :], ps[:, bank, :], x_t[:, m, :], ALU.add).then_inc(x1_ready, 1)

            def h2_split_lo(m):
                d.wait_ge(h2_hi, m + 1)
                v.scalar_tensor_tensor(out=h_lo[:, m, :], in0=x1_t[:, m, :], scalar=pcol(GF, m),
                                       in1=r32(h_hi[:, m, :]), op0=ALU.mult, op1=ALU.subtract).then_inc(h2_lo, 1)

            lo(N_OUT + 2, 0)
            lo(N_OUT + 3, 1)
            d.wait_ge(xt_stored, 8)
            out_tile(0, 0)
            out_tile(1, 1)
            h2_split_lo(0)
            h2_split_lo(1)
            for m in (2, 3):
                out_tile(m, m)
                lo(N_OUT + m + 2, m % 2)
                h2_split_lo(m)
            with d.Fori(2, KD // 2) as mm:
                for i in range(2):
                    out_tile(mm * 2 + i, i)
                    lo(mm * 2 + (N_OUT + i + 2), i)
                    h2_split_lo(mm * 2 + i)
            d.wait_ge(x1_exp, 1)
            v.tensor_tensor(ffn_t[:, 1, :], r_ffn[:, :], r_ffn[:, :], ALU.mult).then_inc(ffn_step, 1)
            d.wait_ge(ffn_step, 1)
            v.tensor_tensor(ffn_t[:, 1, :], ffn_t[:, 1, :], ffn_t[:, 0, :], ALU.mult).then_inc(ffn_step, 1)
            d.wait_ge(ffn_step, 2)
            v.tensor_scalar(ffn_t[:, 1, :], ffn_t[:, 1, :], -0.5, 1.5, ALU.mult, ALU.add).then_inc(ffn_step, 1)
            d.wait_ge(ffn_step, 3)
            v.tensor_tensor(r_ffn[:, :], r_ffn[:, :], ffn_t[:, 1, :], ALU.mult).then_inc(r_ready, 1)
            v.memset(conv_in[:, :, 0:2], 0.0).then_inc(cin_zero, 1)
            d.wait_ge(r_ready, 1)
            d.wait_ge(cin_zero, 1)

            def taps(jj, i, gv):
                j, e = jj * 2 + i, 2 * i + gv
                count = jj * 4 + (e + 1)
                d.wait_ge(tap_init, count)
                v.scalar_tensor_tensor(out=conv_out[:, e, :], in0=conv_in[:, e, 1:1 + S], scalar=pcol(CW1, j + KF * gv),
                                       in1=conv_out[:, e, :], op0=ALU.mult, op1=ALU.add).then_inc(tap1_done, 1)
                d.wait_ge(tap1_done, count)
                v.scalar_tensor_tensor(out=conv_out[:, e, :], in0=conv_in[:, e, 0:S], scalar=pcol(CW0, j + KF * gv),
                                       in1=conv_out[:, e, :], op0=ALU.mult, op1=ALU.add).then_inc(conv_done, 1)

            def up(jj):
                for i in range(2):
                    n = jj * 4 + (N_UP + 2 * i)
                    for gv in range(2):
                        e = 2 * i + gv
                        d.wait_ge(unit_done, n + gv + 1)
                        v.tensor_tensor(conv_in[:, e, 2:2 + S], ps[:, e, :], r_ffn[:, :], ALU.mult)\
                            .then_inc(cin_ready, 1)
                        lo(n + gv + 2, gv)
                        taps(jj, i, gv)

            def a_split(k, slot):
                d.wait_ge(a_hi_ready, k + 1)
                v.tensor_tensor(a_lo[:, slot, :], act_sb[:, k, :], r32(a_hi[:, slot, :]), ALU.subtract).then_inc(a_lo_ready, 1)

            with d.Fori(0, KF // 2 - 1) as jj:
                up(jj)
            a_split(0, 0)
            a_split(1, 1)
            up(KF // 2 - 1)

            with d.Fori(0, KF // 2 - 1) as kk:
                for i in range(2):
                    lo(kk * 2 + (N_DOWN + i + 2), i)
                    a_split(kk * 2 + (i + 2), i)
            for b8 in range(8):
                d.wait_ge(bank_done, b8 + 1)
                h = b8 % 2
                v.tensor_tensor(out_sb[:, b8, :], ps[:, b8, :], x1[:, b8 // 2, h * S:h * S + S], ALU.add)\
                    .then_inc(out_ready, 1)

        @block.tensor
        def _(pe):
            mm3 = nc.tensor.matmul

            def product(dst, l_hi, l_lo, r_hi, r_lo, start, stop, **kw):
                mm3(dst, l_hi, r_lo, start=start, stop=False, **kw)
                mm3(dst, l_hi, r_hi, start=False, stop=False, **kw)
                return mm3(dst, l_lo, r_hi, start=False, stop=stop, **kw)

            def tile_of(n, slot, bank, channels_ready=None, midway=None):
                pe.wait_ge(lo_ready, n + 1)
                for k in range(KD):
                    c = slice(k * P, k * P + P)
                    if channels_ready is not None:
                        pe.wait_ge(channels_ready, k + 1)
                    if midway is not None and k == KD // 2:
                        midway()
                    last = product(ps[:, bank, :], w_hi[:, slot, c], w_lo[:, slot, c], h_hi[:, k, :], h_lo[:, k, :],
                                   k == 0, k == KD - 1)
                last.then_inc(unit_done, 1)

            pe.wait_ge(const_ready, 1)
            pe.wait_ge(gmix_landed, 16)
            nc.tensor.transpose(ps[:, 0, 0:KD], g_row[:, :], ident[0:KD, 0:KD]).then_inc(gmix_in_psum, 1)
            pe.wait_ge(gmix_ready, 1)
            for t in range(TT):
                pe.wait_ge(xs_ready, t + 1)
                for k in range(KD):
                    last = nc.tensor.transpose(ps[:, k, t * P:t * P + P], x_scaled[:, t, k * P:k * P + P], ident[:, :])
                    if t == TT - 1:
                        last.then_inc(xs_used, 1)

            tile_of(N_QK0, 0, PROJ[0], channels_ready=h_lo_ready)
            tile_of(N_QK0 + 1, 1, PROJ[1])
            pe.wait_ge(rows_landed, 11 * 16)
            for t in range(2):
                last = nc.tensor.transpose(ps[:, PAR_BANK, t * P:t * P + P], rows[:, t, :], ident[:, :])
            last.then_inc(par_in_psum, 1)

            def values(n0, banks, u):
                pe.wait_ge(lo_ready, n0 + u + 1)
                for kk in range(2):
                    k = 2 * u + kk
                    for t in range(TT):
                        c = slice(kk * WB, kk * WB + WB)
                        tk = slice(t * P, t * P + P)
                        last = product(ps[:, banks[t], :], h_hi[:, k, tk], h_lo[:, k, tk], w_hi[:, u % 2, c],
                                       w_lo[:, u % 2, c], k == 0, k == KD - 1)
                        if n0 == N_VB and k == KD - 1 and t == 1:
                            last.then_inc(v_b_half, 1)
                last.then_inc(unit_done, 1)

            def sumsq(t, i, bank):
                pe.wait_ge(proj_sq, t + 1)
                mm3(ps[:, bank, :], ones_heads[:, :], sq[:, i, :], start=True, stop=True).then_inc(ss_done, 1)

            values(N_VA, V_A_BANKS, 0)
            pe.wait_ge(par_ready, 1)
            sumsq(0, 0, 6)
            sumsq(1, 1, 7)
            for u in range(1, 4):
                values(N_VA, V_A_BANKS, u)
            pe.wait_ge(ms_done, 2)
            for u in range(4):
                values(N_VB, V_B_BANKS, u)

            def scores(s, attn):
                for qt, c, n in segs():
                    q = slice(qt * P, qt * P + P)
                    dst = [ps[:, HEAD[h]:HEAD[h] + 3, :].rearrange("p b c -> p (b c)")[:, c:c + n] for h in range(2)]
                    for i, (a_q, a_k) in enumerate(((qk_hi, qk_lo), (qk_lo, qk_hi), (qk_hi, qk_hi))):
                        for h in range(2):
                            r = slice(HD * h, HD * h + HD)
                            last = mm3(dst[h], a_q[r, 0, q], a_k[r, 1, 0:n], start=i == 0, stop=i == 2 and attn == "A")
                    if attn == "B":
                        for h in range(2):
                            last = mm3(dst[h][:, qt * P:n], ident_b[:, :], causal_b[:, :], start=False, stop=True)
                last.then_inc(s_done, 1)

            def transposes(s, h):
                pe.wait_ge(p_ready, s * 2 + h + 1)
                flat = ps[:, HEAD[h]:HEAD[h] + 3, :].rearrange("p b c -> p (b c)")
                for kt in range(TT):
                    for qt in range(kt, TT):
                        c = T_OFF[kt] + P * (qt - kt)
                        last = nc.tensor.transpose(flat[:, c:c + P],
                                                   pa[h][:, S_OFF[qt] + kt * P:S_OFF[qt] + kt * P + P], ident[:, :])
                last.then_inc(t_done, 1)

            def output(s, h):
                if h == 0:
                    pe.wait_ge(v_lo_ready, s + 1)
                pe.wait_ge(pt_lo_ready, s * 2 + h + 1)
                for kt in range(TT):
                    n = S - P * kt
                    c = slice(T_OFF[kt], T_OFF[kt] + n)
                    mm3(ps[:, HEAD[h], P * kt:S], v_st[:, h, kt, :], pt_lo[:, c], start=kt == 0, stop=False)
                    last = mm3(ps[:, HEAD[h], P * kt:S], v_st[:, h, kt, :], pt_hi[:, c], start=False, stop=kt == TT - 1)
                last.then_inc(pv_done, 1)

            def slot(s, attn, proj):
                b = s * 4 + N_SLOT
                t = s * 2 + 2
                pe.wait_ge(qk_lo_ready, s * 2 + 2)
                if isinstance(s, int) and s == 0:
                    pe.wait_ge(v_stored, 1)
                    pe.wait_ge(v_b_stored, 1)
                else:
                    pe.wait_ge(o_sum_ready, s * 2)
                scores(s, attn)
                if isinstance(s, int) and s == 0:
                    pe.wait_ge(v_stored, 2)
                else:
                    pe.wait_ge(gate_stored, s * 2)
                tile_of(b, 0, PROJ[0])
                transposes(s, 0)
                tile_of(b + 1, 1, PROJ[1])
                output(s, 0)
                if proj == "A":
                    sumsq(t, 0, HEAD[0] + 1)
                    sumsq(t + 1, 1, HEAD[0] + 2)
                transposes(s, 1)
                if proj == "B":
                    pe.wait_ge(qk_lo_ready, s * 2 + 3)
                elif proj == "U":
                    pe.wait_ge(u_stored, 1)
                tile_of(b + 2, 0, PROJ[0])
                output(s, 1)
                if proj == "B":
                    pe.wait_ge(qk_lo_ready, s * 2 + 4)
                elif proj == "U":
                    pe.wait_ge(u_stored, 2)
                tile_of(b + 3, 1, PROJ[1])

            slot(0, "A", "A")
            with pe.Fori(1, 3) as s:
                slot(s, "A", "A")
            slot(3, "A", "B")
            with pe.Fori(4, 7) as s:
                slot(s, "B", "B")
            slot(7, "B", "U")
            b = N_SLOT + 28

            def mix(i):
                g = GROUPS[i]
                pe.wait_ge(pl_lo_ready, i + 1)
                product(ps[:, MIX + i, :], wp_hi[:, g, :], wp_lo[:, g, :], pl_hi[:, i % 2, :], pl_lo[:, i % 2, :],
                        True, True).then_inc(mix_done, 1)

            pe.wait_ge(wp_lo_ready, 1)
            pe.wait_ge(o_sum_ready, 15)
            mix(0)
            pe.wait_ge(u_stored, 3)
            tile_of(b + 4, 0, PROJ[0])
            mix(1)
            mix(2)
            pe.wait_ge(u_stored, 4)
            tile_of(b + 5, 1, PROJ[1])
            mix(3)

            def merge(mm, i, first):
                m = mm * 2 + i
                n = mm * 6 + (N_MERGE + 3 * i)
                bank = 4 * i
                sl = (i, 1 - i, i)
                pe.wait_ge(lo_ready, n + 1)
                if not first:
                    pe.wait_ge(mg_ready, m - 1)
                for br in range(2):
                    if first and i == 0:
                        pe.wait_ge(o_lo_ready, 16)
                        pe.wait_ge(gate_stored, 2 * KD - 1 + br)
                    for k in range(KB):
                        c = slice((KB * br + k) * P, (KB * br + k) * P + P)
                        last = product(ps[:, bank + br, :], w_hi[:, sl[0], c], w_lo[:, sl[0], c],
                                       o_hi[:, KB * br + k, :], o_lo[:, KB * br + k, :], k == 0, k == KB - 1)
                last.then_inc(unit_done, 1)
                if first and i == 0:
                    pe.wait_ge(o_sum_ready, 16)
                tile_of(n + 1, sl[1], bank + 2)
                if first and i == 0:
                    pe.wait_ge(oc_lo_ready, 4)
                pe.wait_ge(lo_ready, n + 3)
                for k in range(KB):
                    c = slice(k * P, k * P + P)
                    last = product(ps[:, bank + 3, :], w_hi[:, sl[2], c], w_lo[:, sl[2], c], oc_hi[:, k, :],
                                   oc_lo[:, k, :], k == 0, k == KB - 1)
                last.then_inc(unit_done, 1)

            merge(0, 0, True)
            merge(0, 1, True)
            with pe.Fori(1, KD // 2) as mm:
                merge(mm, 0, False)
                merge(mm, 1, False)

            def x_half(half_no):
                pe.wait_ge(xre_landed[half_no], 16)
                if half_no:
                    pe.wait_ge(xt_stored, 4)
                for k in range(KD):
                    for t in range(2):
                        c = (k % 2) * 256 + t * P
                        last = nc.tensor.transpose(ps[:, 4 + k // 2, c:c + P], x_re[:, t, k * P:k * P + P], ident[:, :])
                last.then_inc(xre_t_done, 1)

            def out_tile(n, slot, bank, channels_ready=None):
                pe.wait_ge(lo_ready, n + 1)
                for k in range(KD):
                    c = slice(k * P, k * P + P)
                    if channels_ready is not None:
                        pe.wait_ge(channels_ready, k + 1)
                    last = product(ps[:, bank, :], w_hi[:, slot, c], w_lo[:, slot, c], m_hi[:, k, :], m_lo[:, k, :],
                                   k == 0, k == KD - 1)
                last.then_inc(unit_done, 1)

            pe.wait_ge(mg_ready, KD - 1)
            out_tile(N_OUT, 0, 0, channels_ready=m_lo_ready)
            x_half(0)
            out_tile(N_OUT + 1, 1, 1)
            x_half(1)
            out_tile(N_OUT + 2, 0, 2)
            out_tile(N_OUT + 3, 1, 3)
            with pe.Fori(2, KD // 2) as mm:
                for i in range(2):
                    pe.wait_ge(x1_ready, mm * 2 + (i - 1))
                    out_tile(mm * 2 + (N_OUT + i), i, i)

            def x1_back(half_no):
                for k in range(4):
                    for t in range(TT):
                        last = nc.tensor.transpose(ps[:, 4 + t, k * P:k * P + P],
                                                   x1_t[:, 4 * half_no + k, t * P:t * P + P], ident[:, :])
                last.then_inc(x1n_t_done, 1)

            def x1_sum_channels():
                pe.wait_ge(x1_ss, KD - 1)
                mm3(ps[:, 2, :], ones_all[:, :], ss_x1[:, :], start=True, stop=True).then_inc(x1_total, 1)

            x1_back(0)

            def up(jj, first):
                for i in range(2):
                    for gv in range(2):
                        e = 2 * i + gv
                        if not first:
                            pe.wait_ge(cin_ready, jj * 4 + (e - 3))
                        elif e == 2:
                            pe.wait_ge(x1_ms, 1)
                        begins = first and e == 0
                        if first and e < 2:
                            pe.wait_ge(x1_ready, KD - 1 + e)
                        tile_of(jj * 4 + (N_UP + e), gv, e, channels_ready=h2_lo if begins else None,
                                midway=x1_sum_channels if begins else None)

            up(0, True)
            pe.wait_ge(x1n_stored, 1)
            x1_back(1)
            with pe.Fori(1, KF // 2) as jj:
                up(jj, False)

            pe.wait_ge(x1n_stored, 2)

            def down(k, slot, start):
                pe.wait_ge(lo_ready, k + (N_DOWN + 1))
                pe.wait_ge(a_lo_ready, k + 1)
                for b8 in ((4, 5, 6, 7, 0, 1, 2, 3) if start else range(8)):
                    t, h = b8 // 2, b8 % 2
                    if start and b8 == 0:
                        pe.wait_ge(cin_ready, 2 * KF)
                    tk, c = slice(t * P, t * P + P), slice(h * S, h * S + S)
                    last = product(ps[:, b8, :], a_hi[:, slot, tk], a_lo[:, slot, tk], w_hi[:, slot, c],
                                   w_lo[:, slot, c], start, False)
                last.then_inc(unit_done, 1)

            down(0, 0, True)
            down(1, 1, False)
            with pe.Fori(1, KF // 2 - 1) as kk:
                down(kk * 2, 0, False)
                down(kk * 2 + 1, 1, False)
            down(KF - 2, 0, False)
            pe.wait_ge(lo_ready, N_END)
            pe.wait_ge(a_lo_ready, KF)
            for b8 in range(8):
                t, h = b8 // 2, b8 % 2
                tk, c = slice(t * P, t * P + P), slice(h * S, h * S + S)
                product(ps[:, b8, :], a_hi[:, 1, tk], a_lo[:, 1, tk], w_hi[:, 1, c], w_lo[:, 1, c], False, True)\
                    .then_inc(bank_done, 1)


_INS = ["x", "norm_mix", "w_in", "b_gate", "q_norm_a", "k_norm_a", "rel_bias_a", "w_pool", "pool_scale",
        "w_branch_a", "w_branch_b", "w_branch_c", "w_out", "norm_ffn", "w_up", "conv_w", "conv_b", "w_down"]


def kernel(**inputs):
    import numpy as _np
    import concourse.bacc as _bacc
    from concourse import mybir as _mybir
    from concourse.bass_utils import run_bass_kernel_spmd as _run

    nc = _bacc.Bacc("TRN2", target_bir_lowering=False, num_devices=1)
    arrays, args = {}, []
    for name in _INS:
        a = _np.ascontiguousarray(inputs[name])
        arrays[f"in_{name}_dram"] = a
        args.append(nc.dram_tensor(f"in_{name}_dram", a.shape, _mybir.dt.from_np(a.dtype), kind="ExternalInput").ap())
    args.append(nc.dram_tensor("out_0_dram", (1, S, D), _mybir.dt.float32, kind="ExternalOutput").ap())
    build(nc, *args)
    r = _run(nc, [arrays], core_ids=[0])
    return r.results[0]["out_0_dram"]
```
